# Optimizing a Trainium2 kernel written in Bass

```python
import math
import jax, jax.numpy as jnp
from jax import lax
import numpy as np

D_MODEL = 1024
BATCH = 1
SEQ = 256
DEPTH = 1

D_A = D_MODEL
K_A = 3
D_B = D_MODEL
K_B = 31
N_MEM = 256
N_HEADS = 4
HEAD_DIM = D_MODEL // N_HEADS
D_ATT = N_HEADS * HEAD_DIM
N_BRANCH = 3
D_FF = 2816
K_F = 3
EPS = 1e-6
IN_SPLITS = (3 * D_A, 3 * D_A + 2 * D_B, 3 * D_A + 2 * D_B + D_ATT)
D_IN = 3 * D_A + 2 * D_B + D_ATT + N_BRANCH * D_MODEL


def _rmsnorm(x, g):
    xf = x.astype(jnp.float32)
    r = lax.rsqrt(jnp.mean(xf * xf, axis=-1, keepdims=True) + EPS)
    return (xf * r).astype(x.dtype) * g

def _layernorm(x, g, b):
    xf = x.astype(jnp.float32)
    mu = jnp.mean(xf, axis=-1, keepdims=True)
    var = jnp.mean(jnp.square(xf - mu), axis=-1, keepdims=True)
    return ((xf - mu) * lax.rsqrt(var + EPS)).astype(x.dtype) * g + b

def _causal_dwconv(x, w):
    k, c = w.shape
    return lax.conv_general_dilated(
        x, w[:, None, :].astype(x.dtype), window_strides=(1,), padding=[(k - 1, 0)],
        dimension_numbers=("NWC", "WIO", "NWC"), feature_group_count=c)

def first_inputs(seed: int = 0) -> dict:
    key = jax.random.key(seed)
    ks = jax.random.split(key, 24)
    L, D = DEPTH, D_MODEL

    def nrm(k, shape, fan_in):
        return jax.random.normal(k, shape, jnp.float32) * (fan_in ** -0.5)

    def gain(k, shape):
        return 1.0 + 0.02 * jax.random.normal(k, shape, jnp.float32)

    def small(k, shape):
        return 0.02 * jax.random.normal(k, shape, jnp.float32)

    return {
        "x": jax.random.normal(ks[0], (BATCH, SEQ, D), jnp.float32),
        "mem": jax.random.normal(ks[1], (BATCH, N_MEM, D), jnp.float32),
        "norm_mix_g": gain(ks[2], (L, D)),
        "norm_mem_g": gain(ks[3], (L, D)),
        "w_in": nrm(ks[4], (L, D, D_IN), D),
        "b_gate": small(ks[5], (L, N_BRANCH * D)),
        "conv_a_w": nrm(ks[6], (L, K_A, D_A), K_A),
        "w_a_out": nrm(ks[7], (L, D_A, D), D_A),
        "conv_b_w": nrm(ks[8], (L, K_B, D_B), K_B),
        "conv_b_bias": small(ks[9], (L, D_B)),
        "ln_b_g": gain(ks[10], (L, D_B)),
        "ln_b_b": small(ks[11], (L, D_B)),
        "w_b_out": nrm(ks[12], (L, D_B, D), D_B),
        "w_kv": nrm(ks[13], (L, D, 2 * D_ATT), D),
        "w_att_out": nrm(ks[14], (L, D_ATT, D), D_ATT),
        "w_o": nrm(ks[15], (L, D, D), D),
        "norm_ffn_g": gain(ks[16], (L, D)),
        "w_up": nrm(ks[17], (L, D, 2 * D_FF), D),
        "conv_ffn_w": nrm(ks[18], (L, K_F, 2 * D_FF), K_F),
        "w_down": nrm(ks[19], (L, D_FF, D), D_FF),
        "norm_final_g": gain(ks[20], (D,)),
    }

def _mixer(x, mem, norm_mix_g, norm_mem_g, w_in, b_gate, conv_a_w, w_a_out,
           conv_b_w, conv_b_bias, ln_b_g, ln_b_b, w_b_out, w_kv, w_att_out, w_o):
    bsz, seq, _ = x.shape
    h = _rmsnorm(x, norm_mix_g)
    proj = h @ w_in
    p_a, p_b, q, p_g = jnp.split(proj, IN_SPLITS, axis=-1)

    gb, gc, v = jnp.split(p_a, 3, axis=-1)
    y_a = (gb * _causal_dwconv(gc * v, conv_a_w)) @ w_a_out

    u, ug = jnp.split(p_b, 2, axis=-1)
    u = u * jax.nn.sigmoid(ug)
    u = _causal_dwconv(u, conv_b_w) + conv_b_bias
    u = jax.nn.silu(_layernorm(u, ln_b_g, ln_b_b))
    y_b = u @ w_b_out

    memn = _rmsnorm(mem, norm_mem_g)
    k, vm = jnp.split(memn @ w_kv, 2, axis=-1)
    qh = q.reshape(bsz, seq, N_HEADS, HEAD_DIM)
    kh = k.reshape(bsz, N_MEM, N_HEADS, HEAD_DIM)
    vh = vm.reshape(bsz, N_MEM, N_HEADS, HEAD_DIM)
    s = jnp.einsum("bshd,bmhd->bhsm", qh, kh).astype(jnp.float32) * (1.0 / math.sqrt(HEAD_DIM))
    pr = jax.nn.softmax(s, axis=-1).astype(x.dtype)
    o = jnp.einsum("bhsm,bmhd->bshd", pr, vh).reshape(bsz, seq, D_ATT)
    y_c = o @ w_att_out

    g = jax.nn.sigmoid((p_g + b_gate).reshape(bsz, seq, N_BRANCH, D_MODEL))
    merged = g[:, :, 0] * y_a + g[:, :, 1] * y_b + g[:, :, 2] * y_c
    return merged @ w_o

def _conv_ffn(x, norm_ffn_g, w_up, conv_ffn_w, w_down):
    h = _rmsnorm(x, norm_ffn_g)
    u = _causal_dwconv(h @ w_up, conv_ffn_w)
    gt, up = jnp.split(u, 2, axis=-1)
    return (jax.nn.silu(gt) * up) @ w_down

def first_block(x, mem, norm_mix_g, norm_mem_g, w_in, b_gate, conv_a_w, w_a_out,
              conv_b_w, conv_b_bias, ln_b_g, ln_b_b, w_b_out, w_kv, w_att_out, w_o,
              norm_ffn_g, w_up, conv_ffn_w, w_down, norm_final_g):
    for l in range(DEPTH):
        x = x + _mixer(x, mem, norm_mix_g[l], norm_mem_g[l], w_in[l], b_gate[l],
                       conv_a_w[l], w_a_out[l], conv_b_w[l], conv_b_bias[l],
                       ln_b_g[l], ln_b_b[l], w_b_out[l], w_kv[l], w_att_out[l], w_o[l])
        x = x + _conv_ffn(x, norm_ffn_g[l], w_up[l], conv_ffn_w[l], w_down[l])
    return _rmsnorm(x, norm_final_g)


DEPTH_2 = 2

GRID_W = 64
HEAD_DIM_2 = 64
Q_BLOCK = 128
ROPE_THETA = 10000.0
A_HEADS = 8
A_KV_HEADS = 2
B_HEADS = 8
B_Q_RANK = 384
B_KV_RANK = 256
B_NOPE = 64
B_ROPE = 32
B_V = 64
C_HEADS = 16
C_WIN_ROWS = 8
C_WIN_COLS = 16
D_FF_2 = 4 * D_MODEL

A_Q = A_HEADS * HEAD_DIM_2
A_KV = A_KV_HEADS * HEAD_DIM_2
EVEN_SPLITS = (A_Q, A_Q + A_KV, A_Q + 2 * A_KV, A_Q + 2 * A_KV + B_Q_RANK,
               A_Q + 2 * A_KV + B_Q_RANK + B_KV_RANK)
EVEN_IN = A_Q + 2 * A_KV + B_Q_RANK + B_KV_RANK + B_ROPE
MIX_WIDTH = A_HEADS * HEAD_DIM_2 + B_HEADS * B_V
C_WIDTH = C_HEADS * HEAD_DIM_2
N_EVEN = (DEPTH_2 + 1) // 2
N_ODD = DEPTH_2 // 2


def rmsnorm(x, g):
    xf = x.astype(jnp.float32)
    y = xf * lax.rsqrt(jnp.mean(xf * xf, axis=-1, keepdims=True) + EPS)
    return (y * g.astype(jnp.float32)).astype(x.dtype)

def rope_1d(x, pos):
    d = x.shape[-1]
    inv = ROPE_THETA ** (-jnp.arange(0, d, 2, dtype=jnp.float32) / d)
    ang = pos[:, None] * inv[None, :]
    cos = jnp.cos(ang)[:, None, :].astype(x.dtype)
    sin = jnp.sin(ang)[:, None, :].astype(x.dtype)
    x1, x2 = jnp.split(x, 2, axis=-1)
    return jnp.concatenate([x1 * cos - x2 * sin, x2 * cos + x1 * sin], axis=-1)

def axial_rope(x, row, col):
    xr, xc = jnp.split(x, 2, axis=-1)
    return jnp.concatenate([rope_1d(xr, row), rope_1d(xc, col)], axis=-1)

def block_attention(q, k, v, scale):
    b, s, hq, d = q.shape
    hkv = k.shape[2]
    g = hq // hkv
    nblk = s // Q_BLOCK
    qb = q.reshape(b, nblk, Q_BLOCK, hkv, g, d).transpose(1, 0, 3, 4, 2, 5)
    kt = k.transpose(0, 2, 1, 3)
    vt = v.transpose(0, 2, 1, 3)

    def one(qblk):
        sc = jnp.einsum('bkgqd,bksd->bkgqs', qblk, kt).astype(jnp.float32) * scale
        p = jax.nn.softmax(sc, axis=-1).astype(vt.dtype)
        return jnp.einsum('bkgqs,bksd->bkgqd', p, vt)

    o = lax.map(one, qb)
    return o.transpose(1, 0, 4, 2, 3, 5).reshape(b, s, hq, -1)

def hybrid_attention(h, w_in, a_q_norm, a_k_norm, b_q_norm, b_w_uq, b_kv_norm, b_w_ukv,
                     w_out, row, col):
    b, s, _ = h.shape
    z = h @ w_in
    qa, ka, va, cq, ckv, kr = jnp.split(z, EVEN_SPLITS, axis=-1)
    qa = axial_rope(rmsnorm(qa.reshape(b, s, A_HEADS, HEAD_DIM_2), a_q_norm), row, col)
    ka = axial_rope(rmsnorm(ka.reshape(b, s, A_KV_HEADS, HEAD_DIM_2), a_k_norm), row, col)
    va = va.reshape(b, s, A_KV_HEADS, HEAD_DIM_2)
    oa = block_attention(qa, ka, va, HEAD_DIM_2 ** -0.5)
    qb = (rmsnorm(cq, b_q_norm) @ b_w_uq).reshape(b, s, B_HEADS, B_NOPE + B_ROPE)
    q_nope, q_rope = jnp.split(qb, (B_NOPE,), axis=-1)
    q_rope = axial_rope(q_rope, row, col)
    kvb = (rmsnorm(ckv, b_kv_norm) @ b_w_ukv).reshape(b, s, B_HEADS, B_NOPE + B_V)
    k_nope, vb = jnp.split(kvb, (B_NOPE,), axis=-1)
    k_rope = axial_rope(kr[:, :, None, :], row, col)
    q_full = jnp.concatenate([q_nope, q_rope], axis=-1)
    k_full = jnp.concatenate([k_nope, jnp.broadcast_to(k_rope, (b, s, B_HEADS, B_ROPE))], axis=-1)
    ob = block_attention(q_full, k_full, vb, (B_NOPE + B_ROPE) ** -0.5)
    mixed = jnp.concatenate([oa.reshape(b, s, -1), ob.reshape(b, s, -1)], axis=-1)
    return mixed @ w_out

def neighbourhood_attention(h, w_qkv, rpb, w_out):
    b, s, _ = h.shape
    rows = s // GRID_W
    wr = min(C_WIN_ROWS, rows)
    wc = C_WIN_COLS
    nblk = s // Q_BLOCK
    q, k, v = jnp.split(h @ w_qkv, 3, axis=-1)
    q = q.reshape(b, s, C_HEADS, HEAD_DIM_2).transpose(0, 2, 1, 3)
    k = k.reshape(b, s, C_HEADS, HEAD_DIM_2).transpose(0, 2, 1, 3)
    v = v.reshape(b, s, C_HEADS, HEAD_DIM_2).transpose(0, 2, 1, 3)
    t = jnp.arange(s, dtype=jnp.int32)
    qr, qc = t // GRID_W, t % GRID_W
    rs = jnp.clip(qr - wr // 2, 0, rows - wr)
    cs = jnp.clip(qc - wc // 2, 0, GRID_W - wc)
    kr = rs[:, None, None] + jnp.arange(wr, dtype=jnp.int32)[None, :, None]
    kc = cs[:, None, None] + jnp.arange(wc, dtype=jnp.int32)[None, None, :]
    idx = (kr * GRID_W + kc).reshape(s, wr * wc)
    ridx = jnp.broadcast_to(kr - qr[:, None, None] + (C_WIN_ROWS - 1), (s, wr, wc)).reshape(s, -1)
    cidx = jnp.broadcast_to(kc - qc[:, None, None] + (C_WIN_COLS - 1), (s, wr, wc)).reshape(s, -1)
    qbk = q.reshape(b, C_HEADS, nblk, Q_BLOCK, HEAD_DIM_2).transpose(2, 0, 1, 3, 4)
    blk = lambda a: a.reshape(nblk, Q_BLOCK, -1)
    scale = HEAD_DIM_2 ** -0.5

    def one(args):
        qblk, iblk, rblk, cblk = args
        kg = jnp.take(k, iblk, axis=2)
        vg = jnp.take(v, iblk, axis=2)
        bias = rpb[:, rblk, cblk].astype(jnp.float32)
        sc = jnp.einsum('bhqd,bhqkd->bhqk', qblk, kg).astype(jnp.float32) * scale + bias[None]
        p = jax.nn.softmax(sc, axis=-1).astype(vg.dtype)
        return jnp.einsum('bhqk,bhqkd->bhqd', p, vg)

    o = lax.map(one, (qbk, blk(idx), blk(ridx), blk(cidx)))
    o = o.transpose(1, 0, 3, 2, 4).reshape(b, s, C_WIDTH)
    return o @ w_out

def sq_relu_mlp(h, w_up, w_down):
    u = jax.nn.relu(h @ w_up)
    return (u * u) @ w_down

def second_inputs(seed: int = 0) -> dict:
    key = jax.random.key(seed)
    ks = jax.random.split(key, 20)

    def w(k, shape, fan_in):
        return jax.random.normal(k, shape, jnp.float32) * (fan_in ** -0.5)

    def gain(k, shape):
        return 1.0 + 0.05 * jax.random.normal(k, shape, jnp.float32)

    return {
        "x": jax.random.normal(ks[0], (BATCH, SEQ, D_MODEL), jnp.float32),
        "norm_mix": gain(ks[1], (DEPTH_2, D_MODEL)),
        "ev_w_in": w(ks[2], (N_EVEN, D_MODEL, EVEN_IN), D_MODEL),
        "ev_a_q_norm": gain(ks[3], (N_EVEN, HEAD_DIM_2)),
        "ev_a_k_norm": gain(ks[4], (N_EVEN, HEAD_DIM_2)),
        "ev_b_q_norm": gain(ks[5], (N_EVEN, B_Q_RANK)),
        "ev_b_w_uq": w(ks[6], (N_EVEN, B_Q_RANK, B_HEADS * (B_NOPE + B_ROPE)), B_Q_RANK),
        "ev_b_kv_norm": gain(ks[7], (N_EVEN, B_KV_RANK)),
        "ev_b_w_ukv": w(ks[8], (N_EVEN, B_KV_RANK, B_HEADS * (B_NOPE + B_V)), B_KV_RANK),
        "ev_w_out": w(ks[9], (N_EVEN, MIX_WIDTH, D_MODEL), MIX_WIDTH),
        "od_w_qkv": w(ks[10], (N_ODD, D_MODEL, 3 * C_WIDTH), D_MODEL),
        "od_rpb": 0.1 * jax.random.normal(ks[11], (N_ODD, C_HEADS, 2 * C_WIN_ROWS - 1, 2 * C_WIN_COLS - 1), jnp.float32),
        "od_w_out": w(ks[12], (N_ODD, C_WIDTH, D_MODEL), C_WIDTH),
        "norm_ffn": gain(ks[13], (DEPTH_2, D_MODEL)),
        "ffn_w_up": w(ks[14], (DEPTH_2, D_MODEL, D_FF_2), D_MODEL),
        "ffn_w_down": w(ks[15], (DEPTH_2, D_FF_2, D_MODEL), D_FF_2),
        "final_norm": gain(ks[16], (D_MODEL,)),
    }

def second_block(x, norm_mix, ev_w_in, ev_a_q_norm, ev_a_k_norm, ev_b_q_norm, ev_b_w_uq,
              ev_b_kv_norm, ev_b_w_ukv, ev_w_out, od_w_qkv, od_rpb, od_w_out,
              norm_ffn, ffn_w_up, ffn_w_down, final_norm):
    s = x.shape[1]
    t = jnp.arange(s, dtype=jnp.int32)
    row = (t // GRID_W).astype(jnp.float32)
    col = (t % GRID_W).astype(jnp.float32)
    h = x
    for layer in range(DEPTH_2):
        i = layer // 2
        hn = rmsnorm(h, norm_mix[layer])
        if layer % 2 == 0:
            h = h + hybrid_attention(hn, ev_w_in[i], ev_a_q_norm[i], ev_a_k_norm[i],
                                     ev_b_q_norm[i], ev_b_w_uq[i], ev_b_kv_norm[i],
                                     ev_b_w_ukv[i], ev_w_out[i], row, col)
        else:
            h = h + neighbourhood_attention(hn, od_w_qkv[i], od_rpb[i], od_w_out[i])
        h = h + sq_relu_mlp(rmsnorm(h, norm_ffn[layer]), ffn_w_up[layer], ffn_w_down[layer])
    return rmsnorm(h, final_norm)


def setup_inputs(seed=0):
    out = dict(first_inputs(seed))
    for name, value in second_inputs(seed + 1).items():
        if name != "x":
            out[name + "_2"] = value
    return out


def reference(
    x, mem, norm_mix_g, norm_mem_g, w_in, b_gate, conv_a_w, w_a_out, conv_b_w, conv_b_bias,
    ln_b_g, ln_b_b, w_b_out, w_kv, w_att_out, w_o, norm_ffn_g, w_up, conv_ffn_w, w_down,
    norm_final_g, norm_mix_2, ev_w_in_2, ev_a_q_norm_2, ev_a_k_norm_2, ev_b_q_norm_2,
    ev_b_w_uq_2, ev_b_kv_norm_2, ev_b_w_ukv_2, ev_w_out_2, od_w_qkv_2, od_rpb_2, od_w_out_2,
    norm_ffn_2, ffn_w_up_2, ffn_w_down_2, final_norm_2,
):
    x = first_block(
        x, mem, norm_mix_g, norm_mem_g, w_in, b_gate, conv_a_w, w_a_out, conv_b_w, conv_b_bias,
        ln_b_g, ln_b_b, w_b_out, w_kv, w_att_out, w_o, norm_ffn_g, w_up, conv_ffn_w, w_down,
        norm_final_g,
    )
    return second_block(
        x, norm_mix_2, ev_w_in_2, ev_a_q_norm_2, ev_a_k_norm_2, ev_b_q_norm_2, ev_b_w_uq_2,
        ev_b_kv_norm_2, ev_b_w_ukv_2, ev_w_out_2, od_w_qkv_2, od_rpb_2, od_w_out_2, norm_ffn_2,
        ffn_w_up_2, ffn_w_down_2, final_norm_2,
    )


_drawn_inputs = setup_inputs


def setup_inputs(seed=0):
    import zlib

    import numpy as np

    out = dict(_drawn_inputs(seed))
    spreads = {}
    factors = {'norm_mem_g': 8.0,
     'b_gate': 8.0,
     'conv_b_bias': 3.004,
     'ln_b_g': 6.469,
     'ln_b_b': 6.22,
     'norm_ffn_g': 3.825,
     'norm_mix_2': 3.0,
     'ev_a_q_norm_2': 8.0,
     'ev_a_k_norm_2': 8.0,
     'ev_b_q_norm_2': 8.0,
     'ev_b_kv_norm_2': 8.0,
     'od_rpb_2': 5.035}
    for name, (base, spread) in spreads.items():
        noise = np.random.default_rng([zlib.crc32(name.encode()), seed]).standard_normal(out[name].shape)
        drawn = base * np.exp(spread * noise) if base else spread * noise
        out[name] = __import__('jax').numpy.asarray(drawn.astype(out[name].dtype))
    for name, factor in factors.items():
        out[name] = (out[name] * factor).astype(out[name].dtype)
    return out
```

```python
from contextlib import ExitStack

import concourse.bass as bass
from concourse import mybir

F32 = mybir.dt.float32
F32R = mybir.dt.float32r
ACT = mybir.ActivationFunctionType
ALU = mybir.AluOpType
AX = mybir.AxisListType

P = 128
S = 256
T = S // P
D = 1024
KD = D // P
EPS = 1e-6
R = 3
SLOT = 2048
BW = 512

K_A, K_B, K_F = 3, 31, 3
D_FF = 2816
FG = D_FF // 256
FT = 2 * D_FF // P
D_FF2 = 4096
FP = D_FF2 // 256
MEM_HEADS, MEM_HD = 4, 256
A_HEADS, A_KV, B_HEADS, HD = 8, 2, 8, 64
B_NOPE, B_ROPE = 64, 32
B_QK = B_NOPE + B_ROPE
B_Q_RANK, B_KV_RANK = 384, 256
EV_IN = 1440
Z_K, Z_V, Z_CQ, Z_CKV, Z_KR = 512, 640, 768, 1152, 1408
C_HEADS = 16
GRID_W = 64
RPB_H, RPB_W = 15, 31
NEG = -1.0e30

V_CONVB, V_CONVA, V_MIX, V_MEM, V_GATE, V_CBIAS, V_LNG, V_LNB, V_FFN = 0, 31, 34, 35, 36, 39, 40, 41, 42
V_MIX2, V_FFN2, V_LAT, NV = 43, 45, 47, 48

G_KV, G_UGQ, G_CVB, G_GATE, G_AO, G_ATT, G_BO, G_WO = 0, 8, 20, 32, 44, 48, 52, 56
G_FFN1 = 60
G_EV = G_FFN1 + 3 * FG
G_UQ, G_UKV, G_EVO = G_EV + 8, G_EV + 11, G_EV + 12
G_F2A = G_EVO + 4
G_QK = G_F2A + 2 * FP
G_V, G_ODO = G_QK + 8, G_QK + 12
G_F2B = G_ODO + 4
G_END = G_F2B + 2 * FP

LOW4 = {0: 1, 1: 1, 2: 1, 3: 1}
HIGH4 = {4: 1, 5: 1, 6: 1, 7: 1}
HEADS16 = {2: 8, 3: 8, **HIGH4}
PHASES = [
    ("setup", {0: 1, 1: 1}), ("n_mem", LOW4), ("kv", {**LOW4, **HIGH4}), ("n_mix", LOW4),
    ("ugq", {1: 4, 2: 4}), ("cvb", {0: 4, 1: 4, 2: 4}), ("gate", {0: 4, 1: 4, 2: 4}),
    ("a_out", LOW4), ("att1", {2: 2, 3: 2, **HIGH4}), ("o1", LOW4), ("att_out", LOW4), ("b_out", LOW4),
    ("w_o", HIGH4), ("n_ffn", LOW4), ("ffn1", {0: FG, 1: FG, **HIGH4}), ("n_mix2a", LOW4),
    ("ev_in", {0: 1, 1: 1, 2: 1, 3: 1, 4: 1, 5: 1}), ("lat", {0: 1, 1: 1, 2: 1}), ("uq", LOW4), ("ukv", HIGH4),
    ("ev_tr", {0: 3, 1: 3, 2: 3, 3: 2}), ("att2", HEADS16), ("o2", LOW4), ("ev_out", HIGH4),
    ("n_ffn2a", LOW4), ("ffn2a", HIGH4), ("n_mix2b", LOW4),
    ("qk", {0: 2, 1: 2, 2: 2, 3: 2}), ("v", HIGH4), ("att3", HEADS16), ("o3", LOW4), ("od_out", HIGH4),
    ("n_ffn2b", LOW4), ("ffn2b", HIGH4),
]


def earlier_bank_uses():
    count, uses = [0] * 8, {}
    for name, used in PHASES:
        uses[name] = list(count)
        for bank, n in used.items():
            count[bank] += n
    return uses


USES = earlier_bank_uses()
NORMS = ["n_mem", "n_mix", "n_ffn", "fin1", "n_mix2a", "n_ffn2a", "n_mix2b", "n_ffn2b", "fin2"]
TNORMS = ["n_mem", "n_mix", "n_ffn", "n_mix2a", "n_ffn2a", "n_mix2b", "n_ffn2b"]
TGAIN = [V_MEM, V_MIX, V_FFN, V_MIX2, V_FFN2, V_MIX2 + 1, V_FFN2 + 1]


def two_blocks(nc, d, out):
    with ExitStack() as ctx:
        def sb(name, shape, dt=F32):
            return ctx.enter_context(nc.sbuf_tensor(name, shape, dt))

        def sem(name):
            return ctx.enter_context(nc.semaphore(name))

        raw = sb("raw", [P, R, SLOT])
        whi = sb("whi", [P, R, SLOT], F32R)
        wlo = sb("wlo", [P, R, SLOT], F32R)
        p_hi = sb("p_hi", [P, KD * S], F32R)
        p_lo = sb("p_lo", [P, KD * S], F32R)
        q_hi = sb("q_hi", [P, KD * S], F32R)
        q_lo = sb("q_lo", [P, KD * S], F32R)
        x = sb("x", [P, T, D])
        xn = sb("xn", [P, T, D])
        kreg = sb("kreg", [P, 2048])
        vreg = sb("vreg", [P, 2048])
        qreg = sb("qreg", [P, 2048])
        gates = sb("gates", [P, 3 * KD * S])
        merged = sb("merged", [P, KD * S])
        UP = K_B - 1 + S
        misc = sb("misc", [P, KD * UP + KD * S])
        work = sb("work", [P, 2560])
        vec = sb("vec", [P, KD * NV])
        cwf = sb("cwf", [P, K_F * FT])
        ident = sb("ident", [P, P])
        mean_w = sb("mean_w", [P, P])
        stat = sb("stat", [P, 192])
        ps = ctx.enter_context(nc.psum_tensor("ps", [P, 8, BW], F32))

        ss, ms, rr = stat[:, 0:18], stat[:, 18:36], stat[:, 36:54]
        mhalf = stat[:, 54:74]
        att_max, att_nmax = stat[:, 74:78], stat[:, 78:82]
        att_sum, att_rs = stat[:, 82:114], stat[:, 114:146]
        hss, hr = stat[:, 146:166], stat[:, 166:186]
        lat = stat[:, 186:190]

        def gain(row, c):
            return vec[:, c * NV + row:c * NV + row + 1]

        def bank(b, a=0, z=BW):
            return ps[:, b, a:z]

        mem_rows = merged[:, :].rearrange("p (t n) -> p t n", t=T)
        vec_rows = gates[0:NV, 0:D]
        cwf_rows = gates[0:FT, D:D + K_F * P]
        uglu = misc[:, 0:KD * UP].rearrange("p (c n) -> p c n", c=KD)
        conv = misc[:, KD * UP:KD * UP + KD * S]
        v_tok = vreg[:, :].rearrange("p (t n) -> p t n", t=T)

        ln_v, ln_half, ln_rs = xn[:, 0, 0:S], xn[:, 0, S:2 * S], xn[:, 0, 2 * S:3 * S]
        z = gates[:, 0:2 * EV_IN].rearrange("p (t n) -> p t n", t=T)
        qb = gates[:, 2880:4416].rearrange("p (t n) -> p t n", t=T)
        kf = gates[:, 4416:5952].rearrange("p (t n) -> p t n", t=T)
        kvb = qreg[:, :].rearrange("p (t n) -> p t n", t=T)
        qT_a = merged[:, 0:1024]
        kT_a = merged[:, 1024:1280]
        gq, gk = merged[:, 1280:1344], merged[:, 1344:1408]
        rope = merged[:, 1408:1792].rearrange("p (t n) -> p t n", t=T)
        gfin = merged[:, 0:1024]
        qrot = misc[:, 1408:2432].rearrange("p (t n) -> p t n", t=T)
        rpb = misc[:, 0:16 * 219].rearrange("p (h n) -> p h n", h=C_HEADS)
        bias = gates[:, 0:16 * 384].rearrange("p (h j k) -> p h j k", h=C_HEADS, j=6)
        prob = work[:, 0:1024].rearrange("p (b t n) -> p b t n", b=2, t=T)
        probT = work[:, 1024:2048].rearrange("p (b m n) -> p b m n", b=2, m=T)
        bsc = work[:, 2048:2560].rearrange("p (t n) -> p t n", t=T)

        raw_in = [sem(f"raw_in{r}") for r in range(R)]
        hi_ready = sem("hi_ready")
        lo_ready = sem("lo_ready")
        slot_used = sem("slot_used")
        bank_read = [sem(f"bank_read{b}") for b in range(8)]
        mem_in, x_in, vec_in, cwf_in = sem("mem_in"), sem("x_in"), sem("vec_in"), sem("cwf_in")
        gain_in, rope_in, rpb_in = sem("gain_in"), sem("rope_in"), sem("rpb_in")
        const_ready = sem("const_ready")
        vec_tr = sem("vec_tr")
        norm_sq, norm_ms, norm_r = sem("norm_sq"), sem("norm_ms"), sem("norm_r")
        norm_xn, norm_tr, norm_hi = sem("norm_xn"), sem("norm_tr"), sem("norm_hi")
        glu, conv_tap = sem("glu"), sem("conv_tap")
        ga_ready, ca_step, an_hi, an_lo = sem("ga_ready"), sem("ca_step"), sem("an_hi"), sem("an_lo")
        ln_mean, ln_ctr, ln_sq, ln_var = sem("ln_mean"), sem("ln_ctr"), sem("ln_sq"), sem("ln_var")
        ln_ms, ln_r, ln_z, ln_y, ln_hi, ln_lo = (sem("ln_ms"), sem("ln_r"), sem("ln_z"), sem("ln_y"),
                                                 sem("ln_hi"), sem("ln_lo"))
        mg, mg_hi, mg_lo = sem("mg"), sem("mg_hi"), sem("mg_lo")
        at_s, at_b, at_max, at_nm, at_e = sem("at_s"), sem("at_b"), sem("at_max"), sem("at_nm"), sem("at_e")
        at_t, at_o, at_rs = sem("at_t"), sem("at_o"), sem("at_rs")
        o_tr, o_hi = sem("o_tr"), sem("o_hi")
        f_y, f_c, f_s, f_u, f_hi, f_lo = sem("f_y"), sem("f_c"), sem("f_s"), sem("f_u"), sem("f_hi"), sem("f_lo")
        f2_r, f2_sq, f2_hi, f2_lo = sem("f2_r"), sem("f2_sq"), sem("f2_hi"), sem("f2_lo")
        fin_x = sem("fin_x")
        h_sq, h_ss, h_ms, h_r, h_n = sem("h_sq"), sem("h_ss"), sem("h_ms"), sem("h_r"), sem("h_n")
        l_sq, l_ms, l_r, l_x, l_tr, l_hi = sem("l_sq"), sem("l_ms"), sem("l_r"), sem("l_x"), sem("l_tr"), sem("l_hi")
        rope_a, rope_b, ev_tr, bias_step = sem("rope_a"), sem("rope_b"), sem("ev_tr"), sem("bias_step")
        out_done = sem("out_done")

        block = ctx.enter_context(nc.Block())

        def q_tile(reg, c, lo, hi, t):
            return reg[lo:hi, c * S + t * P:c * S + t * P + P]

        def heads_mem():
            for h in range(MEM_HEADS):
                yield dict(
                    q=lambda t, h=h: [q_tile(qreg, 2 * h + k, 0, P, t) for k in range(2)],
                    k=[kreg[:, (2 * h + k) * S:(2 * h + k + 1) * S] for k in range(2)],
                    v=lambda m, h=h: v_tok[:, m, h * MEM_HD:(h + 1) * MEM_HD],
                    at=h * MEM_HD, wide=MEM_HD)

        def heads_even():
            for h in range(A_HEADS):
                kv = h // (A_HEADS // A_KV)
                yield dict(
                    q=lambda t, h=h, kv=kv: [q_tile(qT_a, h % 4, HD * kv, HD * kv + HD, t)],
                    k=[kT_a[HD * kv:HD * kv + HD, :]],
                    v=lambda m, kv=kv: z[:, m, Z_V + HD * kv:Z_V + HD * kv + HD],
                    at=h * HD, wide=HD)
            for h in range(B_HEADS):
                yield dict(
                    q=lambda t, h=h: [q_tile(kreg, h, 0, B_QK, t)],
                    k=[vreg[0:B_QK, h * S:(h + 1) * S]],
                    v=lambda m, h=h: kvb[:, m, h * 128 + HD:(h + 1) * 128],
                    at=(A_HEADS + h) * HD, wide=HD)

        def heads_odd():
            for h in range(C_HEADS):
                b = HD * (h % 2)
                yield dict(
                    q=lambda t, h=h, b=b: [q_tile(qreg, h // 2, b, b + HD, t)],
                    k=[kreg[b:b + HD, h // 2 * S:(h // 2 + 1) * S]],
                    v=lambda m, h=h: v_tok[:, m, h * HD:(h + 1) * HD],
                    at=h * HD, wide=HD)

        ATT = {
            "att1": (list(heads_mem()), 0, lambda i: MEM_HD ** -0.5, False, 0),
            "att2": (list(heads_even()), 4, lambda i: (HD if i < A_HEADS else B_QK) ** -0.5, False, 1),
            "att3": (list(heads_odd()), 20, lambda i: HD ** -0.5, True, 2),
        }

        @block.sync
        def _(sp):
            sp.dma_start(mem_rows, d["mem"].rearrange("(t p) n -> p t n", p=P)).then_inc(mem_in, 16)

            def load(g, src, kk, i=0):
                n = src.shape[-1]
                if g >= R:
                    sp.wait_ge(lo_ready, g - R + 1 + R * i)
                sp.dma_start(raw[:, g % R, 0:kk * n].rearrange("p (k n) -> p k n", k=kk),
                             src).then_inc(raw_in[g % R], 16)

            def cols(w, c0):
                return d[w].rearrange("(k p) n -> p k n", p=P)[:, :, bass.ds(c0, 256)]

            def rows(w, k0, kk):
                return d[w].rearrange("(k p) n -> p k n", p=P)[:, bass.ds(k0, kk), :]

            for i in range(4):
                load(G_KV + i, cols("w_kv", 256 * i), KD)
                if i == 0:
                    sp.dma_start(x[:, :, :], d["x"].rearrange("(t p) n -> p t n", p=P)).then_inc(x_in, 16)
            for i in range(4):
                load(G_KV + 4 + i, d["w_kv"].rearrange("(k p) n -> p k n", p=P)[:, 2 * i:2 * i + 2, D:2 * D], 2)
            with sp.Fori(0, 4) as i:
                for j, c0 in enumerate((3 * D, 4 * D, 5 * D)):
                    load(G_UGQ + j, cols("w_in", c0 + 256 * i), KD, i)
            with sp.Fori(1, 5) as i:
                for j, c0 in enumerate((D, 2 * D, 0)):
                    load(G_CVB + j, cols("w_in", c0 - 256 + 256 * i), KD, i - 1)
            with sp.Fori(0, 4) as i:
                for j in range(3):
                    load(G_GATE + j, cols("w_in", (6 + j) * D + 256 * i), KD, i)
            for g0, w in ((G_AO, "w_a_out"), (G_ATT, "w_att_out"), (G_BO, "w_b_out")):
                for i in range(4):
                    load(g0 + i, cols(w, 256 * i), KD)
            for i in range(4):
                load(G_WO + i, rows("w_o", 2 * i, 2), 2)
            load(G_FFN1, cols("w_up", 0), KD)
            load(G_FFN1 + 1, cols("w_up", D_FF), KD)
            with sp.Fori(0, FG - 1) as i:
                load(G_FFN1 + 2, cols("w_up", 256 * i + 256), KD, i)
                load(G_FFN1 + 3, cols("w_up", D_FF + 256 * i + 256), KD, i)
                load(G_FFN1 + 4, rows("w_down", 2 * i, 2), 2, i)
            load(G_EV - 1, rows("w_down", 2 * FG - 2, 2), 2)
            for i in range(8):
                load(G_EV + i, rows("ev_w_in", i, 1), 1)
            for i in range(3):
                load(G_UQ + i, rows("uq", i, 1), 1)
            load(G_UKV, rows("ukv", 0, 2), 2)
            for i in range(4):
                load(G_EVO + i, rows("ev_w_out", 2 * i, 2), 2)

            def ffn2(g0, up, down):
                load(g0, cols(up, 0), KD)
                with sp.Fori(0, (FP - 1) // 3) as i:
                    for j in range(3):
                        load(g0 + 1 + 2 * j, cols(up, 768 * i + 256 * (j + 1)), KD, 2 * i)
                        load(g0 + 2 + 2 * j, rows(down, 6 * i + 2 * j, 2), 2, 2 * i)
                load(g0 + 2 * FP - 1, rows(down, 2 * FP - 2, 2), 2)

            ffn2(G_F2A, "up_a", "down_a")
            with sp.Fori(0, 2) as i:
                for j in range(3):
                    load(G_QK + j, cols("od_w_qkv", 768 * i + 256 * j), KD, i)
            for i in range(6, 8):
                load(G_QK + i, cols("od_w_qkv", 256 * i), KD)
            for i in range(4):
                load(G_V + i, d["od_w_qkv"].rearrange("(k p) n -> p k n", p=P)[:, 2 * i:2 * i + 2, 2 * D:3 * D], 2)
            for i in range(4):
                load(G_ODO + i, rows("od_w_out", 2 * i, 2), 2)
            ffn2(G_F2B, "up_b", "down_b")
            out_v = out.rearrange("(t p) n -> p t n", p=P)
            for t in range(T):
                sp.wait_ge(fin_x, T + t + 1)
                sp.dma_start(out_v[:, t, :], x[:, t, :]).then_inc(out_done, 16)
            sp.wait_ge(out_done, 16 * T)

        @block.gpsimd
        def _(pool):
            pool.dma_start(vec_rows, d["vecs"]).then_inc(vec_in, 16)
            pool.dma_start(cwf_rows.rearrange("c (k p) -> c k p", k=K_F),
                           d["conv_ffn_w"].rearrange("k (c p) -> c k p", p=P)).then_inc(cwf_in, 16)
            nc.gpsimd.memset(ident[:, :], 0.0).then_inc(const_ready, 1)
            nc.gpsimd.memset(mean_w[:, :], 1.0 / D)
            nc.gpsimd.memset(mhalf, -0.5)
            pool.wait_ge(const_ready, 1)
            nc.gpsimd.affine_select(out=ident[:, :], in_=ident[:, :], compare_op=ALU.not_equal, fill=1.0, base=0,
                                    pattern=[[-1, P]], channel_multiplier=1).then_inc(const_ready, 1)
            nc.gpsimd.memset(uglu[:, :, 0:K_B - 1], 0.0).then_inc(glu, 1)
            nc.gpsimd.memset(work[:, 1344:1860].rearrange("p (b n) -> p b n", b=2)[:, :, 0:K_A - 1],
                             0.0).then_inc(ca_step, 1)

            def inverse_root(n):
                pool.wait_ge(norm_ms, n + 1)
                nc.gpsimd.tensor_tensor(out=rr[:, 2 * n:2 * n + 2], in0=ms[:, 2 * n:2 * n + 2],
                                        in1=mhalf[:, 0:2], op=ALU.pow).then_inc(norm_r, 1)

            inverse_root(0)
            inverse_root(1)
            pool.wait_ge(ln_ms, 2)
            nc.gpsimd.tensor_tensor(out=ln_rs, in0=ln_v, in1=ln_half, op=ALU.pow).then_inc(ln_r, 1)
            inverse_root(2)
            pool.wait_ge(mg_lo, 4)
            pool.dma_start(gfin, d["norm_final_g"].partition_broadcast(P)).then_inc(gain_in, 16)
            pool.dma_start(gq, d["gq"].partition_broadcast(P)).then_inc(rope_in, 16)
            pool.dma_start(gk, d["gk"].partition_broadcast(P)).then_inc(rope_in, 16)
            pool.dma_start(rope, d["rope"].rearrange("(t p) n -> p t n", p=P)).then_inc(rope_in, 16)
            inverse_root(3)
            inverse_root(4)
            pool.wait_ge(l_ms, 1)
            nc.gpsimd.tensor_tensor(out=lat, in0=lat, in1=mhalf[:, 0:4], op=ALU.pow).then_inc(l_r, 1)
            pool.wait_ge(h_ms, 1)
            nc.gpsimd.tensor_tensor(out=hr, in0=hss, in1=mhalf, op=ALU.pow).then_inc(h_r, 1)
            inverse_root(5)
            pool.wait_ge(o_tr, 2)
            pool.dma_start(gfin, d["final_norm"].partition_broadcast(P)).then_inc(gain_in, 16)
            for half in range(2):
                src = bass.AP(d["rpb_rev"].tensor, (5 - half) * RPB_W + 15 - 63,
                              [[1, GRID_W], [RPB_H * RPB_W, C_HEADS], [1, 219]])
                pool.dma_start(rpb[64 * half:64 * half + 64], src).then_inc(rpb_in, 16)
            pool.wait_ge(rpb_in, 32)
            steps = 0
            for h in range(C_HEADS):
                rev = bass.AP(misc[:, :].tensor, h * 219 + 63, [[KD * UP + KD * S, P], [RPB_W, 6], [-1, 64]])
                nc.gpsimd.tensor_copy(bias[:, h], rev).then_inc(bias_step, 1)
                steps += 1
                for c0, base, sign in ((0, 8, 1), (16, 7 - 16, -1)):
                    for half in range(2):
                        part = bias[64 * half:64 * half + 64, h, :, c0:c0 + 48]
                        pool.wait_ge(bias_step, steps)
                        nc.gpsimd.affine_select(out=part, in_=part, compare_op=ALU.is_ge, fill=NEG, base=base,
                                                pattern=[[0, 6], [sign, 48]], channel_multiplier=-sign)\
                            .then_inc(bias_step, 1)
                        steps += 1
                pool.wait_ge(bias_step, steps)
            inverse_root(6)
            inverse_root(7)
            inverse_root(8)

        @block.scalar
        def _(act):
            def hi(g, i=0):
                if isinstance(i, int):
                    g, i = g + R * i, 0
                    if g >= G_END:
                        return
                act.wait_ge(raw_in[g % R], 16 * (g // R + 1) + 16 * i)
                if g >= R:
                    act.wait_ge(slot_used, g - R + 1 + R * i)
                nc.scalar.activation(whi[:, g % R, :], raw[:, g % R, :], ACT.Copy).then_inc(hi_ready, 1)

            def squares(name, src):
                n = NORMS.index(name)
                for t in range(T):
                    nc.scalar.activation(xn[:, t, :], src[:, t, :], ACT.Square,
                                         accum_out=ss[:, 2 * n + t:2 * n + t + 1]).then_inc(norm_sq, 1)

            def normalise(name, src):
                n, m = NORMS.index(name), TNORMS.index(name)
                act.wait_ge(norm_r, n + 1)
                for t in range(T):
                    nc.scalar.activation(xn[:, t, :], src[:, t, :], ACT.Copy,
                                         scale=rr[:, 2 * n + t:2 * n + t + 1]).then_inc(norm_xn, 1)

            def norm_upper(name, dst):
                m = TNORMS.index(name)
                act.wait_ge(norm_tr, m + 1)
                for c in range(KD):
                    nc.scalar.activation(dst[:, c * S:(c + 1) * S], bank(c // 2, c % 2 * S, c % 2 * S + S), ACT.Copy,
                                         scale=gain(TGAIN[m], c)).then_inc(norm_hi, 1)

            def split_rows(k, phase):
                act.wait_ge(o_tr, k + 1)
                for b in range(4):
                    nc.scalar.activation(p_hi[:, BW * b:BW * (b + 1)], bank(b), ACT.Copy).then_inc(o_hi, 1)

            def exps(name):
                heads, i0, scale, biased, _ = ATT[name]
                for i, _h in enumerate(heads):
                    n = i0 + i
                    act.wait_ge(at_nm, n + 1)
                    if i >= 2:
                        act.wait_ge(at_t, n - 1)
                    for t in range(T):
                        src = bsc[:, t, :] if biased else bank(i % 2, t * S, t * S + S)
                        last = nc.scalar.activation(prob[:, i % 2, t, :], src, ACT.Exp,
                                                    bias=att_nmax[:, 2 * (i % 2) + t:2 * (i % 2) + t + 1],
                                                    scale=1.0 if biased else scale(i),
                                                    accum_out=att_sum[:, 16 * t + i:16 * t + i + 1])
                    last.then_inc(at_e, 1)

            act.wait_ge(vec_tr, 2)
            nc.scalar.activation(vec[:, :], bank(0, 0, KD * NV), ACT.Copy).then_inc(bank_read[0], 1)
            nc.scalar.activation(cwf[:, :], bank(1, 0, K_F * FT), ACT.Copy).then_inc(bank_read[1], 1)
            act.wait_ge(mem_in, 16)
            squares("n_mem", mem_rows)
            hi(0)
            normalise("n_mem", mem_rows)
            hi(1)
            act.wait_ge(bank_read[0], 1)
            act.wait_ge(bank_read[1], 1)
            norm_upper("n_mem", q_hi)
            hi(2)
            act.wait_ge(x_in, 16)
            squares("n_mix", x)
            normalise("n_mix", x)
            for i in range(4):
                act.wait_ge(slot_used, G_KV + i + 1)
                nc.scalar.activation(kreg[:, BW * i:BW * (i + 1)], bank(i), ACT.Copy).then_inc(bank_read[i], 1)
                hi(G_KV + i + 3)
            norm_upper("n_mix", p_hi)
            for i in range(4):
                if i == 3:
                    act.wait_ge(slot_used, G_KV + 8)
                    for b in range(4):
                        nc.scalar.activation(v_tok[:, b // 2, BW * (b % 2):BW * (b % 2) + BW], bank(4 + b),
                                             ACT.Copy).then_inc(bank_read[4 + b], 1)
                hi(G_KV + 7 + i)
            U = USES["ugq"]
            with act.Fori(0, 4) as i:
                hi(G_UGQ + 3, i)
                act.wait_ge(slot_used, G_UGQ + 2 + 3 * i)
                act.wait_ge(glu, i + 1)
                nc.scalar.activation(work[:, 832:1344], bank(1), ACT.Sigmoid).then_inc(bank_read[1], 1)
                hi(G_UGQ + 4, i)
                act.wait_ge(slot_used, G_UGQ + 3 + 3 * i)
                nc.scalar.activation(qreg[:, bass.ds(BW * i, BW)], bank(2), ACT.Copy).then_inc(bank_read[2], 1)
                hi(G_UGQ + 5, i)
            with act.Fori(0, 4) as i:
                act.wait_ge(slot_used, G_CVB + 1 + 3 * i)
                act.wait_ge(bank_read[1], USES["cvb"][1] + i)
                nc.scalar.activation(work[:, 832:1344], bank(0), ACT.Copy).then_inc(bank_read[0], 1)
                hi(G_CVB + 3, i)
                hi(G_CVB + 4, i)
                act.wait_ge(bank_read[2], USES["cvb"][2] + 1 + i)
                nc.scalar.activation(q_hi[:, bass.ds(BW * i, BW)], work[:, 1860:2372], ACT.Copy).then_inc(an_hi, 1)
                hi(G_CVB + 5, i)
            with act.Fori(0, 4) as i:
                for j in range(3):
                    act.wait_ge(slot_used, G_GATE + j + 1 + 3 * i)
                    for b in range(2):
                        last = nc.scalar.activation(
                            gates[:, bass.ds(j * KD * S + BW * i + S * b, S)], bank(j, S * b, S * b + S), ACT.Sigmoid,
                            bias=vec[:, bass.ds(2 * NV * i + b * NV + V_GATE + j, 1)])
                    last.then_inc(bank_read[j], 1)
                    hi(G_GATE + j + 3, i)
            act.wait_ge(ln_ctr, 1)
            nc.scalar.activation(xn[:, :, :].rearrange("p t n -> p (t n)"), conv, ACT.Square).then_inc(ln_sq, 1)
            for i in range(4):
                hi(G_AO + i + 3)
            exps("att1")
            act.wait_ge(ln_z, 1)
            act.wait_ge(slot_used, G_AO + 4)
            for c in range(KD):
                nc.scalar.activation(conv[:, c * S:(c + 1) * S], conv[:, c * S:(c + 1) * S], ACT.Silu,
                                     scale=gain(V_LNG, c), bias=gain(V_LNB, c)).then_inc(ln_y, 1)
            act.wait_ge(ln_y, KD)
            nc.scalar.activation(q_hi[:, :], conv, ACT.Copy).then_inc(ln_hi, 1)
            split_rows(0, "o1")
            for i in range(8):
                hi(G_ATT + i + 3)
            act.wait_ge(slot_used, G_ATT + 4)
            for i in range(4):
                act.wait_ge(mg, 4 + i + 1)
                nc.scalar.activation(p_hi[:, BW * i:BW * (i + 1)], merged[:, BW * i:BW * (i + 1)],
                                     ACT.Copy).then_inc(mg_hi, 1)
            for i in range(3):
                hi(G_WO + i + 3)

            def after_product(name, phase):
                for b in range(4, 8):
                    act.wait_ge(bank_read[b], USES[phase][b] + 1)
                squares(name, x)

            after_product("n_ffn", "w_o")
            hi(G_WO + 6)
            normalise("n_ffn", x)
            norm_upper("n_ffn", p_hi)

            def last_tap(i, part, b, n):
                act.wait_ge(slot_used, n)
                if part and not isinstance(i, int):
                    act.wait_ge(f_u, i)
                for h in range(2):
                    dst = work[:, BW * part + S * h:BW * part + S * h + S]
                    c = 2 * FT + part * (FT // 2) + 2 * i + h
                    last = nc.scalar.activation(dst, bank(b, S * h, S * h + S), ACT.Copy, scale=cwf[:, bass.ds(c, 1)])
                last.then_inc(f_y, 1)

            def silu_gate(n):
                act.wait_ge(bank_read[0], USES["ffn1"][0] + n)
                nc.scalar.activation(work[:, 1024:1536], work[:, 0:512], ACT.Silu).then_inc(f_s, 1)

            def u_upper(n):
                act.wait_ge(f_u, n)
                nc.scalar.activation(q_hi[:, 0:BW], work[:, 1536:2048], ACT.Copy).then_inc(f_hi, 1)

            last_tap(0, 0, 0, G_FFN1 + 1)
            hi(G_FFN1 + 3)
            last_tap(0, 1, 1, G_FFN1 + 2)
            silu_gate(1)
            hi(G_FFN1 + 4)
            u_upper(1)
            with act.Fori(0, FG - 1) as i:
                last_tap(i + 1, 0, 0, G_FFN1 + 3 + 3 * i)
                hi(G_FFN1 + 5, i)
                last_tap(i + 1, 1, 1, G_FFN1 + 4 + 3 * i)
                silu_gate(i + 2)
                hi(G_FFN1 + 6, i)
                act.wait_ge(slot_used, G_FFN1 + 5 + 3 * i)
                u_upper(i + 2)
                hi(G_FFN1 + 7, i)
            after_product("fin1", "ffn1")
            hi(G_EV + 2)
            act.wait_ge(fin_x, 2)
            squares("n_mix2a", x)
            normalise("n_mix2a", x)
            norm_upper("n_mix2a", p_hi)
            for i in range(7):
                hi(G_EV + i + 3)
            act.wait_ge(slot_used, G_EV + 8)
            for b in (5, 2, 4, 1, 3, 0):
                nc.scalar.activation(z[:, b // 3, 480 * (b % 3):480 * (b % 3) + 480], bank(b, 0, 480),
                                     ACT.Copy).then_inc(bank_read[b], 1)
            for b in range(6):
                act.wait_ge(bank_read[b], USES["ev_in"][b] + 1)
            for t in range(T):
                nc.scalar.activation(misc[:, 1920 * t:1920 * t + 384], z[:, t, Z_CQ:Z_CKV], ACT.Square,
                                     accum_out=lat[:, t:t + 1])
                last = nc.scalar.activation(misc[:, 1920 * t + 384:1920 * t + 640], z[:, t, Z_CKV:Z_KR], ACT.Square,
                                            accum_out=lat[:, 2 + t:3 + t])
            last.then_inc(l_sq, 1)
            for t in range(T):
                nc.scalar.activation(misc[:, 640 + 640 * t:1280 + 640 * t], z[:, t, 0:Z_V],
                                     ACT.Square).then_inc(h_sq, 1)
            hi(G_EV + 10)
            act.wait_ge(l_r, 1)
            for t in range(T):
                nc.scalar.activation(z[:, t, Z_CQ:Z_CKV], z[:, t, Z_CQ:Z_CKV], ACT.Copy, scale=lat[:, t:t + 1])
                last = nc.scalar.activation(z[:, t, Z_CKV:Z_KR], z[:, t, Z_CKV:Z_KR], ACT.Copy,
                                            scale=lat[:, 2 + t:3 + t])
            last.then_inc(l_x, 1)
            act.wait_ge(l_tr, 1)
            for c in range(5):
                nc.scalar.activation(p_hi[:, c * S:(c + 1) * S], bank(c // 2, c % 2 * S, c % 2 * S + S), ACT.Copy,
                                     scale=gain(V_LAT, c)).then_inc(l_hi, 1)
            for i in range(4):
                hi(G_UQ + i + 3)
            act.wait_ge(slot_used, G_UQ + 3)
            for b in range(4):
                nc.scalar.activation(qb[:, b // 2, 384 * (b % 2):384 * (b % 2) + 384], bank(b, 0, 384),
                                     ACT.Copy).then_inc(bank_read[b], 1)
            act.wait_ge(slot_used, G_UKV + 1)
            for b in range(4):
                nc.scalar.activation(kvb[:, b // 2, BW * (b % 2):BW * (b % 2) + BW], bank(4 + b),
                                     ACT.Copy).then_inc(bank_read[4 + b], 1)
            for i in range(11):
                act.wait_ge(ev_tr, i + 1)
                n, b = BW, i % 4
                if i < 2:
                    dst = qT_a[:, BW * i:BW * i + BW]
                elif i == 2:
                    dst, n = kT_a, S
                else:
                    reg = kreg if i < 7 else vreg
                    dst = reg[0:B_QK, BW * ((i - 3) % 4):BW * ((i - 3) % 4) + BW]
                src = ps[0:B_QK, b, :] if i > 2 else bank(b, 0, n)
                nc.scalar.activation(dst, src, ACT.Copy).then_inc(bank_read[b], 1)
            exps("att2")
            split_rows(1, "o2")
            for i in range(3):
                hi(G_EVO + i + 3)
            after_product("n_ffn2a", "ev_out")
            hi(G_EVO + 6)
            normalise("n_ffn2a", x)
            norm_upper("n_ffn2a", p_hi)

            def group(k, n, slot, up, i=0):
                act.wait_ge(slot_used, up + 1 + 6 * i)
                if FP * k + n > 0:
                    act.wait_ge(f2_sq, FP * k + n + 3 * i)
                nc.scalar.activation(work[:, 0:BW], bank(slot), ACT.Relu).then_inc(f2_r, 1)
                hi(up + 3, 2 * i)
                act.wait_ge(f2_sq, FP * k + n + 1 + 3 * i)
                nc.scalar.activation(q_hi[:, BW * slot:BW * slot + BW], work[:, 1024:1536], ACT.Copy).then_inc(f2_hi, 1)

            def ffn2(k, g0):
                group(k, 0, 0, g0)

                def three(i):
                    for j in range(3):
                        group(k, 1 + j, (1 + j) % 3, g0 + 1 + 2 * j, i)
                        hi(g0 + 5 + 2 * j, 2 * i)

                with act.Fori(0, (FP - 1) // 3 - 1) as i:
                    three(i)
                three((FP - 1) // 3 - 1)

            ffn2(0, G_F2A)
            after_product("n_mix2b", "ffn2a")
            hi(G_QK + 2)
            normalise("n_mix2b", x)
            norm_upper("n_mix2b", p_hi)
            for i in range(8):
                act.wait_ge(slot_used, G_QK + i + 1)
                reg = qreg if i < 4 else kreg
                nc.scalar.activation(reg[:, BW * (i % 4):BW * (i % 4) + BW], bank(i % 4), ACT.Copy)\
                    .then_inc(bank_read[i % 4], 1)
                hi(G_QK + i + 3)
            for i in range(4):
                if i == 3:
                    act.wait_ge(slot_used, G_V + 4)
                    for b in range(4):
                        nc.scalar.activation(v_tok[:, b // 2, BW * (b % 2):BW * (b % 2) + BW], bank(4 + b),
                                             ACT.Copy).then_inc(bank_read[4 + b], 1)
                hi(G_V + i + 3)
            exps("att3")
            split_rows(2, "o3")
            for i in range(3):
                hi(G_ODO + i + 3)
            after_product("n_ffn2b", "od_out")
            hi(G_ODO + 6)
            normalise("n_ffn2b", x)
            norm_upper("n_ffn2b", p_hi)
            ffn2(1, G_F2B)
            after_product("fin2", "ffn2b")

        @block.vector
        def _(dve):
            def lo(g, i=0):
                if isinstance(i, int):
                    g, i = g + R * i, 0
                    if g >= G_END:
                        return
                dve.wait_ge(hi_ready, g + 1 + R * i)
                nc.vector.tensor_tensor(wlo[:, g % R, :], raw[:, g % R, :], whi[:, g % R, :].bitcast(F32),
                                        ALU.subtract).then_inc(lo_ready, 1)

            def mean_squares(name):
                n = NORMS.index(name)
                dve.wait_ge(norm_sq, 2 * n + 2)
                nc.vector.tensor_scalar(ms[:, 2 * n:2 * n + 2], ss[:, 2 * n:2 * n + 2], 1.0 / D, EPS,
                                        ALU.mult, ALU.add).then_inc(norm_ms, 1)

            def norm_lower(name, hi_part, lo_part):
                m = TNORMS.index(name)
                for c in range(KD):
                    dve.wait_ge(norm_hi, KD * m + c // 2 * 2 + 2)
                    last = nc.vector.scalar_tensor_tensor(
                        out=lo_part[:, c * S:(c + 1) * S], in0=bank(c // 2, c % 2 * S, c % 2 * S + S),
                        scalar=gain(TGAIN[m], c), in1=hi_part[:, c * S:(c + 1) * S].bitcast(F32),
                        op0=ALU.mult, op1=ALU.subtract)
                    if c % 2:
                        last.then_inc(bank_read[c // 2], 1)

            def split_rows(k):
                for b in range(4):
                    dve.wait_ge(o_hi, 4 * k + b + 1)
                    nc.vector.tensor_tensor(p_lo[:, BW * b:BW * (b + 1)], bank(b),
                                            p_hi[:, BW * b:BW * (b + 1)].bitcast(F32),
                                            ALU.subtract).then_inc(bank_read[b], 1)

            def residual(g_end):
                dve.wait_ge(slot_used, g_end)
                for b in range(4):
                    rows = x[:, b // 2, BW * (b % 2):BW * (b % 2) + BW]
                    nc.vector.tensor_tensor(rows, rows, bank(4 + b), ALU.add).then_inc(bank_read[4 + b], 1)

            def attention(name):
                heads, n0, scale, biased, k = ATT[name]
                for i in range(len(heads) + 1):
                    n = n0 + i
                    if i < len(heads):
                        dve.wait_ge(at_s, n + 1)
                        both = ps[:, i % 2, :].rearrange("p (t n) -> p t n", t=T)
                        pair = slice(2 * (i % 2), 2 * (i % 2) + 2)
                        if biased:
                            if i:
                                dve.wait_ge(at_e, n)
                            else:
                                dve.wait_ge(bias_step, 5 * C_HEADS)
                            for t in range(T):
                                last = nc.vector.scalar_tensor_tensor(
                                    out=bsc[:, t, :], in0=both[:, t, :], scalar=scale(i),
                                    in1=bias[:, i, 2 - 2 * t:6 - 2 * t, :].rearrange("p j k -> p (j k)"),
                                    op0=ALU.mult, op1=ALU.add)
                            last.then_inc(at_b, 1)
                            dve.wait_ge(at_b, i + 1)
                            both = bsc
                        nc.vector.tensor_reduce(out=att_max[:, pair], in_=both, axis=AX.X, op=ALU.max)\
                            .then_inc(at_max, 1)
                        dve.wait_ge(at_max, n + 1)
                        nc.vector.tensor_scalar(att_nmax[:, pair], att_max[:, pair],
                                                -1.0 if biased else -scale(i), None, ALU.mult).then_inc(at_nm, 1)
                    if i:
                        dve.wait_ge(at_t, n)
                        b = 2 + (i - 1) % 2
                        nc.vector.tensor_copy(probT[:, (i - 1) % 2].rearrange("p m n -> p (m n)"), bank(b))\
                            .then_inc(bank_read[b], 1)
                sums = att_sum.rearrange("p (t h) -> p t h", t=T)[:, :, 0:len(heads)]
                inv = att_rs.rearrange("p (t h) -> p t h", t=T)[:, :, 0:len(heads)]
                dve.wait_ge(at_e, n0 + len(heads))
                nc.vector.reciprocal(inv, sums).then_inc(at_rs, 1)
                dve.wait_ge(at_rs, k + 1)
                dve.wait_ge(at_o, k + 1)
                wide = heads[0]["wide"]
                m = BW // wide
                for b in range(4):
                    t, half = b // 2, b % 2
                    nc.vector.tensor_tensor(
                        xn[:, t, BW * half:BW * half + BW].rearrange("p (h n) -> p h n", h=m),
                        bank(4 + b).rearrange("p (h n) -> p h n", h=m),
                        inv[:, t, m * half:m * half + m].unsqueeze(2).to_broadcast([P, m, wide]),
                        ALU.mult).then_inc(bank_read[4 + b], 1)

            mean_squares("n_mem")
            lo(0)
            lo(1)
            norm_lower("n_mem", q_hi, q_lo)
            lo(2)
            mean_squares("n_mix")
            for i in range(4):
                lo(G_KV + 3 + i)
            norm_lower("n_mix", p_hi, p_lo)
            for i in range(4):
                lo(G_KV + 7 + i)

            acc = [work[:, 320:576], work[:, 576:832]]
            TAPS = K_B + 3

            def conv_part(c, base, part, glu_at):
                if part == 0:
                    dve.wait_ge(glu, glu_at)
                    nc.vector.tensor_copy(work[:, 0:UP], misc[:, bass.ds(c * UP, UP)]).then_inc(conv_tap, 1)
                    nc.vector.tensor_copy(work[:, UP:UP + K_B], vec[:, bass.ds(c * NV + V_CONVB, K_B)])\
                        .then_inc(conv_tap, 1)
                    dve.wait_ge(conv_tap, base + 2)
                for k in (range(0, 10), range(10, 21), range(21, K_B))[part]:
                    src, w = work[:, k:k + S], work[:, UP + k:UP + k + 1]
                    if k < 2:
                        nc.vector.tensor_scalar(acc[k], src, w, None, ALU.mult).then_inc(conv_tap, 1)
                    else:
                        dve.wait_ge(conv_tap, base + k + 1)
                        nc.vector.scalar_tensor_tensor(out=acc[k % 2], in0=src, scalar=w, in1=acc[k % 2],
                                                       op0=ALU.mult, op1=ALU.add).then_inc(conv_tap, 1)
                if part == 2:
                    dve.wait_ge(conv_tap, base + TAPS - 1)
                    nc.vector.scalar_tensor_tensor(
                        out=conv[:, bass.ds(c * S, S)], in0=acc[0], scalar=vec[:, bass.ds(c * NV + V_CBIAS, 1)],
                        in1=acc[1], op0=ALU.add, op1=ALU.add).then_inc(conv_tap, 1)

            def ugq(i, with_conv):
                lo(G_UGQ + 3, i)
                if with_conv:
                    conv_part(i - 1, TAPS * (i - 1), 0, i + 1)
                dve.wait_ge(bank_read[1], USES["ugq"][1] + 1 + i)
                sig = work[:, 832:1344].rearrange("p (b n) -> p b n", b=2)
                dst = misc[:, bass.ds(2 * UP * i, 2 * UP)].rearrange("p (b n) -> p b n", b=2)[:, :, K_B - 1:UP]
                nc.vector.tensor_tensor(dst, ps[:, 0, :].rearrange("p (b n) -> p b n", b=2), sig,
                                        ALU.mult).then_inc(glu, 1)
                lo(G_UGQ + 4, i)
                if with_conv:
                    conv_part(i - 1, TAPS * (i - 1), 1, 0)
                lo(G_UGQ + 5, i)
                if with_conv:
                    conv_part(i - 1, TAPS * (i - 1), 2, 0)

            ugq(0, False)
            with dve.Fori(1, 4) as i:
                ugq(i, True)
            gcv = work[:, 1344:1860].rearrange("p (b n) -> p b n", b=2)
            ca = work[:, 1860:2372]
            with dve.Fori(0, 4) as i:
                dve.wait_ge(bank_read[0], USES["cvb"][0] + 1 + i)
                dve.wait_ge(slot_used, G_CVB + 2 + 3 * i)
                nc.vector.tensor_tensor(gcv[:, :, K_A - 1:K_A - 1 + S], ps[:, 1, :].rearrange("p (b n) -> p b n", b=2),
                                        work[:, 832:1344].rearrange("p (b n) -> p b n", b=2),
                                        ALU.mult).then_inc(bank_read[1], 1)
                lo(G_CVB + 3, i)
                conv_part(i + 3, TAPS * 3 + TAPS * i, 0, 5)
                dve.wait_ge(bank_read[1], USES["cvb"][1] + 1 + i)
                for m in range(2 * K_A):
                    b, k = m % 2, K_A - 1 - m // 2
                    src = gcv[:, b, k:k + S]
                    w = vec[:, bass.ds(2 * NV * i + b * NV + V_CONVA + k, 1)]
                    dst = ca[:, b * S:(b + 1) * S]
                    if m < 2:
                        nc.vector.tensor_scalar(dst, src, w, None, ALU.mult).then_inc(ca_step, 1)
                    else:
                        dve.wait_ge(ca_step, 2 * K_A * i + m)
                        nc.vector.scalar_tensor_tensor(out=dst, in0=src, scalar=w, in1=dst, op0=ALU.mult,
                                                       op1=ALU.add).then_inc(ca_step, 1)
                lo(G_CVB + 4, i)
                conv_part(i + 3, TAPS * 3 + TAPS * i, 1, 5)
                dve.wait_ge(slot_used, G_CVB + 3 + 3 * i)
                dve.wait_ge(ca_step, 2 * K_A * i + 2 * K_A + 1)
                nc.vector.tensor_tensor(ca, bank(2), ca, ALU.mult).then_inc(bank_read[2], 1)
                lo(G_CVB + 5, i)
                conv_part(i + 3, TAPS * 3 + TAPS * i, 2, 5)
                dve.wait_ge(an_hi, i + 1)
                nc.vector.tensor_tensor(q_lo[:, bass.ds(BW * i, BW)], ca, q_hi[:, bass.ds(BW * i, BW)].bitcast(F32),
                                        ALU.subtract).then_inc(an_lo, 1)
            for j in range(3):
                lo(G_GATE + 3 + j)
                conv_part(KD - 1, TAPS * (KD - 1), j, 5)
            with dve.Fori(1, 4) as i:
                for j in range(3):
                    lo(G_GATE + 3 + j, i)
            dve.wait_ge(ln_mean, 1)
            conv_t = conv.rearrange("p (c n) -> p c n", c=KD)
            nc.vector.tensor_tensor(conv_t, conv_t, bank(3, 0, S).unsqueeze(1).to_broadcast([P, KD, S]),
                                    ALU.subtract).then_inc(ln_ctr, 1)

            def gate_of(j, i):
                return gates[:, j * KD * S + BW * i:j * KD * S + BW * (i + 1)]

            for i in range(4):
                dve.wait_ge(slot_used, G_AO + i + 1)
                nc.vector.tensor_tensor(merged[:, BW * i:BW * (i + 1)], bank(i), gate_of(0, i),
                                        ALU.mult).then_inc(bank_read[i], 1)
                lo(G_AO + i + 3)
            dve.wait_ge(ln_var, 1)
            nc.vector.memset(ln_half, -0.5).then_inc(ln_ms, 1)
            nc.vector.tensor_scalar(ln_v, bank(3, 0, S), EPS, None, ALU.add).then_inc(ln_ms, 1)
            dve.wait_ge(ln_r, 1)
            nc.vector.tensor_tensor(conv_t, conv_t, ln_rs.unsqueeze(1).to_broadcast([P, KD, S]),
                                    ALU.mult).then_inc(ln_z, 1)
            attention("att1")
            split_rows(0)
            dve.wait_ge(ln_hi, 1)
            nc.vector.tensor_tensor(q_lo[:, :], conv, q_hi[:, :].bitcast(F32), ALU.subtract).then_inc(ln_lo, 1)

            def merge(j, g0, count):
                for i in range(4):
                    dve.wait_ge(slot_used, g0 + i + 1)
                    nc.vector.tensor_tensor(gate_of(j, i), bank(i), gate_of(j, i), ALU.mult).then_inc(bank_read[i], 1)
                    dve.wait_ge(bank_read[i], USES[count][i] + 1)
                    nc.vector.tensor_tensor(merged[:, BW * i:BW * (i + 1)], merged[:, BW * i:BW * (i + 1)],
                                            gate_of(j, i), ALU.add).then_inc(mg, 1)
                    lo(g0 + i + 3)

            merge(2, G_ATT, "att_out")
            merge(1, G_BO, "b_out")
            for i in range(4):
                dve.wait_ge(mg_hi, i + 1)
                nc.vector.tensor_tensor(p_lo[:, BW * i:BW * (i + 1)], merged[:, BW * i:BW * (i + 1)],
                                        p_hi[:, BW * i:BW * (i + 1)].bitcast(F32), ALU.subtract).then_inc(mg_lo, 1)
            for i in range(3):
                lo(G_WO + i + 3)
            residual(G_WO + 4)
            mean_squares("n_ffn")
            lo(G_WO + 6)
            norm_lower("n_ffn", p_hi, p_lo)

            def other_taps(i, part, n):
                dve.wait_ge(f_y, n + 1)
                for m in range(4):
                    h, k = m % 2, 1 - m // 2
                    back = K_F - 1 - k
                    dst = work[:, BW * part + S * h + back:BW * part + S * h + S]
                    w = cwf[:, bass.ds(k * FT + part * (FT // 2) + 2 * i + h, 1)]
                    if k == 0:
                        dve.wait_ge(f_c, 2 * n + h + 1)
                    last = nc.vector.scalar_tensor_tensor(out=dst, in0=bank(part, S * h, S * h + S - back), scalar=w,
                                                          in1=dst, op0=ALU.mult, op1=ALU.add)
                    if k == 1:
                        last.then_inc(f_c, 1)
                last.then_inc(bank_read[part], 1)

            def gated(n):
                dve.wait_ge(f_s, n + 1)
                dve.wait_ge(bank_read[1], USES["ffn1"][1] + n + 1)
                nc.vector.tensor_tensor(work[:, 1536:2048], work[:, 1024:1536], work[:, 512:1024],
                                        ALU.mult).then_inc(f_u, 1)

            def u_lower(n):
                dve.wait_ge(f_hi, n + 1)
                nc.vector.tensor_tensor(q_lo[:, 0:BW], work[:, 1536:2048], q_hi[:, 0:BW].bitcast(F32),
                                        ALU.subtract).then_inc(f_lo, 1)

            other_taps(0, 0, 0)
            lo(G_FFN1 + 3)
            other_taps(0, 1, 1)
            gated(0)
            lo(G_FFN1 + 4)
            u_lower(0)
            with dve.Fori(0, FG - 1) as i:
                other_taps(i + 1, 0, 2 * i + 2)
                lo(G_FFN1 + 5, i)
                other_taps(i + 1, 1, 2 * i + 3)
                gated(i + 1)
                lo(G_FFN1 + 6, i)
                u_lower(i + 1)
                lo(G_FFN1 + 7, i)
            residual(G_EV)
            mean_squares("fin1")
            lo(G_EV + 2)

            def final_norm(name, k):
                n = NORMS.index(name)
                dve.wait_ge(norm_r, n + 1)
                dve.wait_ge(gain_in, 16 * (k + 1))
                for t in range(T):
                    nc.vector.scalar_tensor_tensor(out=x[:, t, :], in0=x[:, t, :], scalar=rr[:, 2 * n + t:2 * n + t + 1],
                                                   in1=gfin, op0=ALU.mult, op1=ALU.mult).then_inc(fin_x, 1)

            final_norm("fin1", 0)
            mean_squares("n_mix2a")
            norm_lower("n_mix2a", p_hi, p_lo)
            for i in range(7):
                lo(G_EV + i + 3)
            dve.wait_ge(l_sq, 1)
            nc.vector.tensor_scalar(lat[:, 0:2], lat[:, 0:2], 1.0 / B_Q_RANK, EPS, ALU.mult, ALU.add)
            nc.vector.tensor_scalar(lat[:, 2:4], lat[:, 2:4], 1.0 / B_KV_RANK, EPS, ALU.mult, ALU.add).then_inc(l_ms, 1)
            NH = A_HEADS + A_KV
            dve.wait_ge(h_sq, 2)
            nc.vector.tensor_reduce(out=hss, in_=misc[:, 640:1920].rearrange("p (h n) -> p h n", n=HD), axis=AX.X,
                                    op=ALU.add).then_inc(h_ss, 1)
            dve.wait_ge(h_ss, 1)
            nc.vector.tensor_scalar(hss, hss, 1.0 / HD, EPS, ALU.mult, ALU.add).then_inc(h_ms, 1)
            lo(G_EV + 10)
            for c in range(5):
                dve.wait_ge(l_hi, min(c // 2 * 2 + 2, 5))
                last = nc.vector.scalar_tensor_tensor(
                    out=p_lo[:, c * S:(c + 1) * S], in0=bank(c // 2, c % 2 * S, c % 2 * S + S), scalar=gain(V_LAT, c),
                    in1=p_hi[:, c * S:(c + 1) * S].bitcast(F32), op0=ALU.mult, op1=ALU.subtract)
                if c in (1, 3, 4):
                    last.then_inc(bank_read[c // 2], 1)
            for i in range(4):
                lo(G_UQ + i + 3)

            dve.wait_ge(h_r, 1)
            dve.wait_ge(rope_in, 48)
            for t in range(T):
                heads = z[:, t, 0:Z_V].rearrange("p (h n) -> p h n", h=NH)
                nc.vector.tensor_tensor(heads, heads, hr[:, NH * t:NH * t + NH].unsqueeze(2).to_broadcast([P, NH, HD]),
                                        ALU.mult).then_inc(h_n, 1)
            dve.wait_ge(h_n, 2)
            for t in range(T):
                for h0, nh, g in ((0, A_HEADS, gq), (A_HEADS, A_KV, gk)):
                    part = z[:, t, HD * h0:HD * (h0 + nh)].rearrange("p (h n) -> p h n", h=nh)
                    nc.vector.tensor_tensor(part, part, g.unsqueeze(1).to_broadcast([P, nh, HD]),
                                            ALU.mult).then_inc(h_n, 1)
            dve.wait_ge(h_n, 6)

            def rotate(part, nh, width, cos, sin, m1, m2, step, done, free=0, pairs=None):
                if free:
                    dve.wait_ge(done, free)
                one = m1.rearrange("p (h n) -> p h n", h=nh)
                nc.vector.tensor_tensor(one, part, cos.unsqueeze(1).to_broadcast([P, nh, width]), ALU.mult)
                two = m2.rearrange("p (h n) -> p h n", h=nh)

                def side(a, s):
                    return a.rearrange("p h (r s n) -> p h r s n", r=2, s=2)[:, :, :, s, :]

                sin_b = sin.unsqueeze(1).to_broadcast([P, nh, width])
                nc.vector.tensor_tensor(side(two, 0), side(part, 1), side(sin_b, 0), ALU.mult)
                nc.vector.tensor_tensor(side(two, 1), side(part, 0), side(sin_b, 1), ALU.mult).then_inc(step[0], 1)
                dve.wait_ge(step[0], step[1])
                if nh == NH:
                    def by_pair(a):
                        return a[:, 0:A_HEADS, :].rearrange("p (v h) n -> p v h n", v=A_KV)

                    nc.vector.tensor_tensor(pairs.rearrange("p (h v n) -> p v h n", h=A_HEADS // A_KV, v=A_KV),
                                            by_pair(one), by_pair(two), ALU.add)
                    part, one, two = part[:, A_HEADS:NH, :], one[:, A_HEADS:NH, :], two[:, A_HEADS:NH, :]
                nc.vector.tensor_tensor(part, one, two, ALU.add).then_inc(done, 1)

            for t in range(T):
                rotate(z[:, t, 0:Z_V].rearrange("p (h n) -> p h n", h=NH), NH, HD, rope[:, t, 0:64],
                       rope[:, t, 64:128], misc[:, 0:640], misc[:, 640:1280], (h_n, 7 + t), rope_a,
                       t, qrot[:, t, :])
            for t in range(T):
                rotate(z[:, t, Z_KR:EV_IN].unsqueeze(1), 1, B_ROPE, rope[:, t, 128:160], rope[:, t, 160:192],
                       misc[:, 1280:1312], misc[:, 1312:1344], (h_n, 9 + t), rope_a, 3 * t)
            dve.wait_ge(rope_a, 4)
            for b in range(4, 8):
                dve.wait_ge(bank_read[b], USES["ukv"][b] + 1)
            for t in range(T):
                keys = kf[:, t, :].rearrange("p (h n) -> p h n", h=B_HEADS)
                nc.vector.tensor_copy(keys[:, :, B_NOPE:B_QK],
                                      z[:, t, Z_KR:EV_IN].unsqueeze(1).to_broadcast([P, B_HEADS, B_ROPE]))
                nc.vector.tensor_copy(keys[:, :, 0:B_NOPE],
                                      kvb[:, t, :].rearrange("p (h n) -> p h n", h=B_HEADS)[:, :, 0:B_NOPE])\
                    .then_inc(rope_b, 1)
            for b in range(4):
                dve.wait_ge(bank_read[b], USES["uq"][b] + 1)
            for t in range(T):
                rotate(qb[:, t, :].rearrange("p (h n) -> p h n", h=B_HEADS)[:, :, B_NOPE:B_QK], B_HEADS, B_ROPE,
                       rope[:, t, 128:160], rope[:, t, 160:192], misc[:, 0:256], misc[:, 256:512],
                       (h_n, 11 + t), rope_b, 3 * t)
            attention("att2")
            split_rows(1)
            for i in range(3):
                lo(G_EVO + i + 3)
            residual(G_EVO + 4)
            mean_squares("n_ffn2a")
            lo(G_EVO + 6)
            norm_lower("n_ffn2a", p_hi, p_lo)

            def group(k, n, slot, up, i=0):
                dve.wait_ge(f2_r, FP * k + n + 1 + 3 * i)
                if FP * k + n > 0:
                    dve.wait_ge(f2_lo, FP * k + n + 3 * i)
                nc.vector.tensor_tensor(work[:, 1024:1536], work[:, 0:BW], work[:, 0:BW], ALU.mult).then_inc(f2_sq, 1)
                lo(up + 3, 2 * i)
                dve.wait_ge(f2_hi, FP * k + n + 1 + 3 * i)
                nc.vector.tensor_tensor(q_lo[:, BW * slot:BW * slot + BW], work[:, 1024:1536],
                                        q_hi[:, BW * slot:BW * slot + BW].bitcast(F32), ALU.subtract).then_inc(f2_lo, 1)

            def ffn2(k, g0):
                group(k, 0, 0, g0)

                def three(i):
                    for j in range(3):
                        group(k, 1 + j, (1 + j) % 3, g0 + 1 + 2 * j, i)
                        lo(g0 + 5 + 2 * j, 2 * i)

                with dve.Fori(0, (FP - 1) // 3 - 1) as i:
                    three(i)
                three((FP - 1) // 3 - 1)

            ffn2(0, G_F2A)
            residual(G_QK)
            mean_squares("n_mix2b")
            lo(G_QK + 2)
            norm_lower("n_mix2b", p_hi, p_lo)
            for i in range(8):
                lo(G_QK + i + 3)
            for i in range(4):
                lo(G_V + i + 3)
            attention("att3")
            split_rows(2)
            for i in range(3):
                lo(G_ODO + i + 3)
            residual(G_ODO + 4)
            mean_squares("n_ffn2b")
            lo(G_ODO + 6)
            norm_lower("n_ffn2b", p_hi, p_lo)
            ffn2(1, G_F2B)
            residual(G_END)
            mean_squares("fin2")
            final_norm("fin2", 1)

        @block.tensor
        def _(pe):
            def three_passes(dst, w_at, x_at, weights_first, first, last):
                (wh, wl), (xh, xl) = w_at, x_at
                for n, (w, a) in enumerate(((wh, xh), (wh, xl), (wl, xh))):
                    lhs, rhs = (w, a) if weights_first else (a, w)
                    ins = nc.tensor.matmul(dst, lhs, rhs, start=first and n == 0, stop=last and n == 2)
                return ins

            def to_channels(g, b, pair, i=0):
                pe.wait_ge(lo_ready, g + 1 + R * i)
                r = g % R
                for h in range(2):
                    for k in range(KD):
                        at = slice(256 * k + P * h, 256 * k + P * h + P)
                        ins = three_passes(bank(b, S * h, S * h + S), (whi[:, r, at], wlo[:, r, at]),
                                           [a[:, S * k:S * k + S] for a in pair], True, k == 0, k == KD - 1)
                ins.then_inc(slot_used, 1)

            def to_rows(g, tiles, pair, k0, b0, nb, n, first, last, i=0):
                pe.wait_ge(lo_ready, g + 1 + R * i)
                r = g % R
                for k in range(tiles):
                    for t in range(T):
                        at = S * (k0 + k) + P * t
                        for m in range(nb):
                            c0 = k * nb * n + m * n
                            ins = three_passes(bank(b0 + nb * t + m, 0, n), (whi[:, r, c0:c0 + n], wlo[:, r, c0:c0 + n]),
                                               [a[:, at:at + P] for a in pair], False,
                                               first and k == 0, last and k == tiles - 1)
                ins.then_inc(slot_used, 1)

            def free(b, n):
                if n > 0:
                    pe.wait_ge(bank_read[b], n)

            def transpose_norm(name):
                m = TNORMS.index(name)
                for b in range(4):
                    free(b, USES[name][b])
                for t in range(T):
                    pe.wait_ge(norm_xn, T * m + t + 1)
                    for c in range(KD):
                        last = nc.tensor.transpose(bank(c // 2, c % 2 * S + P * t, c % 2 * S + P * t + P),
                                                   xn[:, t, P * c:P * c + P], ident[:, :])
                last.then_inc(norm_tr, 1)

            def transpose_rows(phase, att):
                for b in range(4, 8):
                    free(b, USES[att][b] + 1)
                for b in range(4):
                    free(b, USES[phase][b])
                for t in range(T):
                    for c in range(KD):
                        last = nc.tensor.transpose(bank(c // 2, c % 2 * S + P * t, c % 2 * S + P * t + P),
                                                   xn[:, t, P * c:P * c + P], ident[:, :])
                last.then_inc(o_tr, 1)

            def ready_low(phase):
                for b in range(4):
                    free(b, USES[phase][b] + 1)

            def attention(name):
                heads, n0, scale, biased, k = ATT[name]
                N = len(heads)
                for b in (0, 1):
                    free(b, USES[name][b])
                for i in range(N + 2):
                    n = n0 + i
                    if i < N:
                        if i >= 2:
                            pe.wait_ge(at_b, i - 1) if biased else pe.wait_ge(at_e, n - 1)
                        for t in range(T):
                            qs, ks = heads[i]["q"](t), heads[i]["k"]
                            for j in range(len(qs)):
                                ins = nc.tensor.matmul(bank(i % 2, S * t, S * t + S), qs[j], ks[j],
                                                       start=j == 0, stop=j == len(qs) - 1)
                        ins.then_inc(at_s, 1)
                    if 1 <= i <= N:
                        b = 2 + (i - 1) % 2
                        free(b, USES[name][b] + (i - 1) // 2)
                        pe.wait_ge(at_e, n)
                        for m in range(2):
                            for t in range(T):
                                ins = nc.tensor.transpose(bank(b, S * m + P * t, S * m + P * t + P),
                                                          prob[:, (i - 1) % 2, t, P * m:P * m + P], ident[:, :])
                        ins.then_inc(at_t, 1)
                    if i >= 2:
                        h, b = heads[i - 2], 2 + i % 2
                        free(b, USES[name][b] + (i - 2) // 2 + 1)
                        if i == 2:
                            for b in range(4, 8):
                                free(b, USES[name][b])
                        for t in range(T):
                            for m in range(2):
                                ins = nc.tensor.matmul(
                                    bank(4 + 2 * t + h["at"] // BW, h["at"] % BW, h["at"] % BW + h["wide"]),
                                    probT[:, i % 2, m, P * t:P * t + P], h["v"](m), start=m == 0, stop=m == 1)
                ins.then_inc(at_o, 1)

            p_pair, q_pair = (p_hi, p_lo), (q_hi, q_lo)

            pe.wait_ge(const_ready, 2)
            pe.wait_ge(vec_in, 16)
            for c in range(KD):
                last = nc.tensor.transpose(bank(0, NV * c, NV * (c + 1)), vec_rows[:, P * c:P * c + P],
                                           ident[0:NV, 0:NV])
            last.then_inc(vec_tr, 1)
            pe.wait_ge(cwf_in, 16)
            for k in range(K_F):
                last = nc.tensor.transpose(bank(1, FT * k, FT * (k + 1)), cwf_rows[:, P * k:P * k + P],
                                           ident[0:FT, 0:FT])
            last.then_inc(vec_tr, 1)
            transpose_norm("n_mem")
            ready_low("n_mem")
            for i in range(4):
                to_channels(G_KV + i, i, q_pair)
            transpose_norm("n_mix")
            for i in range(4):
                to_rows(G_KV + 4 + i, 2, q_pair, 2 * i, 4, 2, BW, i == 0, i == 3)
            ready_low("n_mix")
            for phase, g0 in (("ugq", G_UGQ), ("cvb", G_CVB), ("gate", G_GATE)):
                if phase == "cvb":
                    pe.wait_ge(glu, 5)
                with pe.Fori(0, 4) as i:
                    for j in range(3):
                        if phase == "ugq" and j == 0:
                            pe.wait_ge(glu, 1 + i)
                        elif phase == "cvb" and j == 0:
                            pe.wait_ge(bank_read[0], USES["cvb"][0] + i)
                        else:
                            pe.wait_ge(bank_read[j], USES[phase][j] + i)
                        to_channels(g0 + j, j, p_pair, i)
            pe.wait_ge(conv_tap, (K_B + 3) * KD)
            for c in range(KD):
                last = nc.tensor.matmul(bank(3, 0, S), mean_w[:, :], conv[:, S * c:S * c + S],
                                        start=c == 0, stop=c == KD - 1)
            last.then_inc(ln_mean, 1)
            pe.wait_ge(an_lo, 4)
            for i in range(4):
                if i < 3:
                    free(i, USES["a_out"][i])
                else:
                    pe.wait_ge(ln_ctr, 1)
                to_channels(G_AO + i, i, q_pair)
            pe.wait_ge(ln_sq, 1)
            free(3, USES["a_out"][3] + 1)
            sq = xn[:, :, :].rearrange("p t n -> p (t n)")
            for c in range(KD):
                last = nc.tensor.matmul(bank(3, 0, S), mean_w[:, :], sq[:, S * c:S * c + S],
                                        start=c == 0, stop=c == KD - 1)
            last.then_inc(ln_var, 1)
            pe.wait_ge(ln_ms, 2)
            attention("att1")
            transpose_rows("o1", "att1")
            ready_low("o1")
            for i in range(4):
                free(i, USES["att_out"][i])
                to_channels(G_ATT + i, i, p_pair)
            pe.wait_ge(ln_lo, 1)
            for i in range(4):
                free(i, USES["b_out"][i])
                to_channels(G_BO + i, i, q_pair)
            pe.wait_ge(mg_lo, 4)
            for b in range(4, 8):
                free(b, USES["w_o"][b])
            for i in range(4):
                to_rows(G_WO + i, 2, p_pair, 2 * i, 4, 2, BW, i == 0, i == 3)
            transpose_norm("n_ffn")
            ready_low("n_ffn")

            def gate_up(n, g, i=0):
                for part in range(2):
                    free(part, USES["ffn1"][part] + n + i)
                    to_channels(g + part, part, p_pair, i)

            gate_up(0, G_FFN1)
            pe.wait_ge(f_lo, 1)
            for b in range(4, 8):
                free(b, USES["ffn1"][b])

            def ffn1_round(i):
                first = isinstance(i, int) and i == 0
                gate_up(1, G_FFN1 + 2, i)
                pe.wait_ge(f_lo, 1 + i)
                to_rows(G_FFN1 + 4, 2, q_pair, 0, 4, 2, BW, first, False, i)

            ffn1_round(0)
            with pe.Fori(1, FG - 1) as i:
                ffn1_round(i)
            pe.wait_ge(f_lo, FG)
            to_rows(G_EV - 1, 2, q_pair, 0, 4, 2, BW, False, True)
            transpose_norm("n_mix2a")
            ready_low("n_mix2a")
            for b in (4, 5):
                free(b, USES["ev_in"][b])
            for i in range(KD):
                to_rows(G_EV + i, 1, p_pair, i, 0, 3, 480, i == 0, i == KD - 1)
            pe.wait_ge(l_x, 1)
            for b in range(3):
                free(b, USES["lat"][b])
            for t in range(T):
                for c in range(5):
                    last = nc.tensor.transpose(bank(c // 2, c % 2 * S + P * t, c % 2 * S + P * t + P),
                                               z[:, t, Z_CQ + P * c:Z_CQ + P * c + P], ident[:, :])
            last.then_inc(l_tr, 1)
            for b in range(3):
                free(b, USES["lat"][b] + 1)
            free(3, USES["uq"][3])
            for i in range(3):
                to_rows(G_UQ + i, 1, p_pair, i, 0, 2, 384, i == 0, i == 2)
            for b in range(4, 8):
                free(b, USES["ukv"][b])
            to_rows(G_UKV, 2, p_pair, 3, 4, 2, BW, True, True)
            for i in range(11):
                b = i % 4
                pe.wait_ge(rope_a, 2) if i == 0 else None
                pe.wait_ge(rope_b, 4) if i == 3 else None
                free(b, USES["ev_tr"][b] + i // 4)
                for c in range(1 if i == 2 else 2):
                    for t in range(T):
                        at = slice(S * c + P * t, S * c + P * t + P)
                        if i < 2:
                            src = qrot[:, t, P * (2 * i + c):P * (2 * i + c) + P]
                        elif i == 2:
                            src = z[:, t, Z_K:Z_V]
                        else:
                            h = 2 * ((i - 3) % 4) + c
                            src = (qb if i < 7 else kf)[:, t, B_QK * h:B_QK * h + B_QK]
                        dst = ps[:, b, at] if i < 3 else ps[0:B_QK, b, at]
                        last = nc.tensor.transpose(dst, src, ident[:, :])
                last.then_inc(ev_tr, 1)
            for b in range(4):
                free(b, USES["att2"][b])
            attention("att2")
            transpose_rows("o2", "att2")
            ready_low("o2")
            for b in range(4, 8):
                free(b, USES["ev_out"][b])
            for i in range(4):
                to_rows(G_EVO + i, 2, p_pair, 2 * i, 4, 2, BW, i == 0, i == 3)
            transpose_norm("n_ffn2a")
            ready_low("n_ffn2a")

            def ffn2(phase, k, g0):
                for b in range(4, 8):
                    free(b, USES[phase][b])
                to_channels(g0, 0, p_pair)

                def three(i):
                    for j in range(3):
                        to_channels(g0 + 1 + 2 * j, (1 + j) % 3, p_pair, 2 * i)
                        pe.wait_ge(f2_lo, FP * k + j + 1 + 3 * i)
                        to_rows(g0 + 2 + 2 * j, 2, q_pair, 2 * j, 4, 2, BW,
                                isinstance(i, int) and i == 0 and j == 0, False, 2 * i)

                three(0)
                with pe.Fori(1, (FP - 1) // 3) as i:
                    three(i)
                pe.wait_ge(f2_lo, FP * (k + 1))
                to_rows(g0 + 2 * FP - 1, 2, q_pair, 0, 4, 2, BW, False, True)

            ffn2("ffn2a", 0, G_F2A)
            transpose_norm("n_mix2b")
            ready_low("n_mix2b")
            for i in range(8):
                free(i % 4, USES["qk"][i % 4] + i // 4)
                to_channels(G_QK + i, i % 4, p_pair)
            for b in range(4, 8):
                free(b, USES["v"][b])
            for i in range(4):
                to_rows(G_V + i, 2, p_pair, 2 * i, 4, 2, BW, i == 0, i == 3)
            for b in range(4):
                free(b, USES["att3"][b])
            for b in range(4, 8):
                free(b, USES["att3"][b])
            attention("att3")
            transpose_rows("o3", "att3")
            ready_low("o3")
            for i in range(4):
                to_rows(G_ODO + i, 2, p_pair, 2 * i, 4, 2, BW, i == 0, i == 3)
            transpose_norm("n_ffn2b")
            ready_low("n_ffn2b")
            ffn2("ffn2b", 1, G_F2B)


def rope_table():
    import numpy as np
    t = np.arange(S)
    pos = (t // GRID_W, t % GRID_W)
    parts = []
    for width in (HD // 2, B_ROPE // 2):
        inv = np.float32(10000.0) ** (-np.arange(0, width, 2, dtype=np.float32) / np.float32(width))
        ang = [(p.astype(np.float32)[:, None] * inv[None, :]).astype(np.float32) for p in pos]
        cos, sin = [np.cos(a) for a in ang], [np.sin(a) for a in ang]
        parts += [cos[0], cos[0], cos[1], cos[1], -sin[0], sin[0], -sin[1], sin[1]]
    return np.ascontiguousarray(np.concatenate(parts, axis=1).astype(np.float32))


def kernel(**inputs):
    import numpy as np
    import concourse.bacc as bacc
    from concourse.bass_utils import run_bass_kernel_spmd as run

    a = {k: np.asarray(v) for k, v in inputs.items()}
    rows = [a["conv_b_w"][0], a["conv_a_w"][0], a["norm_mix_g"], a["norm_mem_g"], a["b_gate"].reshape(3, D),
            a["conv_b_bias"], a["ln_b_g"], a["ln_b_b"], a["norm_ffn_g"], a["norm_mix_2"], a["norm_ffn_2"],
            np.concatenate([a["ev_b_q_norm_2"][0], a["ev_b_kv_norm_2"][0],
                            np.zeros(D - B_Q_RANK - B_KV_RANK, np.float32)])[None]]
    data = {
        "x": a["x"][0], "mem": a["mem"][0], "vecs": np.concatenate(rows, axis=0),
        "w_in": a["w_in"][0], "w_a_out": a["w_a_out"][0], "w_b_out": a["w_b_out"][0], "w_kv": a["w_kv"][0],
        "w_att_out": a["w_att_out"][0], "w_o": a["w_o"][0], "w_up": a["w_up"][0],
        "conv_ffn_w": a["conv_ffn_w"][0], "w_down": a["w_down"][0],
        "norm_final_g": a["norm_final_g"], "final_norm": a["final_norm_2"],
        "gq": a["ev_a_q_norm_2"][0], "gk": a["ev_a_k_norm_2"][0], "rope": rope_table(),
        "ev_w_in": a["ev_w_in_2"][0], "uq": a["ev_b_w_uq_2"][0], "ukv": a["ev_b_w_ukv_2"][0],
        "ev_w_out": a["ev_w_out_2"][0], "od_w_qkv": a["od_w_qkv_2"][0], "od_w_out": a["od_w_out_2"][0],
        "rpb_rev": a["od_rpb_2"][0][..., ::-1],
        "up_a": a["ffn_w_up_2"][0], "up_b": a["ffn_w_up_2"][1],
        "down_a": a["ffn_w_down_2"][0], "down_b": a["ffn_w_down_2"][1],
    }
    data = {k: np.ascontiguousarray(v) for k, v in data.items()}
    nc = bacc.Bacc("TRN2", target_bir_lowering=False, num_devices=1)
    aps = {k: nc.dram_tensor("in_" + k, list(v.shape), F32, kind="ExternalInput").ap() for k, v in data.items()}
    out = nc.dram_tensor("out", [S, D], F32, kind="ExternalOutput").ap()
    two_blocks(nc, aps, out)
    r = run(nc, [{"in_" + k: v for k, v in data.items()}], core_ids=[0])
    return r.results[0]["out"].reshape(1, S, D)
```

```python
from contextlib import ExitStack

import concourse.bass as bass
from concourse import mybir

F32 = mybir.dt.float32
F32R = mybir.dt.float32r
ACT = mybir.ActivationFunctionType
ALU = mybir.AluOpType
AX = mybir.AxisListType

P = 128
S = 256
T = S // P
D = 1024
KD = D // P
EPS = 1e-6
R = 3
SLOT = 2048
BW = 512

K_A, K_B, K_F = 3, 31, 3
D_FF = 2816
FG = D_FF // 256
FT = 2 * D_FF // P
D_FF2 = 4096
FP = D_FF2 // 256
MEM_HEADS, MEM_HD = 4, 256
A_HEADS, A_KV, B_HEADS, HD = 8, 2, 8, 64
B_NOPE, B_ROPE = 64, 32
B_QK = B_NOPE + B_ROPE
B_Q_RANK, B_KV_RANK = 384, 256
EV_IN = 1440
Z_K, Z_V, Z_CQ, Z_CKV, Z_KR = 512, 640, 768, 1152, 1408
C_HEADS = 16
GRID_W = 64
RPB_H, RPB_W = 15, 31
NEG = -1.0e30

V_CONVB, V_CONVA, V_MIX, V_MEM, V_GATE, V_CBIAS, V_LNG, V_LNB, V_FFN = 0, 31, 34, 35, 36, 39, 40, 41, 42
V_MIX2, V_FFN2, V_LAT, NV = 43, 45, 47, 48

G_UGQ, G_KV, G_CVB, G_GATE, G_AO, G_ATT, G_BO, G_WO = 0, 12, 20, 32, 44, 48, 52, 56
G_FFN1 = 60
G_EV = G_FFN1 + 3 * FG
G_UQ, G_UKV, G_EVO = G_EV + 8, G_EV + 11, G_EV + 12
G_F2A = G_EVO + 4
G_QK = G_F2A + 2 * FP
G_V, G_ODO = G_QK + 8, G_QK + 12
G_F2B = G_ODO + 4
G_END = G_F2B + 2 * FP

LOW4 = {0: 1, 1: 1, 2: 1, 3: 1}
HIGH4 = {4: 1, 5: 1, 6: 1, 7: 1}
HEADS16 = {2: 8, 3: 8, **HIGH4}
PHASES = [
    ("setup", {0: 1}), ("n_mix", LOW4), ("ugq", {1: 4, 2: 4}), ("setup2", {3: 1}), ("n_mem", LOW4),
    ("kv", {**LOW4, **HIGH4}), ("cvb", {0: 4, 1: 4, 2: 4}), ("gate", {0: 4, 1: 4, 2: 4}),
    ("a_out", LOW4), ("att1", {2: 2, 3: 2, **HIGH4}), ("o1", LOW4), ("att_out", LOW4), ("b_out", LOW4),
    ("w_o", HIGH4), ("n_ffn", LOW4), ("ffn1", {0: FG, 1: FG, **HIGH4}), ("n_mix2a", LOW4),
    ("ev_in", {0: 1, 1: 1, 2: 1, 3: 1, 4: 1, 5: 1}), ("lat", {0: 1, 1: 1, 2: 1}), ("uq", LOW4), ("ukv", HIGH4),
    ("ev_tr", {0: 3, 1: 3, 2: 3, 3: 2}), ("att2", HEADS16), ("o2", LOW4), ("ev_out", HIGH4),
    ("n_ffn2a", LOW4), ("ffn2a", HIGH4), ("n_mix2b", LOW4),
    ("qk", {0: 2, 1: 2, 2: 2, 3: 2}), ("v", HIGH4), ("att3", HEADS16), ("o3", LOW4), ("od_out", HIGH4),
    ("n_ffn2b", LOW4), ("ffn2b", HIGH4),
]


def earlier_bank_uses():
    count, uses = [0] * 8, {}
    for name, used in PHASES:
        uses[name] = list(count)
        for bank, n in used.items():
            count[bank] += n
    return uses


USES = earlier_bank_uses()
NORMS = ["n_mix", "n_mem", "n_ffn", "fin1", "n_mix2a", "n_ffn2a", "n_mix2b", "n_ffn2b", "fin2"]
TNORMS = ["n_mix", "n_mem", "n_ffn", "n_mix2a", "n_ffn2a", "n_mix2b", "n_ffn2b"]
TGAIN = [V_MIX, V_MEM, V_FFN, V_MIX2, V_FFN2, V_MIX2 + 1, V_FFN2 + 1]


def two_blocks(nc, d, out):
    with ExitStack() as ctx:
        def sb(name, shape, dt=F32):
            return ctx.enter_context(nc.sbuf_tensor(name, shape, dt))

        def sem(name):
            return ctx.enter_context(nc.semaphore(name))

        raw = sb("raw", [P, R, SLOT])
        whi = sb("whi", [P, R, SLOT], F32R)
        wlo = sb("wlo", [P, R, SLOT], F32R)
        p_hi = sb("p_hi", [P, KD * S], F32R)
        p_lo = sb("p_lo", [P, KD * S], F32R)
        q_hi = sb("q_hi", [P, KD * S], F32R)
        q_lo = sb("q_lo", [P, KD * S], F32R)
        x = sb("x", [P, T, D])
        xn = sb("xn", [P, T, D])
        kreg = sb("kreg", [P, 2048])
        vreg = sb("vreg", [P, 2048])
        qreg = sb("qreg", [P, 2048])
        gates = sb("gates", [P, 3 * KD * S])
        merged = sb("merged", [P, KD * S])
        UP = K_B - 1 + S
        misc = sb("misc", [P, KD * UP + KD * S])
        work = sb("work", [P, 2560])
        vec = sb("vec", [P, KD * NV])
        cwf = sb("cwf", [P, K_F * FT])
        ident = sb("ident", [P, P])
        mean_w = sb("mean_w", [P, P])
        stat = sb("stat", [P, 260])
        ps = ctx.enter_context(nc.psum_tensor("ps", [P, 8, BW], F32))

        ms, rr = stat[:, 18:36], stat[:, 36:54]
        ss = stat[:, 192:228].rearrange("p (n m) -> p n m", m=2)
        ln_v, ln_rs = stat[:, 228:230], stat[:, 230:232]
        sm = stat[:, 232:250]
        mhalf = stat[:, 54:74]
        att_max, att_nmax = stat[:, 74:78], stat[:, 78:82]
        att_sum, att_rs = stat[:, 82:114], stat[:, 114:146]
        hss, hr = stat[:, 146:166], stat[:, 166:186]
        lat = stat[:, 186:190]

        def gain(row, c):
            return vec[:, c * NV + row:c * NV + row + 1]

        def bank(b, a=0, z=BW):
            return ps[:, b, a:z]

        mem_rows = merged[:, :].rearrange("p (t n) -> p t n", t=T)
        vec_rows = gates[0:NV, 0:D]
        cwf_rows = gates[0:FT, D:D + K_F * P]
        uglu = misc[:, 0:KD * UP].rearrange("p (c n) -> p c n", c=KD)
        conv = misc[:, KD * UP:KD * UP + KD * S]
        v_tok = vreg[:, :].rearrange("p (t n) -> p t n", t=T)

        ln_sqs = misc[:, 0:KD * S]
        ln_diag = work[:, 0:S]
        z = gates[:, 0:2 * EV_IN].rearrange("p (t n) -> p t n", t=T)
        qb = gates[:, 2880:4416].rearrange("p (t n) -> p t n", t=T)
        kf = gates[:, 4416:5952].rearrange("p (t n) -> p t n", t=T)
        kvb = qreg[:, :].rearrange("p (t n) -> p t n", t=T)
        qT_a = merged[:, 0:1024]
        kT_a = merged[:, 1024:1280]
        gq, gk = merged[:, 1280:1344], merged[:, 1344:1408]
        rope = merged[:, 1408:1792].rearrange("p (t n) -> p t n", t=T)
        gfin = merged[:, 0:1024]
        qrot = misc[:, 1408:2432].rearrange("p (t n) -> p t n", t=T)
        rpb = misc[:, 0:16 * 219].rearrange("p (h n) -> p h n", h=C_HEADS)
        bias = gates[:, 0:16 * 384].rearrange("p (h j k) -> p h j k", h=C_HEADS, j=6)
        prob = work[:, 0:1024].rearrange("p (b t n) -> p b t n", b=2, t=T)
        probT = work[:, 1024:2048].rearrange("p (b m n) -> p b m n", b=2, m=T)
        bsc = misc[:, 0:1024].rearrange("p (b t n) -> p b t n", b=2, t=T)

        raw_in = [sem(f"raw_in{r}") for r in range(R)]
        hi_ready = sem("hi_ready")
        lo_ready = sem("lo_ready")
        slot_used = sem("slot_used")
        bank_read = [sem(f"bank_read{b}") for b in range(8)]
        mem_in, x_in, vec_in, cwf_in = sem("mem_in"), [sem(f"x_in{t}") for t in range(T)], sem("vec_in"), sem("cwf_in")
        gain_in, rope_in, rpb_in = sem("gain_in"), sem("rope_in"), sem("rpb_in")
        const_ready = sem("const_ready")
        vec_tr = sem("vec_tr")
        norm_sq, norm_ms, norm_r = sem("norm_sq"), sem("norm_ms"), sem("norm_r")
        norm_xn, norm_tr, norm_hi = sem("norm_xn"), sem("norm_tr"), sem("norm_hi")
        glu, conv_tap = sem("glu"), sem("conv_tap")
        ga_ready, ca_step, an_hi, an_lo = sem("ga_ready"), sem("ca_step"), sem("an_hi"), sem("an_lo")
        ln_mean, ln_ctr, ln_sq, ln_var = sem("ln_mean"), sem("ln_ctr"), sem("ln_sq"), sem("ln_var")
        ln_ms, ln_r, ln_z, ln_y, ln_hi, ln_lo = (sem("ln_ms"), sem("ln_r"), sem("ln_z"), sem("ln_y"),
                                                 sem("ln_hi"), sem("ln_lo"))
        mg, mg_hi, mg_lo = sem("mg"), sem("mg_hi"), sem("mg_lo")
        at_s, at_max, at_nm, at_e = sem("at_s"), sem("at_max"), sem("at_nm"), sem("at_e")
        at_t, at_o, at_rs = sem("at_t"), sem("at_o"), sem("at_rs")
        o_tr, o_hi = sem("o_tr"), sem("o_hi")
        f_y, f_c, f_s, f_u, f_hi, f_lo = sem("f_y"), sem("f_c"), sem("f_s"), sem("f_u"), sem("f_hi"), sem("f_lo")
        f2_r, f2_sq, f2_hi, f2_lo = sem("f2_r"), sem("f2_sq"), sem("f2_hi"), sem("f2_lo")
        fin_x, rows_done = sem("fin_x"), sem("rows_done")
        norm_sum, ln_dg, ln_bc = sem("norm_sum"), sem("ln_dg"), sem("ln_bc")
        h_sq, h_ss, h_ms, h_r, h_n = sem("h_sq"), sem("h_ss"), sem("h_ms"), sem("h_r"), sem("h_n")
        l_sq, l_ms, l_r, l_x, l_tr, l_hi = sem("l_sq"), sem("l_ms"), sem("l_r"), sem("l_x"), sem("l_tr"), sem("l_hi")
        rope_a, rope_b, ev_tr, bias_step = sem("rope_a"), sem("rope_b"), sem("ev_tr"), sem("bias_step")
        out_done = sem("out_done")

        block = ctx.enter_context(nc.Block())

        def q_tile(reg, c, lo, hi, t):
            return reg[lo:hi, c * S + t * P:c * S + t * P + P]

        def heads_mem():
            for h in range(MEM_HEADS):
                yield dict(
                    q=lambda t, h=h: [q_tile(qreg, 2 * h + k, 0, P, t) for k in range(2)],
                    k=[kreg[:, (2 * h + k) * S:(2 * h + k + 1) * S] for k in range(2)],
                    v=lambda m, h=h: v_tok[:, m, h * MEM_HD:(h + 1) * MEM_HD],
                    at=h * MEM_HD, wide=MEM_HD)

        def heads_even():
            for h in range(A_HEADS):
                kv = h // (A_HEADS // A_KV)
                yield dict(
                    q=lambda t, h=h, kv=kv: [q_tile(qT_a, h % 4, HD * kv, HD * kv + HD, t)],
                    k=[kT_a[HD * kv:HD * kv + HD, :]],
                    v=lambda m, kv=kv: z[:, m, Z_V + HD * kv:Z_V + HD * kv + HD],
                    at=h * HD, wide=HD)
            for h in range(B_HEADS):
                yield dict(
                    q=lambda t, h=h: [q_tile(kreg, h, 0, B_QK, t)],
                    k=[vreg[0:B_QK, h * S:(h + 1) * S]],
                    v=lambda m, h=h: kvb[:, m, h * 128 + HD:(h + 1) * 128],
                    at=(A_HEADS + h) * HD, wide=HD)

        def heads_odd():
            for h in range(C_HEADS):
                b = HD * (h % 2)
                yield dict(
                    q=lambda t, h=h, b=b: [q_tile(qreg, h // 2, b, b + HD, t)],
                    k=[kreg[b:b + HD, h // 2 * S:(h // 2 + 1) * S]],
                    v=lambda m, h=h: v_tok[:, m, h * HD:(h + 1) * HD],
                    at=h * HD, wide=HD)

        ATT = {
            "att1": (list(heads_mem()), 0, lambda i: MEM_HD ** -0.5, False, 0),
            "att2": (list(heads_even()), 4, lambda i: (HD if i < A_HEADS else B_QK) ** -0.5, False, 1),
            "att3": (list(heads_odd()), 20, lambda i: HD ** -0.5, True, 2),
        }

        @block.sync
        def _(sp):
            x_rows = d["x"].rearrange("(t p) n -> p t n", p=P)
            for t in range(T):
                sp.dma_start(x[:, t, :], x_rows[:, t, :]).then_inc(x_in[t], 16)

            def load(g, src, kk, i=0):
                n = src.shape[-1]
                if g >= R or not isinstance(i, int):
                    sp.wait_ge(lo_ready, g - R + 1 + R * i)
                sp.dma_start(raw[:, g % R, 0:kk * n].rearrange("p (k n) -> p k n", k=kk),
                             src).then_inc(raw_in[g % R], 16)

            def cols(w, c0):
                return d[w].rearrange("(k p) n -> p k n", p=P)[:, :, bass.ds(c0, 256)]

            def rows(w, k0, kk):
                return d[w].rearrange("(k p) n -> p k n", p=P)[:, bass.ds(k0, kk), :]

            for j, c0 in enumerate((3 * D, 4 * D, 5 * D)):
                load(G_UGQ + j, cols("w_in", c0), KD)
            with sp.Fori(1, 4) as i:
                for j, c0 in enumerate((3 * D, 4 * D, 5 * D)):
                    load(G_UGQ + j, cols("w_in", c0 + 256 * i), KD, i)
            for i in range(4):
                load(G_KV + i, cols("w_kv", 256 * i), KD)
            for i in range(4):
                load(G_KV + 4 + i, d["w_kv"].rearrange("(k p) n -> p k n", p=P)[:, 2 * i:2 * i + 2, D:2 * D], 2)
            with sp.Fori(1, 5) as i:
                for j, c0 in enumerate((D, 2 * D, 0)):
                    load(G_CVB + j, cols("w_in", c0 - 256 + 256 * i), KD, i - 1)
            with sp.Fori(0, 4) as i:
                for j in range(3):
                    load(G_GATE + j, cols("w_in", (6 + j) * D + 256 * i), KD, i)
            for g0, w in ((G_AO, "w_a_out"), (G_ATT, "w_att_out"), (G_BO, "w_b_out")):
                for i in range(4):
                    load(g0 + i, cols(w, 256 * i), KD)
            for i in range(4):
                load(G_WO + i, rows("w_o", 2 * i, 2), 2)
            load(G_FFN1, cols("w_up", 0), KD)
            load(G_FFN1 + 1, cols("w_up", D_FF), KD)
            with sp.Fori(0, FG - 1) as i:
                load(G_FFN1 + 2, cols("w_up", 256 * i + 256), KD, i)
                load(G_FFN1 + 3, cols("w_up", D_FF + 256 * i + 256), KD, i)
                load(G_FFN1 + 4, rows("w_down", 2 * i, 2), 2, i)
            load(G_EV - 1, rows("w_down", 2 * FG - 2, 2), 2)
            for i in range(8):
                load(G_EV + i, rows("ev_w_in", i, 1), 1)
            for i in range(3):
                load(G_UQ + i, rows("uq", i, 1), 1)
            load(G_UKV, rows("ukv", 0, 2), 2)
            for i in range(4):
                load(G_EVO + i, rows("ev_w_out", 2 * i, 2), 2)

            def ffn2(g0, up, down):
                load(g0, cols(up, 0), KD)
                with sp.Fori(0, (FP - 1) // 3) as i:
                    for j in range(3):
                        load(g0 + 1 + 2 * j, cols(up, 768 * i + 256 * (j + 1)), KD, 2 * i)
                        load(g0 + 2 + 2 * j, rows(down, 6 * i + 2 * j, 2), 2, 2 * i)
                load(g0 + 2 * FP - 1, rows(down, 2 * FP - 2, 2), 2)

            ffn2(G_F2A, "up_a", "down_a")
            with sp.Fori(0, 2) as i:
                for j in range(3):
                    load(G_QK + j, cols("od_w_qkv", 768 * i + 256 * j), KD, i)
            for i in range(6, 8):
                load(G_QK + i, cols("od_w_qkv", 256 * i), KD)
            for i in range(4):
                load(G_V + i, d["od_w_qkv"].rearrange("(k p) n -> p k n", p=P)[:, 2 * i:2 * i + 2, 2 * D:3 * D], 2)
            for i in range(4):
                load(G_ODO + i, rows("od_w_out", 2 * i, 2), 2)
            ffn2(G_F2B, "up_b", "down_b")
            out_v = out.rearrange("(t p) n -> p t n", p=P)
            for t in range(T):
                sp.wait_ge(fin_x, T + t + 1)
                sp.dma_start(out_v[:, t, :], x[:, t, :]).then_inc(out_done, 16)
            sp.wait_ge(out_done, 16 * T)

        @block.gpsimd
        def _(pool):
            pool.dma_start(cwf_rows.rearrange("c (k p) -> c k p", k=K_F),
                           d["conv_ffn_w"].rearrange("k (c p) -> c k p", p=P)).then_inc(cwf_in, 16)
            nc.gpsimd.memset(ident[:, :], 0.0).then_inc(const_ready, 1)
            nc.gpsimd.memset(mean_w[:, :], 1.0 / D)
            nc.gpsimd.memset(mhalf, -0.5)
            pool.wait_ge(const_ready, 1)
            nc.gpsimd.affine_select(out=ident[:, :], in_=ident[:, :], compare_op=ALU.not_equal, fill=1.0, base=0,
                                    pattern=[[-1, P]], channel_multiplier=1).then_inc(const_ready, 1)
            nc.gpsimd.memset(uglu[:, :, 0:K_B - 1], 0.0).then_inc(glu, 1)
            nc.gpsimd.memset(work[:, 1344:1860].rearrange("p (b n) -> p b n", b=2)[:, :, 0:K_A - 1],
                             0.0).then_inc(ca_step, 1)

            def inverse_root(n):
                for c in range(T * n, T * n + T):
                    pool.wait_ge(norm_ms, c + 1)
                    nc.gpsimd.tensor_tensor(out=rr[:, c:c + 1], in0=ms[:, c:c + 1], in1=mhalf[:, 0:1],
                                            op=ALU.pow).then_inc(norm_r, 1)

            pool.wait_ge(ca_step, 1)
            inverse_root(0)
            inverse_root(1)
            pool.wait_ge(ln_ms, 1)
            nc.gpsimd.tensor_tensor(out=ln_rs, in0=ln_v, in1=mhalf[:, 0:2], op=ALU.pow).then_inc(ln_r, 1)
            inverse_root(2)
            pool.wait_ge(mg_lo, 4)
            pool.dma_start(gfin, d["norm_final_g"].partition_broadcast(P)).then_inc(gain_in, 16)
            pool.dma_start(gq, d["gq"].partition_broadcast(P)).then_inc(rope_in, 16)
            pool.dma_start(gk, d["gk"].partition_broadcast(P)).then_inc(rope_in, 16)
            pool.dma_start(rope, d["rope"].rearrange("(t p) n -> p t n", p=P)).then_inc(rope_in, 16)
            inverse_root(3)
            inverse_root(4)
            pool.wait_ge(l_ms, 1)
            nc.gpsimd.tensor_tensor(out=lat, in0=lat, in1=mhalf[:, 0:4], op=ALU.pow).then_inc(l_r, 1)
            pool.wait_ge(h_ms, 1)
            nc.gpsimd.tensor_tensor(out=hr, in0=hss, in1=mhalf, op=ALU.pow).then_inc(h_r, 1)
            inverse_root(5)
            pool.wait_ge(o_tr, 2)
            pool.dma_start(gfin, d["final_norm"].partition_broadcast(P)).then_inc(gain_in, 16)
            for half in range(2):
                src = bass.AP(d["rpb_rev"].tensor, (5 - half) * RPB_W + 15 - 63,
                              [[1, GRID_W], [RPB_H * RPB_W, C_HEADS], [1, 219]])
                pool.dma_start(rpb[64 * half:64 * half + 64], src).then_inc(rpb_in, 16)
            pool.wait_ge(rpb_in, 32)
            steps = 0
            for h in range(C_HEADS):
                rev = bass.AP(misc[:, :].tensor, h * 219 + 63, [[KD * UP + KD * S, P], [RPB_W, 6], [-1, 64]])
                nc.gpsimd.tensor_copy(bias[:, h], rev).then_inc(bias_step, 1)
                steps += 1
                for c0, base, sign in ((0, 8, 1), (16, 7 - 16, -1)):
                    for half in range(2):
                        part = bias[64 * half:64 * half + 64, h, :, c0:c0 + 48]
                        pool.wait_ge(bias_step, steps)
                        nc.gpsimd.affine_select(out=part, in_=part, compare_op=ALU.is_ge, fill=NEG, base=base,
                                                pattern=[[0, 6], [sign, 48]], channel_multiplier=-sign)\
                            .then_inc(bias_step, 1)
                        steps += 1
                pool.wait_ge(bias_step, steps)
            inverse_root(6)
            inverse_root(7)
            inverse_root(8)

        @block.scalar
        def _(act):
            def hi(g, i=0):
                if isinstance(i, int):
                    g, i = g + R * i, 0
                    if g >= G_END:
                        return
                act.wait_ge(raw_in[g % R], 16 * (g // R + 1) + 16 * i)
                if g >= R:
                    act.wait_ge(slot_used, g - R + 1 + R * i)
                nc.scalar.activation(whi[:, g % R, :], raw[:, g % R, :], ACT.Copy).then_inc(hi_ready, 1)

            def squares(name, src, ready=None):
                n = NORMS.index(name)
                for b in range(2 * T):
                    if ready:
                        ready(b)
                    t, m = b // 2, b % 2
                    half = slice(BW * m, BW * m + BW)
                    last = nc.scalar.activation(xn[:, t, half], src[:, t, half], ACT.Square,
                                                accum_out=ss[:, T * n + t, m:m + 1])
                    if m:
                        last.then_inc(norm_sq, 1)

            def norm_upper(name, dst):
                m = TNORMS.index(name)
                for c in range(KD):
                    act.wait_ge(norm_tr, 4 * m + c // 2 + 1)
                    nc.scalar.activation(dst[:, c * S:(c + 1) * S], bank(c // 2, c % 2 * S, c % 2 * S + S), ACT.Copy,
                                         scale=gain(TGAIN[m], c)).then_inc(norm_hi, 1)

            def split_rows(k, phase):
                act.wait_ge(o_tr, k + 1)
                for b in range(4):
                    nc.scalar.activation(p_hi[:, BW * b:BW * (b + 1)], bank(b), ACT.Copy).then_inc(o_hi, 1)

            def exps(name):
                heads, i0, scale, biased, _ = ATT[name]
                for i, _h in enumerate(heads):
                    n = i0 + i
                    act.wait_ge(at_nm, n + 1)
                    if i >= 2:
                        act.wait_ge(at_t, n - 1)
                    for t in range(T):
                        src = bsc[:, i % 2, t, :] if biased else bank(i % 2, t * S, t * S + S)
                        last = nc.scalar.activation(prob[:, i % 2, t, :], src, ACT.Exp,
                                                    bias=att_nmax[:, 2 * (i % 2) + t:2 * (i % 2) + t + 1],
                                                    scale=1.0 if biased else scale(i),
                                                    accum_out=att_sum[:, 16 * t + i:16 * t + i + 1])
                    last.then_inc(at_e, 1)

            act.dma_start(vec_rows, d["vecs"]).then_inc(vec_in, 16)
            act.dma_start(mem_rows, d["mem"].rearrange("(t p) n -> p t n", p=P)).then_inc(mem_in, 16)
            squares("n_mix", x, lambda b: act.wait_ge(x_in[b // 2], 16))
            act.wait_ge(vec_tr, 1)
            nc.scalar.activation(vec[:, :], bank(0, 0, KD * NV), ACT.Copy).then_inc(bank_read[0], 1)
            hi(0)
            act.wait_ge(bank_read[0], 1)
            norm_upper("n_mix", p_hi)
            hi(1)
            hi(2)
            squares("n_mem", mem_rows, lambda b: act.wait_ge(mem_in, 16))
            U = USES["ugq"]
            with act.Fori(0, 4) as i:
                hi(G_UGQ + 3, i)
                act.wait_ge(slot_used, G_UGQ + 2 + 3 * i)
                act.wait_ge(glu, i + 1)
                nc.scalar.activation(work[:, 832:1344], bank(1), ACT.Sigmoid).then_inc(bank_read[1], 1)
                hi(G_UGQ + 4, i)
                act.wait_ge(slot_used, G_UGQ + 3 + 3 * i)
                nc.scalar.activation(qreg[:, bass.ds(BW * i, BW)], bank(2), ACT.Copy).then_inc(bank_read[2], 1)
                hi(G_UGQ + 5, i)
            act.wait_ge(vec_tr, 2)
            nc.scalar.activation(cwf[:, :], bank(3, 0, K_F * FT), ACT.Copy).then_inc(bank_read[3], 1)
            norm_upper("n_mem", q_hi)
            for i in range(4):
                act.wait_ge(slot_used, G_KV + i + 1)
                nc.scalar.activation(kreg[:, BW * i:BW * (i + 1)], bank(i), ACT.Copy).then_inc(bank_read[i], 1)
                hi(G_KV + i + 3)
            for i in range(4):
                if i == 3:
                    act.wait_ge(slot_used, G_KV + 8)
                    for b in range(4):
                        nc.scalar.activation(v_tok[:, b // 2, BW * (b % 2):BW * (b % 2) + BW], bank(4 + b),
                                             ACT.Copy).then_inc(bank_read[4 + b], 1)
                hi(G_KV + 7 + i)
            with act.Fori(0, 4) as i:
                act.wait_ge(slot_used, G_CVB + 1 + 3 * i)
                act.wait_ge(bank_read[1], USES["cvb"][1] + i)
                nc.scalar.activation(work[:, 832:1344], bank(0), ACT.Copy).then_inc(bank_read[0], 1)
                hi(G_CVB + 3, i)
                hi(G_CVB + 4, i)
                act.wait_ge(bank_read[2], USES["cvb"][2] + 1 + i)
                nc.scalar.activation(q_hi[:, bass.ds(BW * i, BW)], work[:, 1860:2372], ACT.Copy).then_inc(an_hi, 1)
                hi(G_CVB + 5, i)
            with act.Fori(0, 4) as i:
                for j in range(3):
                    act.wait_ge(slot_used, G_GATE + j + 1 + 3 * i)
                    for b in range(2):
                        last = nc.scalar.activation(
                            gates[:, bass.ds(j * KD * S + BW * i + S * b, S)], bank(j, S * b, S * b + S), ACT.Sigmoid,
                            bias=vec[:, bass.ds(2 * NV * i + b * NV + V_GATE + j, 1)])
                    last.then_inc(bank_read[j], 1)
                    hi(G_GATE + j + 3, i)
            for i in range(4):
                hi(G_AO + i + 3)
            act.wait_ge(ln_ctr, 1)
            nc.scalar.activation(ln_sqs, conv, ACT.Square).then_inc(ln_sq, 1)
            exps("att1")
            split_rows(0, "o1")
            hi(G_ATT + 3)
            hi(G_ATT + 4)
            act.wait_ge(ln_z, 1)
            for c in range(KD):
                nc.scalar.activation(conv[:, c * S:(c + 1) * S], conv[:, c * S:(c + 1) * S], ACT.Silu,
                                     scale=gain(V_LNG, c), bias=gain(V_LNB, c)).then_inc(ln_y, 1)
                if c % 4 == 3:
                    act.wait_ge(ln_y, c + 1)
                    nc.scalar.activation(q_hi[:, 1024 * (c // 4):1024 * (c // 4) + 1024],
                                         conv[:, 1024 * (c // 4):1024 * (c // 4) + 1024], ACT.Copy).then_inc(ln_hi, 1)
                    hi(G_ATT + 5 + c // 4)
            for i in range(4):
                act.wait_ge(mg, 4 + i + 1)
                nc.scalar.activation(p_hi[:, BW * i:BW * (i + 1)], merged[:, BW * i:BW * (i + 1)],
                                     ACT.Copy).then_inc(mg_hi, 1)
                hi(G_BO + i + 3)
            for i in range(3):
                hi(G_WO + i + 3)

            def after_product(name, phase, dst=None):
                squares(name, x, lambda b: act.wait_ge(bank_read[4 + b], USES[phase][4 + b] + 1))
                if dst is not None:
                    norm_upper(name, dst)

            after_product("n_ffn", "w_o", p_hi)
            hi(G_WO + 6)

            def last_tap(i, part, b, n):
                act.wait_ge(slot_used, n)
                if part and not isinstance(i, int):
                    act.wait_ge(f_u, i)
                for h in range(2):
                    dst = work[:, BW * part + S * h:BW * part + S * h + S]
                    c = 2 * FT + part * (FT // 2) + 2 * i + h
                    last = nc.scalar.activation(dst, bank(b, S * h, S * h + S), ACT.Copy, scale=cwf[:, bass.ds(c, 1)])
                last.then_inc(f_y, 1)

            def silu_gate(n):
                act.wait_ge(bank_read[0], USES["ffn1"][0] + n)
                nc.scalar.activation(work[:, 1024:1536], work[:, 0:512], ACT.Silu).then_inc(f_s, 1)

            def u_upper(n):
                act.wait_ge(f_u, n)
                nc.scalar.activation(q_hi[:, 0:BW], work[:, 1536:2048], ACT.Copy).then_inc(f_hi, 1)

            last_tap(0, 0, 0, G_FFN1 + 1)
            hi(G_FFN1 + 3)
            last_tap(0, 1, 1, G_FFN1 + 2)
            silu_gate(1)
            hi(G_FFN1 + 4)
            u_upper(1)
            with act.Fori(0, FG - 1) as i:
                last_tap(i + 1, 0, 0, G_FFN1 + 3 + 3 * i)
                hi(G_FFN1 + 5, i)
                last_tap(i + 1, 1, 1, G_FFN1 + 4 + 3 * i)
                silu_gate(i + 2)
                hi(G_FFN1 + 6, i)
                act.wait_ge(slot_used, G_FFN1 + 5 + 3 * i)
                u_upper(i + 2)
                hi(G_FFN1 + 7, i)
            after_product("fin1", "ffn1")
            squares("n_mix2a", x, lambda b: act.wait_ge(fin_x, b // 2 + 1))
            norm_upper("n_mix2a", p_hi)
            hi(G_EV + 2)
            for i in range(7):
                hi(G_EV + i + 3)
            act.wait_ge(slot_used, G_EV + 8)
            for b in (5, 2, 4, 1, 3, 0):
                nc.scalar.activation(z[:, b // 3, 480 * (b % 3):480 * (b % 3) + 480], bank(b, 0, 480),
                                     ACT.Copy).then_inc(bank_read[b], 1)
            for b in range(6):
                act.wait_ge(bank_read[b], USES["ev_in"][b] + 1)
            for t in range(T):
                nc.scalar.activation(misc[:, 1920 * t:1920 * t + 384], z[:, t, Z_CQ:Z_CKV], ACT.Square,
                                     accum_out=lat[:, t:t + 1])
                last = nc.scalar.activation(misc[:, 1920 * t + 384:1920 * t + 640], z[:, t, Z_CKV:Z_KR], ACT.Square,
                                            accum_out=lat[:, 2 + t:3 + t])
            last.then_inc(l_sq, 1)
            for t in range(T):
                nc.scalar.activation(misc[:, 640 + 640 * t:1280 + 640 * t], z[:, t, 0:Z_V],
                                     ACT.Square).then_inc(h_sq, 1)
            hi(G_EV + 10)
            act.wait_ge(l_r, 1)
            for t in range(T):
                nc.scalar.activation(z[:, t, Z_CQ:Z_CKV], z[:, t, Z_CQ:Z_CKV], ACT.Copy, scale=lat[:, t:t + 1])
                last = nc.scalar.activation(z[:, t, Z_CKV:Z_KR], z[:, t, Z_CKV:Z_KR], ACT.Copy,
                                            scale=lat[:, 2 + t:3 + t])
            last.then_inc(l_x, 1)
            act.wait_ge(l_tr, 1)
            for c in range(5):
                nc.scalar.activation(p_hi[:, c * S:(c + 1) * S], bank(c // 2, c % 2 * S, c % 2 * S + S), ACT.Copy,
                                     scale=gain(V_LAT, c)).then_inc(l_hi, 1)
            for i in range(4):
                hi(G_UQ + i + 3)
            act.wait_ge(slot_used, G_UQ + 3)
            for b in range(4):
                nc.scalar.activation(qb[:, b // 2, 384 * (b % 2):384 * (b % 2) + 384], bank(b, 0, 384),
                                     ACT.Copy).then_inc(bank_read[b], 1)
            act.wait_ge(slot_used, G_UKV + 1)
            for b in range(4):
                nc.scalar.activation(kvb[:, b // 2, BW * (b % 2):BW * (b % 2) + BW], bank(4 + b),
                                     ACT.Copy).then_inc(bank_read[4 + b], 1)
            for i in range(11):
                act.wait_ge(ev_tr, i + 1)
                n, b = BW, i % 4
                if i < 2:
                    dst = qT_a[:, BW * i:BW * i + BW]
                elif i == 2:
                    dst, n = kT_a, S
                else:
                    reg = kreg if i < 7 else vreg
                    dst = reg[0:B_QK, BW * ((i - 3) % 4):BW * ((i - 3) % 4) + BW]
                src = ps[0:B_QK, b, :] if i > 2 else bank(b, 0, n)
                nc.scalar.activation(dst, src, ACT.Copy).then_inc(bank_read[b], 1)
            exps("att2")
            split_rows(1, "o2")
            for i in range(3):
                hi(G_EVO + i + 3)
            after_product("n_ffn2a", "ev_out", p_hi)
            hi(G_EVO + 6)

            def group(k, n, slot, up, i=0):
                act.wait_ge(slot_used, up + 1 + 6 * i)
                if FP * k + n > 0:
                    act.wait_ge(f2_sq, FP * k + n + 3 * i)
                nc.scalar.activation(work[:, 0:BW], bank(slot), ACT.Relu).then_inc(f2_r, 1)
                hi(up + 3, 2 * i)
                act.wait_ge(f2_sq, FP * k + n + 1 + 3 * i)
                nc.scalar.activation(q_hi[:, BW * slot:BW * slot + BW], work[:, 1024:1536], ACT.Copy).then_inc(f2_hi, 1)

            def ffn2(k, g0):
                group(k, 0, 0, g0)

                def three(i):
                    for j in range(3):
                        group(k, 1 + j, (1 + j) % 3, g0 + 1 + 2 * j, i)
                        hi(g0 + 5 + 2 * j, 2 * i)

                with act.Fori(0, (FP - 1) // 3 - 1) as i:
                    three(i)
                three((FP - 1) // 3 - 1)

            ffn2(0, G_F2A)
            after_product("n_mix2b", "ffn2a", p_hi)
            hi(G_QK + 2)
            for i in range(8):
                act.wait_ge(slot_used, G_QK + i + 1)
                reg = qreg if i < 4 else kreg
                nc.scalar.activation(reg[:, BW * (i % 4):BW * (i % 4) + BW], bank(i % 4), ACT.Copy,
                                     scale=HD ** -0.5 if i < 4 else 1.0)\
                    .then_inc(bank_read[i % 4], 1)
                hi(G_QK + i + 3)
            for i in range(4):
                if i == 3:
                    act.wait_ge(slot_used, G_V + 4)
                    for b in range(4):
                        nc.scalar.activation(v_tok[:, b // 2, BW * (b % 2):BW * (b % 2) + BW], bank(4 + b),
                                             ACT.Copy).then_inc(bank_read[4 + b], 1)
                hi(G_V + i + 3)
            exps("att3")
            split_rows(2, "o3")
            for i in range(3):
                hi(G_ODO + i + 3)
            after_product("n_ffn2b", "od_out", p_hi)
            hi(G_ODO + 6)
            ffn2(1, G_F2B)
            after_product("fin2", "ffn2b")

        @block.vector
        def _(dve):
            def lo(g, i=0):
                if isinstance(i, int):
                    g, i = g + R * i, 0
                    if g >= G_END:
                        return
                dve.wait_ge(hi_ready, g + 1 + R * i)
                nc.vector.tensor_tensor(wlo[:, g % R, :], raw[:, g % R, :], whi[:, g % R, :].bitcast(F32),
                                        ALU.subtract).then_inc(lo_ready, 1)

            def mean_square(n, t):
                c = T * n + t
                dve.wait_ge(norm_sq, c + 1)
                nc.vector.tensor_tensor(sm[:, c:c + 1], ss[:, c, 0:1], ss[:, c, 1:2], ALU.add).then_inc(norm_sum, 1)
                dve.wait_ge(norm_sum, c + 1)
                nc.vector.tensor_scalar(ms[:, c:c + 1], sm[:, c:c + 1], 1.0 / D, EPS, ALU.mult,
                                        ALU.add).then_inc(norm_ms, 1)

            def normalise(name, src, with_stats=True):
                n, m = NORMS.index(name), TNORMS.index(name)
                for t in range(T):
                    if with_stats:
                        mean_square(n, t)
                for t in range(T):
                    dve.wait_ge(norm_r, T * n + t + 1)
                    nc.vector.tensor_scalar(xn[:, t, :], src[:, t, :], rr[:, T * n + t:T * n + t + 1], None,
                                            ALU.mult).then_inc(norm_xn, 1)

            def norm_lower(name, hi_part, lo_part):
                m = TNORMS.index(name)
                for c in range(KD):
                    dve.wait_ge(norm_hi, KD * m + c // 2 * 2 + 2)
                    last = nc.vector.scalar_tensor_tensor(
                        out=lo_part[:, c * S:(c + 1) * S], in0=bank(c // 2, c % 2 * S, c % 2 * S + S),
                        scalar=gain(TGAIN[m], c), in1=hi_part[:, c * S:(c + 1) * S].bitcast(F32),
                        op0=ALU.mult, op1=ALU.subtract)
                    if c % 2:
                        last.then_inc(bank_read[c // 2], 1)

            def split_rows(k):
                for b in range(4):
                    dve.wait_ge(o_hi, 4 * k + b + 1)
                    nc.vector.tensor_tensor(p_lo[:, BW * b:BW * (b + 1)], bank(b),
                                            p_hi[:, BW * b:BW * (b + 1)].bitcast(F32),
                                            ALU.subtract).then_inc(bank_read[b], 1)

            def residual(name, k, g_end):
                dve.wait_ge(rows_done, k + 1)
                for b in range(4):
                    if b == 2:
                        mean_square(NORMS.index(name), 0)
                        dve.wait_ge(slot_used, g_end)
                    rows = x[:, b // 2, BW * (b % 2):BW * (b % 2) + BW]
                    nc.vector.tensor_tensor(rows, rows, bank(4 + b), ALU.add).then_inc(bank_read[4 + b], 1)
                mean_square(NORMS.index(name), 1)

            def residual_norm(name, k, g_end):
                residual(name, k, g_end)
                normalise(name, x, False)
                norm_lower(name, p_hi, p_lo)

            def attention(name):
                heads, n0, scale, biased, k = ATT[name]
                for i in range(len(heads) + 1):
                    n = n0 + i
                    if i < len(heads):
                        dve.wait_ge(at_s, n + 1)
                        both = ps[:, i % 2, :].rearrange("p (t n) -> p t n", t=T)
                        pair = slice(2 * (i % 2), 2 * (i % 2) + 2)
                        if biased:
                            if i > 1:
                                dve.wait_ge(at_e, n - 1)
                            elif i == 0:
                                dve.wait_ge(bias_step, 5 * C_HEADS)
                            for t in range(T):
                                last = nc.vector.tensor_tensor_reduce(
                                    out=bsc[:, i % 2, t, :], in0=both[:, t, :],
                                    in1=bias[:, i, 2 - 2 * t:6 - 2 * t, :].rearrange("p j k -> p (j k)"),
                                    scale=1.0, scalar=NEG, op0=ALU.add, op1=ALU.max,
                                    accum_out=att_max[:, 2 * (i % 2) + t:2 * (i % 2) + t + 1])
                            last.then_inc(at_max, 1)
                        else:
                            nc.vector.tensor_reduce(out=att_max[:, pair], in_=both, axis=AX.X, op=ALU.max)\
                                .then_inc(at_max, 1)
                        dve.wait_ge(at_max, n + 1)
                        nc.vector.tensor_scalar(att_nmax[:, pair], att_max[:, pair],
                                                -1.0 if biased else -scale(i), None, ALU.mult).then_inc(at_nm, 1)
                    if i:
                        dve.wait_ge(at_t, n)
                        b = 2 + (i - 1) % 2
                        nc.vector.tensor_copy(probT[:, (i - 1) % 2].rearrange("p m n -> p (m n)"), bank(b))\
                            .then_inc(bank_read[b], 1)
                sums = att_sum.rearrange("p (t h) -> p t h", t=T)[:, :, 0:len(heads)]
                inv = att_rs.rearrange("p (t h) -> p t h", t=T)[:, :, 0:len(heads)]
                dve.wait_ge(at_e, n0 + len(heads))
                nc.vector.reciprocal(inv, sums).then_inc(at_rs, 1)
                dve.wait_ge(at_rs, k + 1)
                dve.wait_ge(at_o, k + 1)
                wide = heads[0]["wide"]
                m = BW // wide
                for b in range(4):
                    t, half = b // 2, b % 2
                    nc.vector.tensor_tensor(
                        xn[:, t, BW * half:BW * half + BW].rearrange("p (h n) -> p h n", h=m),
                        bank(4 + b).rearrange("p (h n) -> p h n", h=m),
                        inv[:, t, m * half:m * half + m].unsqueeze(2).to_broadcast([P, m, wide]),
                        ALU.mult).then_inc(bank_read[4 + b], 1)

            normalise("n_mix", x)
            lo(0)
            norm_lower("n_mix", p_hi, p_lo)
            lo(1)
            lo(2)

            acc = [work[:, 320:576], work[:, 576:832]]
            TAPS = K_B + 3

            def conv_part(c, base, part, glu_at):
                if part == 0:
                    dve.wait_ge(glu, glu_at)
                    nc.vector.tensor_copy(work[:, 0:UP], misc[:, bass.ds(c * UP, UP)]).then_inc(conv_tap, 1)
                    nc.vector.tensor_copy(work[:, UP:UP + K_B], vec[:, bass.ds(c * NV + V_CONVB, K_B)])\
                        .then_inc(conv_tap, 1)
                    dve.wait_ge(conv_tap, base + 2)
                for k in (range(0, 8), range(8, 16), range(16, 24), range(24, K_B))[part]:
                    src, w = work[:, k:k + S], work[:, UP + k:UP + k + 1]
                    if k < 2:
                        nc.vector.tensor_scalar(acc[k], src, w, None, ALU.mult).then_inc(conv_tap, 1)
                    else:
                        dve.wait_ge(conv_tap, base + k + 1)
                        nc.vector.scalar_tensor_tensor(out=acc[k % 2], in0=src, scalar=w, in1=acc[k % 2],
                                                       op0=ALU.mult, op1=ALU.add).then_inc(conv_tap, 1)
                if part == 3:
                    dve.wait_ge(conv_tap, base + TAPS - 1)
                    nc.vector.scalar_tensor_tensor(
                        out=conv[:, bass.ds(c * S, S)], in0=acc[0], scalar=vec[:, bass.ds(c * NV + V_CBIAS, 1)],
                        in1=acc[1], op0=ALU.add, op1=ALU.add).then_inc(conv_tap, 1)

            def ugq(i, with_conv):
                lo(G_UGQ + 3, i)
                if with_conv:
                    conv_part(i - 2, TAPS * (i - 2), 0, i)
                dve.wait_ge(bank_read[1], USES["ugq"][1] + 1 + i)
                sig = work[:, 832:1344].rearrange("p (b n) -> p b n", b=2)
                dst = misc[:, bass.ds(2 * UP * i, 2 * UP)].rearrange("p (b n) -> p b n", b=2)[:, :, K_B - 1:UP]
                nc.vector.tensor_tensor(dst, ps[:, 0, :].rearrange("p (b n) -> p b n", b=2), sig,
                                        ALU.mult).then_inc(glu, 1)
                lo(G_UGQ + 4, i)
                if with_conv:
                    conv_part(i - 2, TAPS * (i - 2), 1, 0)
                    conv_part(i - 2, TAPS * (i - 2), 2, 0)
                lo(G_UGQ + 5, i)
                if with_conv:
                    conv_part(i - 2, TAPS * (i - 2), 3, 0)

            ugq(0, False)
            normalise("n_mem", mem_rows)
            ugq(1, False)
            with dve.Fori(2, 4) as i:
                ugq(i, True)
            norm_lower("n_mem", q_hi, q_lo)
            for i in range(8):
                lo(G_KV + 3 + i)
                conv_part(2 + i // 4, TAPS * (2 + i // 4), i % 4, 5)
            gcv = work[:, 1344:1860].rearrange("p (b n) -> p b n", b=2)
            ca = work[:, 1860:2372]
            with dve.Fori(0, 4) as i:
                dve.wait_ge(bank_read[0], USES["cvb"][0] + 1 + i)
                dve.wait_ge(slot_used, G_CVB + 2 + 3 * i)
                nc.vector.tensor_tensor(gcv[:, :, K_A - 1:K_A - 1 + S], ps[:, 1, :].rearrange("p (b n) -> p b n", b=2),
                                        work[:, 832:1344].rearrange("p (b n) -> p b n", b=2),
                                        ALU.mult).then_inc(bank_read[1], 1)
                lo(G_CVB + 3, i)
                dve.wait_ge(bank_read[1], USES["cvb"][1] + 1 + i)
                for m in range(2 * K_A):
                    b, k = m % 2, K_A - 1 - m // 2
                    src = gcv[:, b, k:k + S]
                    w = vec[:, bass.ds(2 * NV * i + b * NV + V_CONVA + k, 1)]
                    dst = ca[:, b * S:(b + 1) * S]
                    if m < 2:
                        nc.vector.tensor_scalar(dst, src, w, None, ALU.mult).then_inc(ca_step, 1)
                    else:
                        dve.wait_ge(ca_step, 2 * K_A * i + m)
                        nc.vector.scalar_tensor_tensor(out=dst, in0=src, scalar=w, in1=dst, op0=ALU.mult,
                                                       op1=ALU.add).then_inc(ca_step, 1)
                lo(G_CVB + 4, i)
                dve.wait_ge(slot_used, G_CVB + 3 + 3 * i)
                dve.wait_ge(ca_step, 2 * K_A * i + 2 * K_A + 1)
                nc.vector.tensor_tensor(ca, bank(2), ca, ALU.mult).then_inc(bank_read[2], 1)
                lo(G_CVB + 5, i)
                dve.wait_ge(an_hi, i + 1)
                nc.vector.tensor_tensor(q_lo[:, bass.ds(BW * i, BW)], ca, q_hi[:, bass.ds(BW * i, BW)].bitcast(F32),
                                        ALU.subtract).then_inc(an_lo, 1)
            with dve.Fori(0, 3) as i:
                for j in range(3):
                    lo(G_GATE + 3 + j, i)
                    conv_part(i + 4, TAPS * 4 + TAPS * i, j, 5)
                conv_part(i + 4, TAPS * 4 + TAPS * i, 3, 5)
            for j in range(3):
                lo(G_GATE + 3 + j, 3)
            conv_t = conv.rearrange("p (c n) -> p c n", c=KD)

            def gate_of(j, i):
                return gates[:, j * KD * S + BW * i:j * KD * S + BW * (i + 1)]

            for i in range(4):
                dve.wait_ge(slot_used, G_AO + i + 1)
                nc.vector.tensor_tensor(merged[:, BW * i:BW * (i + 1)], bank(i), gate_of(0, i),
                                        ALU.mult).then_inc(bank_read[i], 1)
                lo(G_AO + i + 3)
                conv_part(KD - 1, TAPS * (KD - 1), i, 5)
            dve.wait_ge(ln_mean, 1)
            nc.vector.tensor_tensor(conv_t, conv_t, bank(7, 0, S).unsqueeze(1).to_broadcast([P, KD, S]),
                                    ALU.subtract).then_inc(ln_ctr, 1)
            attention("att1")
            dve.wait_ge(ln_var, 1)
            nc.vector.tensor_scalar(ln_v, bank(0, 0, T), EPS, None, ALU.add).then_inc(ln_ms, 1)
            dve.wait_ge(ln_r, 1)
            for t in range(T):
                last = nc.vector.tensor_scalar(ln_diag[:, P * t:P * t + P], ident[:, :], ln_rs[:, t:t + 1], float(D),
                                               ALU.mult, ALU.mult)
            last.then_inc(ln_dg, 1)
            split_rows(0)
            lo(G_ATT + 3)

            def norm_channels():
                dve.wait_ge(ln_bc, 1)
                nc.vector.tensor_tensor(conv_t, conv_t, bank(4, 0, S).unsqueeze(1).to_broadcast([P, KD, S]),
                                        ALU.mult).then_inc(ln_z, 1)

            def merge(j, g0, count, between):
                for i in range(4):
                    dve.wait_ge(slot_used, g0 + i + 1)
                    nc.vector.tensor_tensor(gate_of(j, i), bank(i), gate_of(j, i), ALU.mult).then_inc(bank_read[i], 1)
                    dve.wait_ge(bank_read[i], USES[count][i] + 1)
                    nc.vector.tensor_tensor(merged[:, BW * i:BW * (i + 1)], merged[:, BW * i:BW * (i + 1)],
                                            gate_of(j, i), ALU.add).then_inc(mg, 1)
                    between(i)

            def during_att_out(i):
                if i == 0:
                    norm_channels()
                else:
                    lo(G_ATT + 3 + i)
                if i > 1:
                    dve.wait_ge(ln_hi, i - 1)
                    half = slice(1024 * (i - 2), 1024 * (i - 1))
                    nc.vector.tensor_tensor(q_lo[:, half], conv[:, half], q_hi[:, half].bitcast(F32),
                                            ALU.subtract).then_inc(ln_lo, 1)

            def merged_lower(i):
                dve.wait_ge(mg_hi, i + 1)
                nc.vector.tensor_tensor(p_lo[:, BW * i:BW * (i + 1)], merged[:, BW * i:BW * (i + 1)],
                                        p_hi[:, BW * i:BW * (i + 1)].bitcast(F32), ALU.subtract).then_inc(mg_lo, 1)

            def during_b_out(i):
                if i:
                    merged_lower(i - 1)
                if i == 3:
                    merged_lower(3)
                lo(G_BO + i + 3)

            merge(2, G_ATT, "att_out", during_att_out)
            merge(1, G_BO, "b_out", during_b_out)
            for i in range(3):
                lo(G_WO + i + 3)
            residual_norm("n_ffn", 0, G_WO + 4)
            lo(G_WO + 6)

            def other_taps(i, part, n):
                dve.wait_ge(f_y, n + 1)
                for m in range(4):
                    h, k = m % 2, 1 - m // 2
                    back = K_F - 1 - k
                    dst = work[:, BW * part + S * h + back:BW * part + S * h + S]
                    w = cwf[:, bass.ds(k * FT + part * (FT // 2) + 2 * i + h, 1)]
                    if k == 0:
                        dve.wait_ge(f_c, 2 * n + h + 1)
                    last = nc.vector.scalar_tensor_tensor(out=dst, in0=bank(part, S * h, S * h + S - back), scalar=w,
                                                          in1=dst, op0=ALU.mult, op1=ALU.add)
                    if k == 1:
                        last.then_inc(f_c, 1)
                last.then_inc(bank_read[part], 1)

            def gated(n):
                dve.wait_ge(f_s, n + 1)
                dve.wait_ge(bank_read[1], USES["ffn1"][1] + n + 1)
                nc.vector.tensor_tensor(work[:, 1536:2048], work[:, 1024:1536], work[:, 512:1024],
                                        ALU.mult).then_inc(f_u, 1)

            def u_lower(n):
                dve.wait_ge(f_hi, n + 1)
                nc.vector.tensor_tensor(q_lo[:, 0:BW], work[:, 1536:2048], q_hi[:, 0:BW].bitcast(F32),
                                        ALU.subtract).then_inc(f_lo, 1)

            other_taps(0, 0, 0)
            lo(G_FFN1 + 3)
            other_taps(0, 1, 1)
            gated(0)
            lo(G_FFN1 + 4)
            u_lower(0)
            with dve.Fori(0, FG - 1) as i:
                other_taps(i + 1, 0, 2 * i + 2)
                lo(G_FFN1 + 5, i)
                other_taps(i + 1, 1, 2 * i + 3)
                gated(i + 1)
                lo(G_FFN1 + 6, i)
                u_lower(i + 1)
                lo(G_FFN1 + 7, i)
            def final_norm(name, k):
                n = NORMS.index(name)
                dve.wait_ge(gain_in, 16 * (k + 1))
                for t in range(T):
                    dve.wait_ge(norm_r, T * n + t + 1)
                    nc.vector.scalar_tensor_tensor(out=x[:, t, :], in0=x[:, t, :], scalar=rr[:, 2 * n + t:2 * n + t + 1],
                                                   in1=gfin, op0=ALU.mult, op1=ALU.mult).then_inc(fin_x, 1)

            residual("fin1", 1, G_EV)
            final_norm("fin1", 0)
            dve.wait_ge(fin_x, 2)
            normalise("n_mix2a", x)
            norm_lower("n_mix2a", p_hi, p_lo)
            lo(G_EV + 2)
            for i in range(7):
                lo(G_EV + i + 3)
            dve.wait_ge(l_sq, 1)
            nc.vector.tensor_scalar(lat[:, 0:2], lat[:, 0:2], 1.0 / B_Q_RANK, EPS, ALU.mult, ALU.add)
            nc.vector.tensor_scalar(lat[:, 2:4], lat[:, 2:4], 1.0 / B_KV_RANK, EPS, ALU.mult, ALU.add).then_inc(l_ms, 1)
            NH = A_HEADS + A_KV
            dve.wait_ge(h_sq, 2)
            nc.vector.tensor_reduce(out=hss, in_=misc[:, 640:1920].rearrange("p (h n) -> p h n", n=HD), axis=AX.X,
                                    op=ALU.add).then_inc(h_ss, 1)
            dve.wait_ge(h_ss, 1)
            nc.vector.tensor_scalar(hss, hss, 1.0 / HD, EPS, ALU.mult, ALU.add).then_inc(h_ms, 1)
            lo(G_EV + 10)
            for c in range(5):
                dve.wait_ge(l_hi, min(c // 2 * 2 + 2, 5))
                last = nc.vector.scalar_tensor_tensor(
                    out=p_lo[:, c * S:(c + 1) * S], in0=bank(c // 2, c % 2 * S, c % 2 * S + S), scalar=gain(V_LAT, c),
                    in1=p_hi[:, c * S:(c + 1) * S].bitcast(F32), op0=ALU.mult, op1=ALU.subtract)
                if c in (1, 3, 4):
                    last.then_inc(bank_read[c // 2], 1)
            for i in range(4):
                lo(G_UQ + i + 3)

            dve.wait_ge(h_r, 1)
            dve.wait_ge(rope_in, 48)
            for t in range(T):
                heads = z[:, t, 0:Z_V].rearrange("p (h n) -> p h n", h=NH)
                nc.vector.tensor_tensor(heads, heads, hr[:, NH * t:NH * t + NH].unsqueeze(2).to_broadcast([P, NH, HD]),
                                        ALU.mult).then_inc(h_n, 1)
            dve.wait_ge(h_n, 2)
            for t in range(T):
                for h0, nh, g in ((0, A_HEADS, gq), (A_HEADS, A_KV, gk)):
                    part = z[:, t, HD * h0:HD * (h0 + nh)].rearrange("p (h n) -> p h n", h=nh)
                    nc.vector.tensor_tensor(part, part, g.unsqueeze(1).to_broadcast([P, nh, HD]),
                                            ALU.mult).then_inc(h_n, 1)
            dve.wait_ge(h_n, 6)

            def rotate(part, nh, width, cos, sin, m1, m2, step, done, free=0, pairs=None):
                if free:
                    dve.wait_ge(done, free)
                one = m1.rearrange("p (h n) -> p h n", h=nh)
                nc.vector.tensor_tensor(one, part, cos.unsqueeze(1).to_broadcast([P, nh, width]), ALU.mult)
                two = m2.rearrange("p (h n) -> p h n", h=nh)

                def side(a, s):
                    return a.rearrange("p h (r s n) -> p h r s n", r=2, s=2)[:, :, :, s, :]

                sin_b = sin.unsqueeze(1).to_broadcast([P, nh, width])
                nc.vector.tensor_tensor(side(two, 0), side(part, 1), side(sin_b, 0), ALU.mult)
                nc.vector.tensor_tensor(side(two, 1), side(part, 0), side(sin_b, 1), ALU.mult).then_inc(step[0], 1)
                dve.wait_ge(step[0], step[1])
                if nh == NH:
                    def by_pair(a):
                        return a[:, 0:A_HEADS, :].rearrange("p (v h) n -> p v h n", v=A_KV)

                    nc.vector.tensor_tensor(pairs.rearrange("p (h v n) -> p v h n", h=A_HEADS // A_KV, v=A_KV),
                                            by_pair(one), by_pair(two), ALU.add)
                    part, one, two = part[:, A_HEADS:NH, :], one[:, A_HEADS:NH, :], two[:, A_HEADS:NH, :]
                nc.vector.tensor_tensor(part, one, two, ALU.add).then_inc(done, 1)

            for t in range(T):
                rotate(z[:, t, 0:Z_V].rearrange("p (h n) -> p h n", h=NH), NH, HD, rope[:, t, 0:64],
                       rope[:, t, 64:128], misc[:, 0:640], misc[:, 640:1280], (h_n, 7 + t), rope_a,
                       t, qrot[:, t, :])
            for t in range(T):
                rotate(z[:, t, Z_KR:EV_IN].unsqueeze(1), 1, B_ROPE, rope[:, t, 128:160], rope[:, t, 160:192],
                       misc[:, 1280:1312], misc[:, 1312:1344], (h_n, 9 + t), rope_a, 3 * t)
            dve.wait_ge(rope_a, 4)
            for b in range(4, 8):
                dve.wait_ge(bank_read[b], USES["ukv"][b] + 1)
            for t in range(T):
                keys = kf[:, t, :].rearrange("p (h n) -> p h n", h=B_HEADS)
                nc.vector.tensor_copy(keys[:, :, B_NOPE:B_QK],
                                      z[:, t, Z_KR:EV_IN].unsqueeze(1).to_broadcast([P, B_HEADS, B_ROPE]))
                nc.vector.tensor_copy(keys[:, :, 0:B_NOPE],
                                      kvb[:, t, :].rearrange("p (h n) -> p h n", h=B_HEADS)[:, :, 0:B_NOPE])\
                    .then_inc(rope_b, 1)
            for b in range(4):
                dve.wait_ge(bank_read[b], USES["uq"][b] + 1)
            for t in range(T):
                rotate(qb[:, t, :].rearrange("p (h n) -> p h n", h=B_HEADS)[:, :, B_NOPE:B_QK], B_HEADS, B_ROPE,
                       rope[:, t, 128:160], rope[:, t, 160:192], misc[:, 0:256], misc[:, 256:512],
                       (h_n, 11 + t), rope_b, 3 * t)
            attention("att2")
            split_rows(1)
            for i in range(3):
                lo(G_EVO + i + 3)
            residual_norm("n_ffn2a", 2, G_EVO + 4)
            lo(G_EVO + 6)

            def group(k, n, slot, up, i=0):
                dve.wait_ge(f2_r, FP * k + n + 1 + 3 * i)
                if FP * k + n > 0:
                    dve.wait_ge(f2_lo, FP * k + n + 3 * i)
                nc.vector.tensor_tensor(work[:, 1024:1536], work[:, 0:BW], work[:, 0:BW], ALU.mult).then_inc(f2_sq, 1)
                lo(up + 3, 2 * i)
                dve.wait_ge(f2_hi, FP * k + n + 1 + 3 * i)
                nc.vector.tensor_tensor(q_lo[:, BW * slot:BW * slot + BW], work[:, 1024:1536],
                                        q_hi[:, BW * slot:BW * slot + BW].bitcast(F32), ALU.subtract).then_inc(f2_lo, 1)

            def ffn2(k, g0):
                group(k, 0, 0, g0)

                def three(i):
                    for j in range(3):
                        group(k, 1 + j, (1 + j) % 3, g0 + 1 + 2 * j, i)
                        lo(g0 + 5 + 2 * j, 2 * i)

                with dve.Fori(0, (FP - 1) // 3 - 1) as i:
                    three(i)
                three((FP - 1) // 3 - 1)

            ffn2(0, G_F2A)
            residual_norm("n_mix2b", 3, G_QK)
            lo(G_QK + 2)
            for i in range(8):
                lo(G_QK + i + 3)
            for i in range(4):
                lo(G_V + i + 3)
            attention("att3")
            split_rows(2)
            for i in range(3):
                lo(G_ODO + i + 3)
            residual_norm("n_ffn2b", 4, G_ODO + 4)
            lo(G_ODO + 6)
            ffn2(1, G_F2B)
            residual("fin2", 5, G_END)
            final_norm("fin2", 1)

        @block.tensor
        def _(pe):
            def three_passes(dst, w_at, x_at, weights_first, first, last):
                (wh, wl), (xh, xl) = w_at, x_at
                for n, (w, a) in enumerate(((wh, xh), (wh, xl), (wl, xh))):
                    lhs, rhs = (w, a) if weights_first else (a, w)
                    ins = nc.tensor.matmul(dst, lhs, rhs, start=first and n == 0, stop=last and n == 2)
                return ins

            def to_channels(g, b, pair, i=0, after=None):
                pe.wait_ge(lo_ready, g + 1 + R * i)
                r = g % R
                for h in range(2):
                    for k in range(KD):
                        if after and h == 0 and k % 2 == 0:
                            free(k // 2, USES[after][k // 2] + 1)
                        at = slice(256 * k + P * h, 256 * k + P * h + P)
                        ins = three_passes(bank(b, S * h, S * h + S), (whi[:, r, at], wlo[:, r, at]),
                                           [a[:, S * k:S * k + S] for a in pair], True, k == 0, k == KD - 1)
                ins.then_inc(slot_used, 1)

            def to_rows(g, tiles, pair, k0, b0, nb, n, first, last, i=0, signal=False):
                pe.wait_ge(lo_ready, g + 1 + R * i)
                r = g % R
                for t in range(T):
                    for k in range(tiles):
                        at = S * (k0 + k) + P * t
                        for m in range(nb):
                            c0 = k * nb * n + m * n
                            ins = three_passes(bank(b0 + nb * t + m, 0, n), (whi[:, r, c0:c0 + n], wlo[:, r, c0:c0 + n]),
                                               [a[:, at:at + P] for a in pair], False,
                                               first and k == 0, last and k == tiles - 1)
                    if signal and t == 0:
                        ins.then_inc(rows_done, 1)
                ins.then_inc(slot_used, 1)

            def free(b, n):
                if n > 0:
                    pe.wait_ge(bank_read[b], n)

            def transpose_norm(name):
                m = TNORMS.index(name)
                for b in range(4):
                    free(b, USES[name][b])
                for t in range(T):
                    pe.wait_ge(norm_xn, T * m + t + 1)
                    for c in range(KD):
                        last = nc.tensor.transpose(bank(c // 2, c % 2 * S + P * t, c % 2 * S + P * t + P),
                                                   xn[:, t, P * c:P * c + P], ident[:, :])
                        if t == T - 1 and c % 2:
                            last.then_inc(norm_tr, 1)

            def transpose_rows(phase, att):
                for b in range(4, 8):
                    free(b, USES[att][b] + 1)
                for b in range(4):
                    free(b, USES[phase][b])
                for t in range(T):
                    for c in range(KD):
                        last = nc.tensor.transpose(bank(c // 2, c % 2 * S + P * t, c % 2 * S + P * t + P),
                                                   xn[:, t, P * c:P * c + P], ident[:, :])
                last.then_inc(o_tr, 1)

            def ready_low(phase):
                for b in range(4):
                    free(b, USES[phase][b] + 1)

            def attention(name):
                heads, n0, scale, biased, k = ATT[name]
                N = len(heads)
                for b in (0, 1):
                    free(b, USES[name][b])
                for i in range(N + 2):
                    n = n0 + i
                    if i < N:
                        if i >= 2:
                            pe.wait_ge(at_max if biased else at_e, n - 1)
                        for t in range(T):
                            qs, ks = heads[i]["q"](t), heads[i]["k"]
                            for j in range(len(qs)):
                                ins = nc.tensor.matmul(bank(i % 2, S * t, S * t + S), qs[j], ks[j],
                                                       start=j == 0, stop=j == len(qs) - 1)
                        ins.then_inc(at_s, 1)
                    if 1 <= i <= N:
                        b = 2 + (i - 1) % 2
                        free(b, USES[name][b] + (i - 1) // 2)
                        pe.wait_ge(at_e, n)
                        for m in range(2):
                            for t in range(T):
                                ins = nc.tensor.transpose(bank(b, S * m + P * t, S * m + P * t + P),
                                                          prob[:, (i - 1) % 2, t, P * m:P * m + P], ident[:, :])
                        ins.then_inc(at_t, 1)
                    if i >= 2:
                        h, b = heads[i - 2], 2 + i % 2
                        free(b, USES[name][b] + (i - 2) // 2 + 1)
                        if i == 2:
                            if name == "att1":
                                pe.wait_ge(ln_ctr, 1)
                            for b in range(4, 8):
                                free(b, USES[name][b])
                        for t in range(T):
                            for m in range(2):
                                ins = nc.tensor.matmul(
                                    bank(4 + 2 * t + h["at"] // BW, h["at"] % BW, h["at"] % BW + h["wide"]),
                                    probT[:, i % 2, m, P * t:P * t + P], h["v"](m), start=m == 0, stop=m == 1)
                ins.then_inc(at_o, 1)

            p_pair, q_pair = (p_hi, p_lo), (q_hi, q_lo)

            pe.wait_ge(const_ready, 2)
            pe.wait_ge(vec_in, 16)
            for c in range(KD):
                last = nc.tensor.transpose(bank(0, NV * c, NV * (c + 1)), vec_rows[:, P * c:P * c + P],
                                           ident[0:NV, 0:NV])
            last.then_inc(vec_tr, 1)
            transpose_norm("n_mix")
            phases = (("ugq", G_UGQ), ("cvb", G_CVB), ("gate", G_GATE))

            def memory():
                pe.wait_ge(cwf_in, 16)
                for k in range(K_F):
                    last = nc.tensor.transpose(bank(3, FT * k, FT * (k + 1)), cwf_rows[:, P * k:P * k + P],
                                               ident[0:FT, 0:FT])
                last.then_inc(vec_tr, 1)
                pe.wait_ge(glu, 5)
                transpose_norm("n_mem")
                for i in range(4):
                    free(i, USES["kv"][i])
                    to_channels(G_KV + i, i, q_pair, 0, "n_mem" if i == 0 else None)
                for i in range(4):
                    to_rows(G_KV + 4 + i, 2, q_pair, 2 * i, 4, 2, BW, i == 0, i == 3)

            ready_low("n_mix")
            for phase, g0 in phases:
                if phase == "cvb":
                    memory()
                with pe.Fori(0, 4) as i:
                    for j in range(3):
                        if phase == "ugq" and j == 0:
                            pe.wait_ge(glu, 1 + i)
                        elif phase == "cvb" and j == 0:
                            pe.wait_ge(bank_read[0], USES["cvb"][0] + i)
                        else:
                            pe.wait_ge(bank_read[j], USES[phase][j] + i)
                        to_channels(g0 + j, j, p_pair, i)
            for i in range(4):
                free(i, USES["a_out"][i])
                if i == 0:
                    pe.wait_ge(an_lo, 4)
                to_channels(G_AO + i, i, q_pair)
            pe.wait_ge(conv_tap, (K_B + 3) * KD)
            free(7, USES["att1"][7])
            for c in range(KD):
                last = nc.tensor.matmul(bank(7, 0, S), mean_w[:, :], conv[:, S * c:S * c + S],
                                        start=c == 0, stop=c == KD - 1)
            last.then_inc(ln_mean, 1)
            attention("att1")
            pe.wait_ge(ln_sq, 1)
            for t in range(T):
                for c in range(KD):
                    last = nc.tensor.matmul(bank(0, t, t + 1), ln_sqs[:, S * c + P * t:S * c + P * t + P],
                                            mean_w[:, 0:1], start=c == 0, stop=c == KD - 1)
            last.then_inc(ln_var, 1)
            pe.wait_ge(ln_ms, 1)
            transpose_rows("o1", "att1")
            for i in range(4):
                free(i, USES["att_out"][i])
                to_channels(G_ATT + i, i, p_pair, 0, "o1" if i == 0 else None)
                if i == 0:
                    pe.wait_ge(ln_dg, 1)
                    for t in range(T):
                        last = nc.tensor.matmul(bank(4, P * t, P * t + P), mean_w[:, :], ln_diag[:, P * t:P * t + P],
                                                start=True, stop=True)
                    last.then_inc(ln_bc, 1)
            pe.wait_ge(ln_lo, 2)
            for i in range(4):
                free(i, USES["b_out"][i])
                to_channels(G_BO + i, i, q_pair)
            for b in range(4, 8):
                free(b, USES["w_o"][b])
            for i in range(4):
                pe.wait_ge(mg_lo, i + 1)
                to_rows(G_WO + i, 2, p_pair, 2 * i, 4, 2, BW, i == 0, i == 3, 0, i == 3)
            transpose_norm("n_ffn")

            def gate_up(n, g, i=0, after=None):
                for part in range(2):
                    if not after or part:
                        free(part, USES["ffn1"][part] + n + i)
                    to_channels(g + part, part, p_pair, i, after if part == 0 else None)

            gate_up(0, G_FFN1, 0, "n_ffn")
            pe.wait_ge(f_lo, 1)
            for b in range(4, 8):
                free(b, USES["ffn1"][b])

            def ffn1_round(i):
                first = isinstance(i, int) and i == 0
                gate_up(1, G_FFN1 + 2, i)
                pe.wait_ge(f_lo, 1 + i)
                to_rows(G_FFN1 + 4, 2, q_pair, 0, 4, 2, BW, first, False, i)

            ffn1_round(0)
            with pe.Fori(1, FG - 1) as i:
                ffn1_round(i)
            pe.wait_ge(f_lo, FG)
            to_rows(G_EV - 1, 2, q_pair, 0, 4, 2, BW, False, True, 0, True)
            transpose_norm("n_mix2a")
            ready_low("n_mix2a")
            for b in (4, 5):
                free(b, USES["ev_in"][b])
            for i in range(KD):
                to_rows(G_EV + i, 1, p_pair, i, 0, 3, 480, i == 0, i == KD - 1)
            pe.wait_ge(l_x, 1)
            for b in range(3):
                free(b, USES["lat"][b])
            for t in range(T):
                for c in range(5):
                    last = nc.tensor.transpose(bank(c // 2, c % 2 * S + P * t, c % 2 * S + P * t + P),
                                               z[:, t, Z_CQ + P * c:Z_CQ + P * c + P], ident[:, :])
            last.then_inc(l_tr, 1)
            for b in range(3):
                free(b, USES["lat"][b] + 1)
            free(3, USES["uq"][3])
            for i in range(3):
                to_rows(G_UQ + i, 1, p_pair, i, 0, 2, 384, i == 0, i == 2)
            for b in range(4, 8):
                free(b, USES["ukv"][b])
            to_rows(G_UKV, 2, p_pair, 3, 4, 2, BW, True, True)
            for i in range(11):
                b = i % 4
                pe.wait_ge(rope_a, 2) if i == 0 else None
                pe.wait_ge(rope_b, 4) if i == 3 else None
                free(b, USES["ev_tr"][b] + i // 4)
                for c in range(1 if i == 2 else 2):
                    for t in range(T):
                        at = slice(S * c + P * t, S * c + P * t + P)
                        if i < 2:
                            src = qrot[:, t, P * (2 * i + c):P * (2 * i + c) + P]
                        elif i == 2:
                            src = z[:, t, Z_K:Z_V]
                        else:
                            h = 2 * ((i - 3) % 4) + c
                            src = (qb if i < 7 else kf)[:, t, B_QK * h:B_QK * h + B_QK]
                        dst = ps[:, b, at] if i < 3 else ps[0:B_QK, b, at]
                        last = nc.tensor.transpose(dst, src, ident[:, :])
                last.then_inc(ev_tr, 1)
            for b in range(4):
                free(b, USES["att2"][b])
            attention("att2")
            transpose_rows("o2", "att2")
            for b in range(4, 8):
                free(b, USES["ev_out"][b])
            for i in range(4):
                free(i, USES["ev_out"][i])
                to_rows(G_EVO + i, 2, p_pair, 2 * i, 4, 2, BW, i == 0, i == 3, 0, i == 3)
            transpose_norm("n_ffn2a")

            def ffn2(phase, k, g0, after):
                to_channels(g0, 0, p_pair, 0, after)
                for b in range(4, 8):
                    free(b, USES[phase][b])

                def three(i):
                    for j in range(3):
                        to_channels(g0 + 1 + 2 * j, (1 + j) % 3, p_pair, 2 * i)
                        pe.wait_ge(f2_lo, FP * k + j + 1 + 3 * i)
                        to_rows(g0 + 2 + 2 * j, 2, q_pair, 2 * j, 4, 2, BW,
                                isinstance(i, int) and i == 0 and j == 0, False, 2 * i)

                three(0)
                with pe.Fori(1, (FP - 1) // 3) as i:
                    three(i)
                pe.wait_ge(f2_lo, FP * (k + 1))
                to_rows(g0 + 2 * FP - 1, 2, q_pair, 0, 4, 2, BW, False, True, 0, True)

            ffn2("ffn2a", 0, G_F2A, "n_ffn2a")
            transpose_norm("n_mix2b")
            for i in range(8):
                if i:
                    free(i % 4, USES["qk"][i % 4] + i // 4)
                to_channels(G_QK + i, i % 4, p_pair, 0, None if i else "n_mix2b")
            for b in range(4, 8):
                free(b, USES["v"][b])
            for i in range(4):
                to_rows(G_V + i, 2, p_pair, 2 * i, 4, 2, BW, i == 0, i == 3)
            for b in range(4):
                free(b, USES["att3"][b])
            for b in range(4, 8):
                free(b, USES["att3"][b])
            attention("att3")
            transpose_rows("o3", "att3")
            for i in range(4):
                free(i, USES["od_out"][i])
                to_rows(G_ODO + i, 2, p_pair, 2 * i, 4, 2, BW, i == 0, i == 3, 0, i == 3)
            transpose_norm("n_ffn2b")
            ffn2("ffn2b", 1, G_F2B, "n_ffn2b")


def rope_table():
    import numpy as np
    t = np.arange(S)
    pos = (t // GRID_W, t % GRID_W)
    parts = []
    for width in (HD // 2, B_ROPE // 2):
        inv = np.float32(10000.0) ** (-np.arange(0, width, 2, dtype=np.float32) / np.float32(width))
        ang = [(p.astype(np.float32)[:, None] * inv[None, :]).astype(np.float32) for p in pos]
        cos, sin = [np.cos(a) for a in ang], [np.sin(a) for a in ang]
        parts += [cos[0], cos[0], cos[1], cos[1], -sin[0], sin[0], -sin[1], sin[1]]
    return np.ascontiguousarray(np.concatenate(parts, axis=1).astype(np.float32))


def kernel(**inputs):
    import numpy as np
    import concourse.bacc as bacc
    from concourse.bass_utils import run_bass_kernel_spmd as run

    a = {k: np.asarray(v) for k, v in inputs.items()}
    rows = [a["conv_b_w"][0], a["conv_a_w"][0], a["norm_mix_g"], a["norm_mem_g"], a["b_gate"].reshape(3, D),
            a["conv_b_bias"], a["ln_b_g"], a["ln_b_b"], a["norm_ffn_g"], a["norm_mix_2"], a["norm_ffn_2"],
            np.concatenate([a["ev_b_q_norm_2"][0], a["ev_b_kv_norm_2"][0],
                            np.zeros(D - B_Q_RANK - B_KV_RANK, np.float32)])[None]]
    data = {
        "x": a["x"][0], "mem": a["mem"][0], "vecs": np.concatenate(rows, axis=0),
        "w_in": a["w_in"][0], "w_a_out": a["w_a_out"][0], "w_b_out": a["w_b_out"][0], "w_kv": a["w_kv"][0],
        "w_att_out": a["w_att_out"][0], "w_o": a["w_o"][0], "w_up": a["w_up"][0],
        "conv_ffn_w": a["conv_ffn_w"][0], "w_down": a["w_down"][0],
        "norm_final_g": a["norm_final_g"], "final_norm": a["final_norm_2"],
        "gq": a["ev_a_q_norm_2"][0], "gk": a["ev_a_k_norm_2"][0], "rope": rope_table(),
        "ev_w_in": a["ev_w_in_2"][0], "uq": a["ev_b_w_uq_2"][0], "ukv": a["ev_b_w_ukv_2"][0],
        "ev_w_out": a["ev_w_out_2"][0], "od_w_qkv": a["od_w_qkv_2"][0], "od_w_out": a["od_w_out_2"][0],
        "rpb_rev": a["od_rpb_2"][0][..., ::-1],
        "up_a": a["ffn_w_up_2"][0], "up_b": a["ffn_w_up_2"][1],
        "down_a": a["ffn_w_down_2"][0], "down_b": a["ffn_w_down_2"][1],
    }
    data = {k: np.ascontiguousarray(v) for k, v in data.items()}
    nc = bacc.Bacc("TRN2", target_bir_lowering=False, num_devices=1)
    aps = {k: nc.dram_tensor("in_" + k, list(v.shape), F32, kind="ExternalInput").ap() for k, v in data.items()}
    out = nc.dram_tensor("out", [S, D], F32, kind="ExternalOutput").ap()
    two_blocks(nc, aps, out)
    r = run(nc, [{"in_" + k: v for k, v in data.items()}], core_ids=[0])
    return r.results[0]["out"].reshape(1, S, D)
```

```python
from contextlib import ExitStack

import concourse.bass as bass
from concourse import mybir

F32 = mybir.dt.float32
F32R = mybir.dt.float32r
ACT = mybir.ActivationFunctionType
ALU = mybir.AluOpType
AX = mybir.AxisListType

P = 128
S = 256
T = S // P
D = 1024
KD = D // P
EPS = 1e-6
R = 3
SLOT = 2048
BW = 512

K_A, K_B, K_F = 3, 31, 3
CONV_DVE = 6
D_FF = 2816
FG = D_FF // 256
FT = 2 * D_FF // P
D_FF2 = 4096
FP = D_FF2 // 256
MEM_HEADS, MEM_HD = 4, 256
A_HEADS, A_KV, B_HEADS, HD = 8, 2, 8, 64
B_NOPE, B_ROPE = 64, 32
B_QK = B_NOPE + B_ROPE
B_Q_RANK, B_KV_RANK = 384, 256
EV_IN = 1440
Z_K, Z_V, Z_CQ, Z_CKV, Z_KR = 512, 640, 768, 1152, 1408
C_HEADS = 16
GRID_W = 64
RPB_H, RPB_W = 15, 31
NEG = -1.0e30

V_CONVB, V_CONVA, V_MIX, V_MEM, V_GATE, V_CBIAS, V_LNG, V_LNB, V_FFN = 0, 31, 34, 35, 36, 39, 40, 41, 42
V_MIX2, V_FFN2, V_LAT, NV = 43, 45, 47, 48

G_UGQ, G_KV, G_CVB, G_GATE, G_AO, G_ATT, G_BO, G_WO = 0, 12, 20, 32, 44, 48, 52, 56
G_FFN1 = 60
G_EV = G_FFN1 + 3 * FG
G_UQ, G_UKV, G_EVO = G_EV + 8, G_EV + 11, G_EV + 12
G_F2A = G_EVO + 4
G_QK = G_F2A + 2 * FP
G_V, G_ODO = G_QK + 8, G_QK + 12
G_F2B = G_ODO + 4
G_END = G_F2B + 2 * FP

LOW4 = {0: 1, 1: 1, 2: 1, 3: 1}
HIGH4 = {4: 1, 5: 1, 6: 1, 7: 1}
HEADS16 = {2: 8, 3: 8, **HIGH4}
PHASES = [
    ("setup", {0: 1}), ("n_mix", LOW4), ("ugq", {1: 4, 2: 4}), ("setup2", {3: 1}), ("n_mem", LOW4),
    ("kv", {**LOW4, **HIGH4}), ("cvb", {0: 4, 1: 4, 2: 4}), ("gate", {0: 4, 1: 4, 2: 4}),
    ("a_out", LOW4), ("att1", {2: 2, 3: 2, **HIGH4}), ("att_out", LOW4), ("b_out", LOW4),
    ("w_o", HIGH4), ("n_ffn", LOW4), ("ffn1", {0: FG, 1: FG, **HIGH4}), ("n_mix2a", LOW4),
    ("ev_in", {0: 1, 1: 1, 2: 1, 3: 1, 4: 1, 5: 1}), ("lat", {0: 1, 1: 1, 2: 1}), ("uq", LOW4), ("ukv", HIGH4),
    ("ev_tr", {0: 3, 1: 3, 2: 3, 3: 2}), ("att2", HEADS16), ("ev_out", LOW4),
    ("n_ffn2a", LOW4), ("ffn2a", HIGH4), ("n_mix2b", LOW4),
    ("qk", {0: 2, 1: 2, 2: 2, 3: 2}), ("v", HIGH4), ("att3", HEADS16), ("od_out", LOW4),
    ("n_ffn2b", LOW4), ("ffn2b", HIGH4),
]


def earlier_bank_uses():
    count, uses = [0] * 8, {}
    for name, used in PHASES:
        uses[name] = list(count)
        for bank, n in used.items():
            count[bank] += n
    return uses


USES = earlier_bank_uses()
NORMS = ["n_mix", "n_mem", "n_ffn", "fin1", "n_mix2a", "n_ffn2a", "n_mix2b", "n_ffn2b", "fin2"]
TNORMS = ["n_mix", "n_mem", "n_ffn", "n_mix2a", "n_ffn2a", "n_mix2b", "n_ffn2b"]
TGAIN = [V_MIX, V_MEM, V_FFN, V_MIX2, V_FFN2, V_MIX2 + 1, V_FFN2 + 1]


def two_blocks(nc, d, out):
    with ExitStack() as ctx:
        def sb(name, shape, dt=F32):
            return ctx.enter_context(nc.sbuf_tensor(name, shape, dt))

        def sem(name):
            return ctx.enter_context(nc.semaphore(name))

        raw = sb("raw", [P, R, SLOT])
        whi = sb("whi", [P, R, SLOT], F32R)
        wlo = sb("wlo", [P, R, SLOT], F32R)
        p_hi = sb("p_hi", [P, KD * S], F32R)
        p_lo = sb("p_lo", [P, KD * S], F32R)
        q_hi = sb("q_hi", [P, KD * S], F32R)
        q_lo = sb("q_lo", [P, KD * S], F32R)
        x = sb("x", [P, T, D])
        xn = sb("xn", [P, T, D])
        kreg = sb("kreg", [P, 2048])
        vreg = sb("vreg", [P, 2048])
        qreg = sb("qreg", [P, 2048])
        gates = sb("gates", [P, 3 * KD * S])
        merged = sb("merged", [P, KD * S])
        UP = K_B - 1 + S
        misc = sb("misc", [P, KD * UP + KD * S])
        work = sb("work", [P, 2560])
        vec = sb("vec", [P, KD * NV])
        cwf = sb("cwf", [P, K_F * FT])
        ident = sb("ident", [P, P])
        mean_w = sb("mean_w", [P, P])
        stat = sb("stat", [P, 260])
        ps = ctx.enter_context(nc.psum_tensor("ps", [P, 8, BW], F32))

        ms, rr = stat[:, 18:36], stat[:, 36:54]
        ss = stat[:, 192:228].rearrange("p (n m) -> p n m", m=2)
        ln_v, ln_rs = stat[:, 228:230], stat[:, 230:232]
        sm = stat[:, 232:250]
        mhalf = stat[:, 54:74]
        att_max, att_nmax = stat[:, 74:78], stat[:, 78:82]
        att_sum, att_rs = stat[:, 82:114], stat[:, 114:146]
        hss, hr = stat[:, 146:166], stat[:, 166:186]
        lat = stat[:, 186:190]

        def gain(row, c):
            return vec[:, c * NV + row:c * NV + row + 1]

        def bank(b, a=0, z=BW):
            return ps[:, b, a:z]

        mem_rows = merged[:, :].rearrange("p (t n) -> p t n", t=T)
        vec_rows = gates[0:NV, 0:D]
        cwf_rows = gates[0:FT, D:D + K_F * P]
        uglu = misc[:, 0:KD * UP].rearrange("p (c n) -> p c n", c=KD)
        conv = misc[:, KD * UP:KD * UP + KD * S]
        v_tok = vreg[:, :].rearrange("p (t n) -> p t n", t=T)

        ln_sqs = misc[:, 0:KD * S]
        ln_diag = misc[:, 0:S]
        z = gates[:, 0:2 * EV_IN].rearrange("p (t n) -> p t n", t=T)
        qb = gates[:, 2880:4416].rearrange("p (t n) -> p t n", t=T)
        kf = gates[:, 4416:5952].rearrange("p (t n) -> p t n", t=T)
        kvb = qreg[:, :].rearrange("p (t n) -> p t n", t=T)
        qT_a = merged[:, 0:1024]
        kT_a = merged[:, 1024:1280]
        gq, gk = merged[:, 1280:1344], merged[:, 1344:1408]
        rope = merged[:, 1408:1792].rearrange("p (t n) -> p t n", t=T)
        gfin = merged[:, 0:1024]
        qrot = misc[:, 1408:2432].rearrange("p (t n) -> p t n", t=T)
        rpb = misc[:, 0:16 * 219].rearrange("p (h n) -> p h n", h=C_HEADS)
        bias = gates[:, 0:16 * 384].rearrange("p (h j k) -> p h j k", h=C_HEADS, j=6)
        prob = work[:, 0:1536].rearrange("p (b t n) -> p b t n", b=3, t=T)
        UNIT_Q, UNIT_K, UNIT_V, UNIT = 0, 512, 1024, 1536
        unit_hi, unit_lo = (q_hi, p_hi), (q_lo, p_lo)
        PT = slice(UNIT, UNIT + T * S)
        bsc = misc[:, 0:1024].rearrange("p (b t n) -> p b t n", b=2, t=T)

        raw_in = [sem(f"raw_in{r}") for r in range(R)]
        hi_ready = sem("hi_ready")
        lo_ready = sem("lo_ready")
        slot_used = sem("slot_used")
        bank_read = [sem(f"bank_read{b}") for b in range(8)]
        mem_in, x_in, vec_in, cwf_in = sem("mem_in"), [sem(f"x_in{t}") for t in range(T)], sem("vec_in"), sem("cwf_in")
        gain_in, rope_in, rpb_in = sem("gain_in"), sem("rope_in"), sem("rpb_in")
        const_ready = sem("const_ready")
        vec_tr = sem("vec_tr")
        norm_sq, norm_ms, norm_r = sem("norm_sq"), sem("norm_ms"), sem("norm_r")
        norm_xn, norm_tr, norm_hi = sem("norm_xn"), sem("norm_tr"), sem("norm_hi")
        glu, conv_tap, pool_tap = sem("glu"), sem("conv_tap"), sem("pool_tap")
        pool_mul = sem("pool_mul")
        ga_ready, ca_step, an_hi, an_lo = sem("ga_ready"), sem("ca_step"), sem("an_hi"), sem("an_lo")
        ln_mean, ln_ctr, ln_sq, ln_var = sem("ln_mean"), sem("ln_ctr"), sem("ln_sq"), sem("ln_var")
        ln_ms, ln_r, ln_z, ln_y, ln_hi, ln_lo = (sem("ln_ms"), sem("ln_r"), sem("ln_z"), sem("ln_y"),
                                                 sem("ln_hi"), sem("ln_lo"))
        mg, mg_hi, mg_lo = sem("mg"), sem("mg_hi"), sem("mg_lo")
        at_s, at_max, at_nm, at_e = sem("at_s"), sem("at_max"), sem("at_nm"), sem("at_e")
        at_rs, at_p, at_t, at_h, at_v = sem("at_rs"), sem("at_p"), sem("at_t"), sem("at_h"), sem("at_v")
        qk_hi, qk_lo, v_hi, v_lo, v_zero = sem("qk_hi"), sem("qk_lo"), sem("v_hi"), sem("v_lo"), sem("v_zero")
        o_hi = sem("o_hi")
        f_y, f_c, f_s, f_u, f_hi, f_lo = sem("f_y"), sem("f_c"), sem("f_s"), sem("f_u"), sem("f_hi"), sem("f_lo")
        f2_r, f2_sq, f2_hi, f2_lo = sem("f2_r"), sem("f2_sq"), sem("f2_hi"), sem("f2_lo")
        fin_x, rows_done = sem("fin_x"), sem("rows_done")
        norm_sum, ln_dg, ln_bc = sem("norm_sum"), sem("ln_dg"), sem("ln_bc")
        h_sq, h_ss, h_ms, h_r, h_n = sem("h_sq"), sem("h_ss"), sem("h_ms"), sem("h_r"), sem("h_n")
        l_sq, l_ms, l_r, l_x, l_tr, l_hi = sem("l_sq"), sem("l_ms"), sem("l_r"), sem("l_x"), sem("l_tr"), sem("l_hi")
        rope_a, rope_b, ev_tr, bias_step = sem("rope_a"), sem("rope_b"), sem("ev_tr"), sem("bias_step")
        out_done = sem("out_done")

        block = ctx.enter_context(nc.Block())

        def heads_mem():
            units = [dict(q=(qreg[:, BW * h:BW * h + BW], P, BW), k=(kreg[:, BW * h:BW * h + BW], P, BW),
                          v=v_tok[:, :, h * MEM_HD:(h + 1) * MEM_HD], rows=(slice(0, P),),
                          chunks=(((0, 0), (S, S)),)) for h in range(MEM_HEADS)]
            return units

        def heads_even():
            both = (slice(0, HD), slice(HD, P))
            units = [dict(q=(qT_a[:, S * c:S * c + S], P, S), k=(kT_a, P, S),
                          v=z[:, :, Z_V:Z_V + P].rearrange("p t (h n) -> p t h n", h=2), rows=both,
                          chunks=(((0, 0),), ((0, 0),))) for c in range(A_HEADS // 2)]
            rows = (slice(0, B_QK),) * 2
            units += [dict(q=(kreg[0:B_QK, BW * c:BW * c + BW], B_QK, BW), k=(vreg[0:B_QK, BW * c:BW * c + BW], B_QK, BW),
                           v=kvb.rearrange("p t (h n) -> p t h n", h=B_HEADS)[:, :, 2 * c:2 * c + 2, HD:P], rows=rows,
                           chunks=(((0, 0),), ((S, S),))) for c in range(B_HEADS // 2)]
            return units

        def heads_odd():
            both = (slice(0, HD), slice(HD, P))
            return [dict(q=(qreg[:, S * c:S * c + S], P, S), k=(kreg[:, S * c:S * c + S], P, S),
                         v=v_tok[:, :, P * c:P * c + P].rearrange("p t (h n) -> p t h n", h=2), rows=both,
                         chunks=(((0, 0),), ((0, 0),))) for c in range(C_HEADS // 2)]

        ATT = {
            "att1": (heads_mem(), 1, 0, 0, lambda i: MEM_HD ** -0.5, False, 0),
            "att2": (heads_even(), 2, 4, 4, lambda i: (HD if i < A_HEADS else B_QK) ** -0.5, False, 1),
            "att3": (heads_odd(), 2, 12, 20, lambda i: HD ** -0.5, True, 2),
        }

        def unit_sides(u, H):
            side = (u + 2 - H) % 2
            return unit_hi[side], unit_lo[side]

        def unit_parts(u, unit, H):
            hi_part, lo_part = unit_sides(u, H)
            qk = []
            for at, (src, rows, n) in ((UNIT_Q, unit["q"]), (UNIT_K, unit["k"])):
                qk.append((src, hi_part[0:rows, at:at + n], lo_part[0:rows, at:at + n]))

            def v_place(part):
                if H == 1:
                    return part[:, UNIT_V:UNIT_V + T * S].rearrange("p (t n) -> p t n", t=T)
                return part[:, UNIT_V:UNIT_V + T * 256].rearrange("p (t h n) -> p t h n", t=T, h=4)[:, :, 0:3:2, 0:HD]

            return qk, (unit["v"], v_place(hi_part), v_place(lo_part))

        @block.sync
        def _(sp):
            x_rows = d["x"].rearrange("(t p) n -> p t n", p=P)
            for t in range(T):
                sp.dma_start(x[:, t, :], x_rows[:, t, :]).then_inc(x_in[t], 16)

            def load(g, src, kk, i=0):
                n = src.shape[-1]
                if g >= R or not isinstance(i, int):
                    sp.wait_ge(lo_ready, g - R + 1 + R * i)
                sp.dma_start(raw[:, g % R, 0:kk * n].rearrange("p (k n) -> p k n", k=kk),
                             src).then_inc(raw_in[g % R], 16)

            def cols(w, c0):
                return d[w].rearrange("(k p) n -> p k n", p=P)[:, :, bass.ds(c0, 256)]

            def rows(w, k0, kk):
                return d[w].rearrange("(k p) n -> p k n", p=P)[:, bass.ds(k0, kk), :]

            for j, c0 in enumerate((3 * D, 4 * D, 5 * D)):
                load(G_UGQ + j, cols("w_in", c0), KD)
            with sp.Fori(1, 4) as i:
                for j, c0 in enumerate((3 * D, 4 * D, 5 * D)):
                    load(G_UGQ + j, cols("w_in", c0 + 256 * i), KD, i)
            for i in range(4):
                load(G_KV + i, cols("w_kv", 256 * i), KD)
            for i in range(4):
                load(G_KV + 4 + i, d["w_kv"].rearrange("(k p) n -> p k n", p=P)[:, 2 * i:2 * i + 2, D:2 * D], 2)
            with sp.Fori(1, 5) as i:
                for j, c0 in enumerate((D, 2 * D, 0)):
                    load(G_CVB + j, cols("w_in", c0 - 256 + 256 * i), KD, i - 1)
            with sp.Fori(0, 4) as i:
                for j in range(3):
                    load(G_GATE + j, cols("w_in", (6 + j) * D + 256 * i), KD, i)
            for g0, w in ((G_AO, "w_a_out"), (G_ATT, "w_att_out"), (G_BO, "w_b_out")):
                for i in range(4):
                    load(g0 + i, cols(w, 256 * i), KD)
            for i in range(4):
                load(G_WO + i, rows("w_o", 2 * i, 2), 2)
            load(G_FFN1, cols("w_up", 0), KD)
            load(G_FFN1 + 1, cols("w_up", D_FF), KD)
            with sp.Fori(0, FG - 1) as i:
                load(G_FFN1 + 2, cols("w_up", 256 * i + 256), KD, i)
                load(G_FFN1 + 3, cols("w_up", D_FF + 256 * i + 256), KD, i)
                load(G_FFN1 + 4, rows("w_down", 2 * i, 2), 2, i)
            load(G_EV - 1, rows("w_down", 2 * FG - 2, 2), 2)
            for i in range(8):
                load(G_EV + i, rows("ev_w_in", i, 1), 1)
            for i in range(3):
                load(G_UQ + i, rows("uq", i, 1), 1)
            load(G_UKV, rows("ukv", 0, 2), 2)
            for i in range(4):
                load(G_EVO + i, rows("ev_w_out", 2 * i, 2), 2)

            def ffn2(g0, up, down):
                load(g0, cols(up, 0), KD)
                with sp.Fori(0, (FP - 1) // 3) as i:
                    for j in range(3):
                        load(g0 + 1 + 2 * j, cols(up, 768 * i + 256 * (j + 1)), KD, 2 * i)
                        load(g0 + 2 + 2 * j, rows(down, 6 * i + 2 * j, 2), 2, 2 * i)
                load(g0 + 2 * FP - 1, rows(down, 2 * FP - 2, 2), 2)

            ffn2(G_F2A, "up_a", "down_a")
            with sp.Fori(0, 2) as i:
                for j in range(3):
                    load(G_QK + j, cols("od_w_qkv", 768 * i + 256 * j), KD, i)
            for i in range(6, 8):
                load(G_QK + i, cols("od_w_qkv", 256 * i), KD)
            for i in range(4):
                load(G_V + i, d["od_w_qkv"].rearrange("(k p) n -> p k n", p=P)[:, 2 * i:2 * i + 2, 2 * D:3 * D], 2)
            for i in range(4):
                load(G_ODO + i, rows("od_w_out", 2 * i, 2), 2)
            ffn2(G_F2B, "up_b", "down_b")
            out_v = out.rearrange("(t p) n -> p t n", p=P)
            for t in range(T):
                sp.wait_ge(fin_x, T + t + 1)
                sp.dma_start(out_v[:, t, :], x[:, t, :]).then_inc(out_done, 16)
            sp.wait_ge(out_done, 16 * T)

        @block.gpsimd
        def _(pool):
            pool.dma_start(cwf_rows.rearrange("c (k p) -> c k p", k=K_F),
                           d["conv_ffn_w"].rearrange("k (c p) -> c k p", p=P)).then_inc(cwf_in, 16)
            nc.gpsimd.memset(ident[:, :], 0.0).then_inc(const_ready, 1)
            nc.gpsimd.memset(mean_w[:, :], 1.0 / D)
            nc.gpsimd.memset(mhalf, -0.5)
            pool.wait_ge(const_ready, 1)
            nc.gpsimd.affine_select(out=ident[:, :], in_=ident[:, :], compare_op=ALU.not_equal, fill=1.0, base=0,
                                    pattern=[[-1, P]], channel_multiplier=1).then_inc(const_ready, 1)
            nc.gpsimd.memset(uglu[:, :, 0:K_B - 1], 0.0).then_inc(glu, 1)
            nc.gpsimd.memset(work[:, 1344:1860].rearrange("p (b n) -> p b n", b=2)[:, :, 0:K_A - 1],
                             0.0).then_inc(ca_step, 1)

            def inverse_root(n):
                for c in range(T * n, T * n + T):
                    pool.wait_ge(norm_ms, c + 1)
                    nc.gpsimd.tensor_tensor(out=rr[:, c:c + 1], in0=ms[:, c:c + 1], in1=mhalf[:, 0:1],
                                            op=ALU.pow).then_inc(norm_r, 1)

            pool.wait_ge(ca_step, 1)
            def lower(places):
                for src, up, low in places:
                    last = nc.gpsimd.tensor_tensor(out=low, in0=src, in1=up.bitcast(F32), op=ALU.subtract)
                return last

            def attention(name):
                units, H, u0, n0, scale, biased, k = ATT[name]
                if H == 1:
                    for part, u in (("qk", 0), ("v", 0), ("qk", 1), ("qk", 2), ("v", 1), ("qk", 3), ("v", 2), ("v", 3)):
                        pool.wait_ge(qk_hi if part == "qk" else v_hi, u + 1)
                        qk, v = unit_parts(u, units[u], H)
                        if part == "qk":
                            lower(qk).then_inc(qk_lo, 1)
                        else:
                            lower([v]).then_inc(v_lo, 1)
                        if part == "qk" and u == 3:
                            pool.wait_ge(ln_ms, 1)
                            nc.gpsimd.tensor_tensor(out=ln_rs, in0=ln_v, in1=mhalf[:, 0:2], op=ALU.pow)\
                                .then_inc(ln_r, 1)
                    return
                for i in range(-H - 1, H * len(units) + 2):
                    if (i + 1) % H == 0 and (i + 1) // H + 1 < len(units):
                        u = (i + 1) // H + 1
                        pool.wait_ge(qk_hi, u0 + u + 1)
                        lower(unit_parts(u, units[u], H)[0]).then_inc(qk_lo, 1)
                    if i >= 2 and (i - 2) % H == 0 and (i - 2) // H < len(units):
                        u = (i - 2) // H
                        pool.wait_ge(v_hi, u0 + u + 1)
                        lower([unit_parts(u, units[u], H)[1]]).then_inc(v_lo, 1)

            inverse_root(0)
            inverse_root(1)
            pool.wait_ge(norm_tr, 8)
            steps = taps = 0
            for c in range(CONV_DVE, KD):
                pool.wait_ge(glu, 2 + c // 2)
                dst = conv[:, c * S:(c + 1) * S]
                for k in range(K_B):
                    src, w = misc[:, c * UP + k:c * UP + k + S], gain(V_CONVB + k, c)
                    if k == 0:
                        nc.gpsimd.tensor_scalar(dst, src, w, gain(V_CBIAS, c), ALU.mult, ALU.add).then_inc(pool_tap, 1)
                    else:
                        tap = xn[:, 0, S * (k % 2):S * (k % 2) + S]
                        nc.gpsimd.tensor_scalar(tap, src, w, None, ALU.mult).then_inc(pool_mul, 1)
                        steps += 1
                        pool.wait_ge(pool_mul, steps)
                        pool.wait_ge(pool_tap, taps)
                        nc.gpsimd.tensor_tensor(out=dst, in0=dst, in1=tap, op=ALU.add).then_inc(pool_tap, 1)
                    taps += 1
            attention("att1")
            inverse_root(2)
            pool.wait_ge(mg_lo, 4)
            pool.dma_start(gfin, d["norm_final_g"].partition_broadcast(P)).then_inc(gain_in, 16)
            pool.dma_start(gq, d["gq"].partition_broadcast(P)).then_inc(rope_in, 16)
            pool.dma_start(gk, d["gk"].partition_broadcast(P)).then_inc(rope_in, 16)
            pool.dma_start(rope, d["rope"].rearrange("(t p) n -> p t n", p=P)).then_inc(rope_in, 16)
            inverse_root(3)
            inverse_root(4)
            pool.wait_ge(l_ms, 1)
            nc.gpsimd.tensor_tensor(out=lat, in0=lat, in1=mhalf[:, 0:4], op=ALU.pow).then_inc(l_r, 1)
            pool.wait_ge(h_ms, 1)
            nc.gpsimd.tensor_tensor(out=hr, in0=hss, in1=mhalf, op=ALU.pow).then_inc(h_r, 1)
            attention("att2")
            inverse_root(5)
            pool.wait_ge(at_v, 20)
            pool.dma_start(gfin, d["final_norm"].partition_broadcast(P)).then_inc(gain_in, 16)
            for half in range(2):
                src = bass.AP(d["rpb_rev"].tensor, (5 - half) * RPB_W + 15 - 63,
                              [[1, GRID_W], [RPB_H * RPB_W, C_HEADS], [1, 219]])
                pool.dma_start(rpb[64 * half:64 * half + 64], src).then_inc(rpb_in, 16)
            pool.wait_ge(rpb_in, 32)
            steps = 0
            for h in range(C_HEADS):
                rev = bass.AP(misc[:, :].tensor, h * 219 + 63, [[KD * UP + KD * S, P], [RPB_W, 6], [-1, 64]])
                nc.gpsimd.tensor_copy(bias[:, h], rev).then_inc(bias_step, 1)
                steps += 1
                for c0, base, sign in ((0, 8, 1), (16, 7 - 16, -1)):
                    for half in range(2):
                        part = bias[64 * half:64 * half + 64, h, :, c0:c0 + 48]
                        pool.wait_ge(bias_step, steps)
                        nc.gpsimd.affine_select(out=part, in_=part, compare_op=ALU.is_ge, fill=NEG, base=base,
                                                pattern=[[0, 6], [sign, 48]], channel_multiplier=-sign)\
                            .then_inc(bias_step, 1)
                        steps += 1
                pool.wait_ge(bias_step, steps)
            inverse_root(6)
            attention("att3")
            inverse_root(7)
            inverse_root(8)

        @block.scalar
        def _(act):
            def hi(g, i=0):
                if isinstance(i, int):
                    g, i = g + R * i, 0
                    if g >= G_END:
                        return
                act.wait_ge(raw_in[g % R], 16 * (g // R + 1) + 16 * i)
                if g >= R:
                    act.wait_ge(slot_used, g - R + 1 + R * i)
                nc.scalar.activation(whi[:, g % R, :], raw[:, g % R, :], ACT.Copy).then_inc(hi_ready, 1)

            def squares(name, src, ready=None):
                n = NORMS.index(name)
                for b in range(2 * T):
                    if ready:
                        ready(b)
                    t, m = b // 2, b % 2
                    half = slice(BW * m, BW * m + BW)
                    last = nc.scalar.activation(xn[:, t, half], src[:, t, half], ACT.Square,
                                                accum_out=ss[:, T * n + t, m:m + 1])
                    if m:
                        last.then_inc(norm_sq, 1)

            def norm_upper(name, dst):
                m = TNORMS.index(name)
                for c in range(KD):
                    act.wait_ge(norm_tr, 4 * m + c // 2 + 1)
                    nc.scalar.activation(dst[:, c * S:(c + 1) * S], bank(c // 2, c % 2 * S, c % 2 * S + S), ACT.Copy,
                                         scale=gain(TGAIN[m], c)).then_inc(norm_hi, 1)

            def split_upper(unit_places):
                for src, upper, _lower in unit_places:
                    last = nc.scalar.activation(upper, src, ACT.Copy)
                return last

            def queries_keys(name, u):
                units, H, u0, n0, scale, biased, k = ATT[name]
                if u >= 2:
                    act.wait_ge(at_s, n0 + H * (u - 1))
                split_upper(unit_parts(u, units[u], H)[0]).then_inc(qk_hi, 1)

            def values(name, u):
                units, H, u0, n0, scale, biased, k = ATT[name]
                if u >= 2:
                    act.wait_ge(at_v, n0 + H * (u - 1))
                split_upper([unit_parts(u, units[u], H)[1]]).then_inc(v_hi, 1)

            def zeros_beside_values(parts):
                for part in parts:
                    gap = part[:, UNIT_V:UNIT_V + T * 256].rearrange("p (t n) -> p t n", t=T)[:, :, HD:P]
                    nc.scalar.activation(gap, ident[:, :].rearrange("p (t n) -> p t n", t=T), ACT.Copy,
                                         scale=0.0).then_inc(v_zero, 1)

            def attention(name, late=None):
                units, H, u0, n0, scale, biased, k = ATT[name]
                N = H * len(units)
                for i in range(N + 3):
                    n = n0 + i
                    if i == 1 and late:
                        late()
                    if i < N:
                        act.wait_ge(at_nm, n + 1)
                        if i >= 3:
                            act.wait_ge(at_t, n - 2)
                        for t in range(T):
                            src = bsc[:, i % 2, t, :] if biased else bank(i % 2, t * S, t * S + S)
                            last = nc.scalar.activation(prob[:, i % 3, t, :], src, ACT.Exp,
                                                        bias=att_nmax[:, 2 * (i % 2) + t:2 * (i % 2) + t + 1],
                                                        scale=1.0 if biased else scale(i),
                                                        accum_out=att_sum[:, 16 * t + i:16 * t + i + 1])
                        last.then_inc(at_e, 1)
                    if 2 <= i < N + 2:
                        act.wait_ge(at_t, n - 1)
                        if i >= 4:
                            act.wait_ge(at_v, n - 3)
                        nc.scalar.activation(unit_hi[i % 2][:, PT], bank(2 + i % 2), ACT.Copy).then_inc(at_h, 1)
                    if H == 2 and i % 2 and (i + 1) // 2 + 1 < len(units):
                        queries_keys(name, (i + 1) // 2 + 1)
                    if H == 1 and i == 1:
                        queries_keys(name, 3)
                    if i >= (2 if H == 2 else 4) and (i - 2) % H == 0 and (i - 2) // H < len(units):
                        values(name, (i - 2) // H)
                act.wait_ge(at_v, n0 + N)
                for b in range(4):
                    nc.scalar.activation(p_hi[:, BW * b:BW * (b + 1)], bank(4 + b), ACT.Copy).then_inc(o_hi, 1)

            act.dma_start(vec_rows, d["vecs"]).then_inc(vec_in, 16)
            act.dma_start(mem_rows, d["mem"].rearrange("(t p) n -> p t n", p=P)).then_inc(mem_in, 16)
            squares("n_mix", x, lambda b: act.wait_ge(x_in[b // 2], 16))
            act.wait_ge(vec_tr, 1)
            nc.scalar.activation(vec[:, :], bank(0, 0, KD * NV), ACT.Copy).then_inc(bank_read[0], 1)
            act.wait_ge(bank_read[0], 1)
            norm_upper("n_mix", p_hi)
            hi(0)
            hi(1)
            hi(2)
            squares("n_mem", mem_rows, lambda b: act.wait_ge(mem_in, 16))
            with act.Fori(0, 4) as i:
                hi(G_UGQ + 3, i)
                act.wait_ge(slot_used, G_UGQ + 2 + 3 * i)
                act.wait_ge(glu, i + 1)
                nc.scalar.activation(work[:, 832:1344], bank(1), ACT.Sigmoid).then_inc(bank_read[1], 1)
                hi(G_UGQ + 4, i)
                act.wait_ge(slot_used, G_UGQ + 3 + 3 * i)
                nc.scalar.activation(qreg[:, bass.ds(BW * i, BW)], bank(2), ACT.Copy).then_inc(bank_read[2], 1)
                hi(G_UGQ + 5, i)
            act.wait_ge(vec_tr, 2)
            nc.scalar.activation(cwf[:, :], bank(3, 0, K_F * FT), ACT.Copy).then_inc(bank_read[3], 1)
            norm_upper("n_mem", q_hi)
            for i in range(4):
                act.wait_ge(slot_used, G_KV + i + 1)
                nc.scalar.activation(kreg[:, BW * i:BW * (i + 1)], bank(i), ACT.Copy).then_inc(bank_read[i], 1)
                hi(G_KV + i + 3)
            for i in range(4):
                if i == 3:
                    act.wait_ge(slot_used, G_KV + 8)
                    for b in range(4):
                        nc.scalar.activation(v_tok[:, b // 2, BW * (b % 2):BW * (b % 2) + BW], bank(4 + b),
                                             ACT.Copy).then_inc(bank_read[4 + b], 1)
                hi(G_KV + 7 + i)
            with act.Fori(0, 4) as i:
                act.wait_ge(slot_used, G_CVB + 1 + 3 * i)
                act.wait_ge(bank_read[1], USES["cvb"][1] + i)
                nc.scalar.activation(work[:, 832:1344], bank(0), ACT.Copy).then_inc(bank_read[0], 1)
                hi(G_CVB + 3, i)
                hi(G_CVB + 4, i)
                act.wait_ge(bank_read[2], USES["cvb"][2] + 1 + i)
                nc.scalar.activation(q_hi[:, bass.ds(BW * i, BW)], work[:, 1860:2372], ACT.Copy).then_inc(an_hi, 1)
                hi(G_CVB + 5, i)
            with act.Fori(0, 4) as i:
                for j in range(3):
                    act.wait_ge(slot_used, G_GATE + j + 1 + 3 * i)
                    for b in range(2):
                        last = nc.scalar.activation(
                            gates[:, bass.ds(j * KD * S + BW * i + S * b, S)], bank(j, S * b, S * b + S), ACT.Sigmoid,
                            bias=vec[:, bass.ds(2 * NV * i + b * NV + V_GATE + j, 1)])
                    last.then_inc(bank_read[j], 1)
                    hi(G_GATE + j + 3, i)
            hi(G_AO + 3)
            queries_keys("att1", 0)
            values("att1", 0)
            for i in range(1, 4):
                hi(G_AO + i + 3)
            act.wait_ge(slot_used, G_AO + 4)
            queries_keys("att1", 1)
            queries_keys("att1", 2)
            values("att1", 1)
            act.wait_ge(ln_ctr, 1)
            nc.scalar.activation(ln_sqs, conv, ACT.Square).then_inc(ln_sq, 1)
            attention("att1")
            act.wait_ge(ln_z, 1)
            for c in range(KD):
                nc.scalar.activation(conv[:, c * S:(c + 1) * S], conv[:, c * S:(c + 1) * S], ACT.Silu,
                                     scale=gain(V_LNG, c), bias=gain(V_LNB, c)).then_inc(ln_y, 1)
                if c % 4 == 3:
                    act.wait_ge(ln_y, c + 1)
                    nc.scalar.activation(q_hi[:, 1024 * (c // 4):1024 * (c // 4) + 1024],
                                         conv[:, 1024 * (c // 4):1024 * (c // 4) + 1024], ACT.Copy).then_inc(ln_hi, 1)
                    hi(G_ATT + 3 + c // 4)
            hi(G_ATT + 5)
            hi(G_ATT + 6)
            for i in range(4):
                act.wait_ge(mg, 4 + i + 1)
                nc.scalar.activation(p_hi[:, BW * i:BW * (i + 1)], merged[:, BW * i:BW * (i + 1)],
                                     ACT.Copy).then_inc(mg_hi, 1)
                hi(G_BO + i + 3)
            for i in range(3):
                hi(G_WO + i + 3)

            def after_product(name, phase, dst=None, b0=4):
                squares(name, x, lambda b: act.wait_ge(bank_read[b0 + b], USES[phase][b0 + b] + 1))
                if dst is not None:
                    norm_upper(name, dst)

            after_product("n_ffn", "w_o", p_hi)
            hi(G_WO + 6)

            def last_tap(i, part, b, n):
                act.wait_ge(slot_used, n)
                if part and not isinstance(i, int):
                    act.wait_ge(f_u, i)
                for h in range(2):
                    dst = work[:, BW * part + S * h:BW * part + S * h + S]
                    c = 2 * FT + part * (FT // 2) + 2 * i + h
                    last = nc.scalar.activation(dst, bank(b, S * h, S * h + S), ACT.Copy, scale=cwf[:, bass.ds(c, 1)])
                last.then_inc(f_y, 1)

            def silu_gate(n):
                act.wait_ge(bank_read[0], USES["ffn1"][0] + n)
                nc.scalar.activation(work[:, 1024:1536], work[:, 0:512], ACT.Silu).then_inc(f_s, 1)

            def u_upper(n):
                act.wait_ge(f_u, n)
                nc.scalar.activation(q_hi[:, 0:BW], work[:, 1536:2048], ACT.Copy).then_inc(f_hi, 1)

            last_tap(0, 0, 0, G_FFN1 + 1)
            hi(G_FFN1 + 3)
            last_tap(0, 1, 1, G_FFN1 + 2)
            silu_gate(1)
            hi(G_FFN1 + 4)
            u_upper(1)
            with act.Fori(0, FG - 1) as i:
                last_tap(i + 1, 0, 0, G_FFN1 + 3 + 3 * i)
                hi(G_FFN1 + 5, i)
                last_tap(i + 1, 1, 1, G_FFN1 + 4 + 3 * i)
                silu_gate(i + 2)
                hi(G_FFN1 + 6, i)
                act.wait_ge(slot_used, G_FFN1 + 5 + 3 * i)
                u_upper(i + 2)
                hi(G_FFN1 + 7, i)
            after_product("fin1", "ffn1")
            squares("n_mix2a", x, lambda b: act.wait_ge(fin_x, b // 2 + 1))
            norm_upper("n_mix2a", p_hi)
            hi(G_EV + 2)
            for i in range(7):
                hi(G_EV + i + 3)
            act.wait_ge(slot_used, G_EV + 8)
            for b in (5, 2):
                nc.scalar.activation(z[:, b // 3, 480 * (b % 3):480 * (b % 3) + 480], bank(b, 0, 480),
                                     ACT.Copy).then_inc(bank_read[b], 1)
            for b in (1, 2, 4, 5):
                act.wait_ge(bank_read[b], USES["ev_in"][b] + 1)
            for t in range(T):
                nc.scalar.activation(misc[:, 1920 * t:1920 * t + 384], z[:, t, Z_CQ:Z_CKV], ACT.Square,
                                     accum_out=lat[:, t:t + 1])
                last = nc.scalar.activation(misc[:, 1920 * t + 384:1920 * t + 640], z[:, t, Z_CKV:Z_KR], ACT.Square,
                                            accum_out=lat[:, 2 + t:3 + t])
            last.then_inc(l_sq, 1)
            for b in (0, 3):
                act.wait_ge(bank_read[b], USES["ev_in"][b] + 1)
            for t in range(T):
                nc.scalar.activation(misc[:, 640 + 640 * t:1280 + 640 * t], z[:, t, 0:Z_V],
                                     ACT.Square).then_inc(h_sq, 1)
            act.wait_ge(l_r, 1)
            nc.scalar.activation(z[:, 0, Z_CQ:Z_CKV], z[:, 0, Z_CQ:Z_CKV], ACT.Copy, scale=lat[:, 0:1])
            nc.scalar.activation(z[:, 0, Z_CKV:Z_KR], z[:, 0, Z_CKV:Z_KR], ACT.Copy, scale=lat[:, 2:3]).then_inc(l_x, 1)
            hi(G_EV + 10)
            act.wait_ge(l_tr, 1)
            for c in range(5):
                nc.scalar.activation(p_hi[:, c * S:(c + 1) * S], bank(c // 2, c % 2 * S, c % 2 * S + S), ACT.Copy,
                                     scale=gain(V_LAT, c)).then_inc(l_hi, 1)
            hi(G_UQ + 3)
            act.wait_ge(slot_used, G_UQ + 3)
            for b in range(4):
                nc.scalar.activation(qb[:, b // 2, 384 * (b % 2):384 * (b % 2) + 384], bank(b, 0, 384),
                                     ACT.Copy).then_inc(bank_read[b], 1)
            hi(G_UQ + 4)
            hi(G_UQ + 5)
            act.wait_ge(slot_used, G_UKV + 1)
            for b in range(4):
                nc.scalar.activation(kvb[:, b // 2, BW * (b % 2):BW * (b % 2) + BW], bank(4 + b),
                                     ACT.Copy).then_inc(bank_read[4 + b], 1)
            hi(G_UQ + 6)
            for i in range(11):
                act.wait_ge(ev_tr, i + 1)
                n, b = BW, i % 4
                if i < 2:
                    dst = qT_a[:, BW * i:BW * i + BW]
                elif i == 2:
                    dst, n = kT_a, S
                else:
                    reg = kreg if i < 7 else vreg
                    dst = reg[0:B_QK, BW * ((i - 3) % 4):BW * ((i - 3) % 4) + BW]
                src = ps[0:B_QK, b, :] if i > 2 else bank(b, 0, n)
                nc.scalar.activation(dst, src, ACT.Copy).then_inc(bank_read[b], 1)
                if i == 2:
                    zeros_beside_values((q_hi, q_lo, p_hi, p_lo))
                    for b in range(3):
                        act.wait_ge(bank_read[b], USES["ev_tr"][b] + 1)
                    queries_keys("att2", 0)
                    queries_keys("att2", 1)
            attention("att2")
            for i in range(3):
                hi(G_EVO + i + 3)
            after_product("n_ffn2a", "ev_out", p_hi, 0)
            hi(G_EVO + 6)

            def group(k, n, slot, up, i=0):
                act.wait_ge(slot_used, up + 1 + 6 * i)
                if FP * k + n > 0:
                    act.wait_ge(f2_sq, FP * k + n + 3 * i)
                nc.scalar.activation(work[:, 0:BW], bank(slot), ACT.Relu).then_inc(f2_r, 1)
                hi(up + 3, 2 * i)
                act.wait_ge(f2_sq, FP * k + n + 1 + 3 * i)
                nc.scalar.activation(q_hi[:, BW * slot:BW * slot + BW], work[:, 1024:1536], ACT.Copy).then_inc(f2_hi, 1)

            def ffn2(k, g0):
                group(k, 0, 0, g0)

                def three(i):
                    for j in range(3):
                        group(k, 1 + j, (1 + j) % 3, g0 + 1 + 2 * j, i)
                        hi(g0 + 5 + 2 * j, 2 * i)

                with act.Fori(0, (FP - 1) // 3 - 1) as i:
                    three(i)
                three((FP - 1) // 3 - 1)

            ffn2(0, G_F2A)
            after_product("n_mix2b", "ffn2a", p_hi)
            hi(G_QK + 2)
            for i in range(8):
                act.wait_ge(slot_used, G_QK + i + 1)
                reg = qreg if i < 4 else kreg
                nc.scalar.activation(reg[:, BW * (i % 4):BW * (i % 4) + BW], bank(i % 4), ACT.Copy,
                                     scale=HD ** -0.5 if i < 4 else 1.0)\
                    .then_inc(bank_read[i % 4], 1)
                hi(G_QK + i + 3)
            zeros_beside_values((q_hi, q_lo))
            for b in range(4):
                act.wait_ge(bank_read[b], USES["qk"][b] + 2)
            queries_keys("att3", 0)
            for i in range(3):
                hi(G_V + i + 3)

            def after_values():
                act.wait_ge(slot_used, G_V + 4)
                queries_keys("att3", 1)
                for b in range(4):
                    nc.scalar.activation(v_tok[:, b // 2, BW * (b % 2):BW * (b % 2) + BW], bank(4 + b),
                                         ACT.Copy).then_inc(bank_read[4 + b], 1)
                zeros_beside_values((p_hi, p_lo))
                for b in range(4, 8):
                    act.wait_ge(bank_read[b], USES["v"][b] + 1)

            attention("att3", after_values)
            hi(G_V + 6)
            for i in range(3):
                hi(G_ODO + i + 3)
            after_product("n_ffn2b", "od_out", p_hi, 0)
            hi(G_ODO + 6)
            ffn2(1, G_F2B)
            after_product("fin2", "ffn2b")

        @block.vector
        def _(dve):
            def lo(g, i=0):
                if isinstance(i, int):
                    g, i = g + R * i, 0
                    if g >= G_END:
                        return
                dve.wait_ge(hi_ready, g + 1 + R * i)
                nc.vector.tensor_tensor(wlo[:, g % R, :], raw[:, g % R, :], whi[:, g % R, :].bitcast(F32),
                                        ALU.subtract).then_inc(lo_ready, 1)

            def mean_square(n, t):
                c = T * n + t
                dve.wait_ge(norm_sq, c + 1)
                nc.vector.tensor_tensor(sm[:, c:c + 1], ss[:, c, 0:1], ss[:, c, 1:2], ALU.add).then_inc(norm_sum, 1)
                dve.wait_ge(norm_sum, c + 1)
                nc.vector.tensor_scalar(ms[:, c:c + 1], sm[:, c:c + 1], 1.0 / D, EPS, ALU.mult,
                                        ALU.add).then_inc(norm_ms, 1)

            def normalise(name, src, with_stats=True):
                n, m = NORMS.index(name), TNORMS.index(name)
                for t in range(T):
                    if with_stats:
                        mean_square(n, t)
                for t in range(T):
                    dve.wait_ge(norm_r, T * n + t + 1)
                    nc.vector.tensor_scalar(xn[:, t, :], src[:, t, :], rr[:, T * n + t:T * n + t + 1], None,
                                            ALU.mult).then_inc(norm_xn, 1)

            def norm_lower(name, hi_part, lo_part):
                m = TNORMS.index(name)
                for c in range(KD):
                    dve.wait_ge(norm_hi, KD * m + c // 2 * 2 + 2)
                    last = nc.vector.scalar_tensor_tensor(
                        out=lo_part[:, c * S:(c + 1) * S], in0=bank(c // 2, c % 2 * S, c % 2 * S + S),
                        scalar=gain(TGAIN[m], c), in1=hi_part[:, c * S:(c + 1) * S].bitcast(F32),
                        op0=ALU.mult, op1=ALU.subtract)
                    if c % 2:
                        last.then_inc(bank_read[c // 2], 1)

            def residual(name, k, g_end, b0=4):
                dve.wait_ge(rows_done, k + 1)
                for b in range(4):
                    if b == 2:
                        mean_square(NORMS.index(name), 0)
                        dve.wait_ge(slot_used, g_end)
                    rows = x[:, b // 2, BW * (b % 2):BW * (b % 2) + BW]
                    nc.vector.tensor_tensor(rows, rows, bank(b0 + b), ALU.add).then_inc(bank_read[b0 + b], 1)
                mean_square(NORMS.index(name), 1)

            def residual_norm(name, k, g_end, b0=4):
                residual(name, k, g_end, b0)
                normalise(name, x, False)
                norm_lower(name, p_hi, p_lo)

            def attention(name):
                units, H, u0, n0, scale, biased, k = ATT[name]
                N = H * len(units)

                if name == "att3":
                    dve.wait_ge(bias_step, 5 * C_HEADS)
                for i in range(N + 3):
                    n = n0 + i
                    if i < N:
                        dve.wait_ge(at_s, n + 1)
                        both = ps[:, i % 2, :].rearrange("p (t n) -> p t n", t=T)
                        pair = slice(2 * (i % 2), 2 * (i % 2) + 2)
                        if biased:
                            for t in range(T):
                                last = nc.vector.tensor_tensor_reduce(
                                    out=bsc[:, i % 2, t, :], in0=both[:, t, :],
                                    in1=bias[:, i, 2 - 2 * t:6 - 2 * t, :].rearrange("p j k -> p (j k)"),
                                    scale=1.0, scalar=NEG, op0=ALU.add, op1=ALU.max,
                                    accum_out=att_max[:, 2 * (i % 2) + t:2 * (i % 2) + t + 1])
                            last.then_inc(at_max, 1)
                        else:
                            nc.vector.tensor_reduce(out=att_max[:, pair], in_=both, axis=AX.X, op=ALU.max)\
                                .then_inc(at_max, 1)
                        dve.wait_ge(at_max, n + 1)
                        nc.vector.tensor_scalar(att_nmax[:, pair], att_max[:, pair],
                                                -1.0 if biased else -scale(i), None, ALU.mult).then_inc(at_nm, 1)
                    if 1 <= i <= N:
                        dve.wait_ge(at_e, n)
                        sums = att_sum.rearrange("p (t h) -> p t h", t=T)[:, :, i - 1:i]
                        inv = att_rs.rearrange("p (t h) -> p t h", t=T)[:, :, i - 1:i]
                        nc.vector.reciprocal(inv, sums).then_inc(at_rs, 1)
                        dve.wait_ge(at_rs, n)
                        for t in range(T):
                            rows = prob[:, (i - 1) % 3, t, :]
                            last = nc.vector.tensor_scalar(rows, rows, att_rs[:, 16 * t + i - 1:16 * t + i], None,
                                                           ALU.mult)
                        last.then_inc(at_p, 1)
                    if i >= 3:
                        b = (i - 3) % 2
                        dve.wait_ge(at_h, n - 2)
                        nc.vector.tensor_tensor(unit_lo[b][:, PT], bank(2 + b), unit_hi[b][:, PT].bitcast(F32),
                                                ALU.subtract).then_inc(bank_read[2 + b], 1)
                    if name == "att1":
                        layer_norm_scales(i)
                for b in range(4):
                    dve.wait_ge(o_hi, 4 * k + b + 1)
                    nc.vector.tensor_tensor(p_lo[:, BW * b:BW * (b + 1)], bank(4 + b),
                                            p_hi[:, BW * b:BW * (b + 1)].bitcast(F32),
                                            ALU.subtract).then_inc(bank_read[4 + b], 1)

            normalise("n_mix", x)
            norm_lower("n_mix", p_hi, p_lo)
            lo(0)
            lo(1)
            lo(2)

            acc = [work[:, 320:576], work[:, 576:832]]
            TAPS = K_B + 3

            def conv_part(c, base, part, glu_at):
                if part == 0:
                    dve.wait_ge(glu, glu_at)
                    nc.vector.tensor_copy(work[:, 0:UP], misc[:, bass.ds(c * UP, UP)]).then_inc(conv_tap, 1)
                    nc.vector.tensor_copy(work[:, UP:UP + K_B], vec[:, bass.ds(c * NV + V_CONVB, K_B)])\
                        .then_inc(conv_tap, 1)
                    dve.wait_ge(conv_tap, base + 2)
                for k in (range(0, 8), range(8, 16), range(16, 24), range(24, K_B))[part]:
                    src, w = work[:, k:k + S], work[:, UP + k:UP + k + 1]
                    if k < 2:
                        nc.vector.tensor_scalar(acc[k], src, w, None, ALU.mult).then_inc(conv_tap, 1)
                    else:
                        dve.wait_ge(conv_tap, base + k + 1)
                        nc.vector.scalar_tensor_tensor(out=acc[k % 2], in0=src, scalar=w, in1=acc[k % 2],
                                                       op0=ALU.mult, op1=ALU.add).then_inc(conv_tap, 1)
                if part == 3:
                    dve.wait_ge(conv_tap, base + TAPS - 1)
                    nc.vector.scalar_tensor_tensor(
                        out=conv[:, bass.ds(c * S, S)], in0=acc[0], scalar=vec[:, bass.ds(c * NV + V_CBIAS, 1)],
                        in1=acc[1], op0=ALU.add, op1=ALU.add).then_inc(conv_tap, 1)

            def ugq(i, parts=()):
                lo(G_UGQ + 3, i)
                dve.wait_ge(bank_read[1], USES["ugq"][1] + 1 + i)
                sig = work[:, 832:1344].rearrange("p (b n) -> p b n", b=2)
                dst = misc[:, bass.ds(2 * UP * i, 2 * UP)].rearrange("p (b n) -> p b n", b=2)[:, :, K_B - 1:UP]
                nc.vector.tensor_tensor(dst, ps[:, 0, :].rearrange("p (b n) -> p b n", b=2), sig,
                                        ALU.mult).then_inc(glu, 1)
                lo(G_UGQ + 4, i)
                for part in parts[:1]:
                    conv_part(0, 0, part, 2)
                lo(G_UGQ + 5, i)
                for part in parts[1:]:
                    conv_part(0, 0, part, 2)

            ugq(0)
            normalise("n_mem", mem_rows)
            ugq(1, (0, 1))
            ugq(2, (2, 3))
            ugq(3)
            norm_lower("n_mem", q_hi, q_lo)
            for i in range(8):
                lo(G_KV + 3 + i)
                conv_part(1 + i // 4, TAPS * (1 + i // 4), i % 4, 3)
            gcv = work[:, 1344:1860].rearrange("p (b n) -> p b n", b=2)
            ca = work[:, 1860:2372]

            def branch_a(i):
                dve.wait_ge(bank_read[0], USES["cvb"][0] + 1 + i)
                dve.wait_ge(slot_used, G_CVB + 2 + 3 * i)
                nc.vector.tensor_tensor(gcv[:, :, K_A - 1:K_A - 1 + S], ps[:, 1, :].rearrange("p (b n) -> p b n", b=2),
                                        work[:, 832:1344].rearrange("p (b n) -> p b n", b=2),
                                        ALU.mult).then_inc(bank_read[1], 1)
                lo(G_CVB + 3, i)
                dve.wait_ge(bank_read[1], USES["cvb"][1] + 1 + i)
                for m in range(2 * K_A):
                    b, k = m % 2, K_A - 1 - m // 2
                    src = gcv[:, b, k:k + S]
                    w = vec[:, bass.ds(2 * NV * i + b * NV + V_CONVA + k, 1)]
                    dst = ca[:, b * S:(b + 1) * S]
                    if m < 2:
                        nc.vector.tensor_scalar(dst, src, w, None, ALU.mult).then_inc(ca_step, 1)
                    else:
                        dve.wait_ge(ca_step, 2 * K_A * i + m)
                        nc.vector.scalar_tensor_tensor(out=dst, in0=src, scalar=w, in1=dst, op0=ALU.mult,
                                                       op1=ALU.add).then_inc(ca_step, 1)
                lo(G_CVB + 4, i)
                dve.wait_ge(slot_used, G_CVB + 3 + 3 * i)
                dve.wait_ge(ca_step, 2 * K_A * i + 2 * K_A + 1)
                nc.vector.tensor_tensor(ca, bank(2), ca, ALU.mult).then_inc(bank_read[2], 1)
                lo(G_CVB + 5, i)
                dve.wait_ge(an_hi, i + 1)
                nc.vector.tensor_tensor(q_lo[:, bass.ds(BW * i, BW)], ca, q_hi[:, bass.ds(BW * i, BW)].bitcast(F32),
                                        ALU.subtract).then_inc(an_lo, 1)

            for i in range(4):
                branch_a(i)
                conv_part(3, 3 * TAPS, i, 3)
            for i in range(4):
                for j in range(3):
                    lo(G_GATE + 3 + j, i)
                    if j:
                        c = 4 + i // 2
                        conv_part(c, c * TAPS, 2 * (i % 2) + j - 1, 4)
            conv_t = conv.rearrange("p (c n) -> p c n", c=KD)

            def gate_of(j, i):
                return gates[:, j * KD * S + BW * i:j * KD * S + BW * (i + 1)]

            for i in range(4):
                dve.wait_ge(slot_used, G_AO + i + 1)
                nc.vector.tensor_tensor(merged[:, BW * i:BW * (i + 1)], bank(i), gate_of(0, i),
                                        ALU.mult).then_inc(bank_read[i], 1)
                lo(G_AO + i + 3)
            dve.wait_ge(ln_mean, 1)
            nc.vector.tensor_tensor(conv_t, conv_t, bank(7, 0, S).unsqueeze(1).to_broadcast([P, KD, S]),
                                    ALU.subtract).then_inc(ln_ctr, 1)

            def layer_norm_scales(i):
                if i == 3:
                    dve.wait_ge(ln_var, 1)
                    nc.vector.tensor_scalar(ln_v, bank(7, 0, T), EPS, None, ALU.add).then_inc(ln_ms, 1)
                elif i == 4:
                    dve.wait_ge(ln_r, 1)
                    for t in range(T):
                        last = nc.vector.tensor_scalar(ln_diag[:, P * t:P * t + P], ident[:, :], ln_rs[:, t:t + 1],
                                                       float(D), ALU.mult, ALU.mult)
                    last.then_inc(ln_dg, 1)

            attention("att1")
            dve.wait_ge(ln_bc, 1)
            nc.vector.tensor_tensor(conv_t, conv_t, bank(3, 0, S).unsqueeze(1).to_broadcast([P, KD, S]),
                                    ALU.mult).then_inc(ln_z, 1)
            lo(G_ATT + 3)

            def merge(j, g0, count, between):
                for i in range(4):
                    dve.wait_ge(slot_used, g0 + i + 1)
                    nc.vector.tensor_tensor(gate_of(j, i), bank(i), gate_of(j, i), ALU.mult).then_inc(bank_read[i], 1)
                    dve.wait_ge(bank_read[i], USES[count][i] + 1)
                    nc.vector.tensor_tensor(merged[:, BW * i:BW * (i + 1)], merged[:, BW * i:BW * (i + 1)],
                                            gate_of(j, i), ALU.add).then_inc(mg, 1)
                    between(i)

            def during_att_out(i):
                if i:
                    lo(G_ATT + 3 + i)
                if i < 2:
                    dve.wait_ge(ln_hi, i + 1)
                    half = slice(1024 * i, 1024 * (i + 1))
                    nc.vector.tensor_tensor(q_lo[:, half], conv[:, half], q_hi[:, half].bitcast(F32),
                                            ALU.subtract).then_inc(ln_lo, 1)

            def merged_lower(i):
                dve.wait_ge(mg_hi, i + 1)
                nc.vector.tensor_tensor(p_lo[:, BW * i:BW * (i + 1)], merged[:, BW * i:BW * (i + 1)],
                                        p_hi[:, BW * i:BW * (i + 1)].bitcast(F32), ALU.subtract).then_inc(mg_lo, 1)

            def during_b_out(i):
                if i:
                    merged_lower(i - 1)
                if i == 3:
                    merged_lower(3)
                lo(G_BO + i + 3)

            merge(2, G_ATT, "att_out", during_att_out)
            merge(1, G_BO, "b_out", during_b_out)
            for i in range(3):
                lo(G_WO + i + 3)
            residual_norm("n_ffn", 0, G_WO + 4)
            lo(G_WO + 6)

            def other_taps(i, part, n):
                dve.wait_ge(f_y, n + 1)
                for m in range(4):
                    h, k = m % 2, 1 - m // 2
                    back = K_F - 1 - k
                    dst = work[:, BW * part + S * h + back:BW * part + S * h + S]
                    w = cwf[:, bass.ds(k * FT + part * (FT // 2) + 2 * i + h, 1)]
                    if k == 0:
                        dve.wait_ge(f_c, 2 * n + h + 1)
                    last = nc.vector.scalar_tensor_tensor(out=dst, in0=bank(part, S * h, S * h + S - back), scalar=w,
                                                          in1=dst, op0=ALU.mult, op1=ALU.add)
                    if k == 1:
                        last.then_inc(f_c, 1)
                last.then_inc(bank_read[part], 1)

            def gated(n):
                dve.wait_ge(f_s, n + 1)
                dve.wait_ge(bank_read[1], USES["ffn1"][1] + n + 1)
                nc.vector.tensor_tensor(work[:, 1536:2048], work[:, 1024:1536], work[:, 512:1024],
                                        ALU.mult).then_inc(f_u, 1)

            def u_lower(n):
                dve.wait_ge(f_hi, n + 1)
                nc.vector.tensor_tensor(q_lo[:, 0:BW], work[:, 1536:2048], q_hi[:, 0:BW].bitcast(F32),
                                        ALU.subtract).then_inc(f_lo, 1)

            other_taps(0, 0, 0)
            lo(G_FFN1 + 3)
            other_taps(0, 1, 1)
            gated(0)
            lo(G_FFN1 + 4)
            u_lower(0)
            with dve.Fori(0, FG - 1) as i:
                other_taps(i + 1, 0, 2 * i + 2)
                lo(G_FFN1 + 5, i)
                other_taps(i + 1, 1, 2 * i + 3)
                gated(i + 1)
                lo(G_FFN1 + 6, i)
                u_lower(i + 1)
                lo(G_FFN1 + 7, i)
            def final_norm(name, k):
                n = NORMS.index(name)
                dve.wait_ge(gain_in, 16 * (k + 1))
                for t in range(T):
                    dve.wait_ge(norm_r, T * n + t + 1)
                    nc.vector.scalar_tensor_tensor(out=x[:, t, :], in0=x[:, t, :], scalar=rr[:, 2 * n + t:2 * n + t + 1],
                                                   in1=gfin, op0=ALU.mult, op1=ALU.mult).then_inc(fin_x, 1)

            residual("fin1", 1, G_EV)
            final_norm("fin1", 0)
            dve.wait_ge(fin_x, 2)
            normalise("n_mix2a", x)
            norm_lower("n_mix2a", p_hi, p_lo)
            lo(G_EV + 2)
            for i in range(7):
                lo(G_EV + i + 3)
            dve.wait_ge(slot_used, G_EV + 8)
            for b in (4, 1, 3, 0):
                nc.vector.tensor_copy(z[:, b // 3, 480 * (b % 3):480 * (b % 3) + 480], bank(b, 0, 480))\
                    .then_inc(bank_read[b], 1)
            dve.wait_ge(l_sq, 1)
            nc.vector.tensor_scalar(lat[:, 0:2], lat[:, 0:2], 1.0 / B_Q_RANK, EPS, ALU.mult, ALU.add)
            nc.vector.tensor_scalar(lat[:, 2:4], lat[:, 2:4], 1.0 / B_KV_RANK, EPS, ALU.mult, ALU.add).then_inc(l_ms, 1)
            NH = A_HEADS + A_KV
            dve.wait_ge(l_r, 1)
            for cols, r in ((slice(Z_CQ, Z_CKV), lat[:, 1:2]), (slice(Z_CKV, Z_KR), lat[:, 3:4])):
                last = nc.vector.tensor_scalar(z[:, 1, cols], z[:, 1, cols], r, None, ALU.mult)
            last.then_inc(l_x, 1)
            dve.wait_ge(h_sq, 2)
            nc.vector.tensor_reduce(out=hss, in_=misc[:, 640:1920].rearrange("p (h n) -> p h n", n=HD), axis=AX.X,
                                    op=ALU.add).then_inc(h_ss, 1)
            dve.wait_ge(h_ss, 1)
            nc.vector.tensor_scalar(hss, hss, 1.0 / HD, EPS, ALU.mult, ALU.add).then_inc(h_ms, 1)
            lo(G_EV + 10)
            for c in range(5):
                dve.wait_ge(l_hi, min(c // 2 * 2 + 2, 5))
                last = nc.vector.scalar_tensor_tensor(
                    out=p_lo[:, c * S:(c + 1) * S], in0=bank(c // 2, c % 2 * S, c % 2 * S + S), scalar=gain(V_LAT, c),
                    in1=p_hi[:, c * S:(c + 1) * S].bitcast(F32), op0=ALU.mult, op1=ALU.subtract)
                if c in (1, 3, 4):
                    last.then_inc(bank_read[c // 2], 1)

            dve.wait_ge(h_r, 1)
            dve.wait_ge(rope_in, 48)
            for t in range(T):
                heads = z[:, t, 0:Z_V].rearrange("p (h n) -> p h n", h=NH)
                nc.vector.tensor_tensor(heads, heads, hr[:, NH * t:NH * t + NH].unsqueeze(2).to_broadcast([P, NH, HD]),
                                        ALU.mult).then_inc(h_n, 1)
            dve.wait_ge(h_n, 2)
            for t in range(T):
                for h0, nh, g in ((0, A_HEADS, gq), (A_HEADS, A_KV, gk)):
                    part = z[:, t, HD * h0:HD * (h0 + nh)].rearrange("p (h n) -> p h n", h=nh)
                    nc.vector.tensor_tensor(part, part, g.unsqueeze(1).to_broadcast([P, nh, HD]),
                                            ALU.mult).then_inc(h_n, 1)
            lo(G_UQ + 3)
            dve.wait_ge(h_n, 6)

            def rotate(part, nh, width, cos, sin, m1, m2, step, done, free=0, pairs=None):
                if free:
                    dve.wait_ge(done, free)
                one = m1.rearrange("p (h n) -> p h n", h=nh)
                nc.vector.tensor_tensor(one, part, cos.unsqueeze(1).to_broadcast([P, nh, width]), ALU.mult)
                two = m2.rearrange("p (h n) -> p h n", h=nh)

                def side(a, s):
                    return a.rearrange("p h (r s n) -> p h r s n", r=2, s=2)[:, :, :, s, :]

                sin_b = sin.unsqueeze(1).to_broadcast([P, nh, width])
                nc.vector.tensor_tensor(side(two, 0), side(part, 1), side(sin_b, 0), ALU.mult)
                nc.vector.tensor_tensor(side(two, 1), side(part, 0), side(sin_b, 1), ALU.mult).then_inc(step[0], 1)
                dve.wait_ge(step[0], step[1])
                if nh == NH:
                    def by_pair(a):
                        return a[:, 0:A_HEADS, :].rearrange("p (v h) n -> p v h n", v=A_KV)

                    nc.vector.tensor_tensor(pairs.rearrange("p (h v n) -> p v h n", h=A_HEADS // A_KV, v=A_KV),
                                            by_pair(one), by_pair(two), ALU.add)
                    part, one, two = part[:, A_HEADS:NH, :], one[:, A_HEADS:NH, :], two[:, A_HEADS:NH, :]
                nc.vector.tensor_tensor(part, one, two, ALU.add).then_inc(done, 1)

            for t in range(T):
                rotate(z[:, t, 0:Z_V].rearrange("p (h n) -> p h n", h=NH), NH, HD, rope[:, t, 0:64],
                       rope[:, t, 64:128], misc[:, 0:640], misc[:, 640:1280], (h_n, 7 + t), rope_a,
                       t, qrot[:, t, :])
            for t in range(T):
                rotate(z[:, t, Z_KR:EV_IN].unsqueeze(1), 1, B_ROPE, rope[:, t, 128:160], rope[:, t, 160:192],
                       misc[:, 1280:1312], misc[:, 1312:1344], (h_n, 9 + t), rope_a, 3 * t)
            for b in range(4):
                dve.wait_ge(bank_read[b], USES["uq"][b] + 1)
            for t in range(T):
                rotate(qb[:, t, :].rearrange("p (h n) -> p h n", h=B_HEADS)[:, :, B_NOPE:B_QK], B_HEADS, B_ROPE,
                       rope[:, t, 128:160], rope[:, t, 160:192], misc[:, 0:256], misc[:, 256:512],
                       (h_n, 11 + t), rope_b, t)
            dve.wait_ge(rope_a, 4)
            for t in range(T):
                keys = kf[:, t, :].rearrange("p (h n) -> p h n", h=B_HEADS)
                nc.vector.tensor_copy(keys[:, :, B_NOPE:B_QK],
                                      z[:, t, Z_KR:EV_IN].unsqueeze(1).to_broadcast([P, B_HEADS, B_ROPE]))
            for b in range(4, 8):
                dve.wait_ge(bank_read[b], USES["ukv"][b] + 1)
            for t in range(T):
                keys = kf[:, t, :].rearrange("p (h n) -> p h n", h=B_HEADS)
                nc.vector.tensor_copy(keys[:, :, 0:B_NOPE],
                                      kvb[:, t, :].rearrange("p (h n) -> p h n", h=B_HEADS)[:, :, 0:B_NOPE])\
                    .then_inc(rope_b, 1)
            for i in range(1, 4):
                lo(G_UQ + i + 3)
            attention("att2")
            for i in range(3):
                lo(G_EVO + i + 3)
            residual_norm("n_ffn2a", 2, G_EVO + 4, 0)
            lo(G_EVO + 6)

            def group(k, n, slot, up, i=0):
                dve.wait_ge(f2_r, FP * k + n + 1 + 3 * i)
                if FP * k + n > 0:
                    dve.wait_ge(f2_lo, FP * k + n + 3 * i)
                nc.vector.tensor_tensor(work[:, 1024:1536], work[:, 0:BW], work[:, 0:BW], ALU.mult).then_inc(f2_sq, 1)
                lo(up + 3, 2 * i)
                dve.wait_ge(f2_hi, FP * k + n + 1 + 3 * i)
                nc.vector.tensor_tensor(q_lo[:, BW * slot:BW * slot + BW], work[:, 1024:1536],
                                        q_hi[:, BW * slot:BW * slot + BW].bitcast(F32), ALU.subtract).then_inc(f2_lo, 1)

            def ffn2(k, g0):
                group(k, 0, 0, g0)

                def three(i):
                    for j in range(3):
                        group(k, 1 + j, (1 + j) % 3, g0 + 1 + 2 * j, i)
                        lo(g0 + 5 + 2 * j, 2 * i)

                with dve.Fori(0, (FP - 1) // 3 - 1) as i:
                    three(i)
                three((FP - 1) // 3 - 1)

            ffn2(0, G_F2A)
            residual_norm("n_mix2b", 3, G_QK)
            lo(G_QK + 2)
            for i in range(8):
                lo(G_QK + i + 3)
            for i in range(3):
                lo(G_V + i + 3)
            attention("att3")
            lo(G_V + 6)
            for i in range(3):
                lo(G_ODO + i + 3)
            residual_norm("n_ffn2b", 4, G_ODO + 4, 0)
            lo(G_ODO + 6)
            ffn2(1, G_F2B)
            residual("fin2", 5, G_END)
            final_norm("fin2", 1)

        @block.tensor
        def _(pe):
            def three_passes(dst, w_at, x_at, weights_first, first, last):
                (wh, wl), (xh, xl) = w_at, x_at
                for n, (w, a) in enumerate(((wh, xh), (wh, xl), (wl, xh))):
                    lhs, rhs = (w, a) if weights_first else (a, w)
                    ins = nc.tensor.matmul(dst, lhs, rhs, start=first and n == 0, stop=last and n == 2)
                return ins

            def to_channels(g, b, pair, i=0, after=None, low=0):
                pe.wait_ge(lo_ready, g + 1 + R * i)
                r = g % R
                for h in range(2):
                    for k in range(KD):
                        if after and h == 0 and k % 2 == 0:
                            free(low + k // 2, USES[after][low + k // 2] + 1)
                        at = slice(256 * k + P * h, 256 * k + P * h + P)
                        ins = three_passes(bank(b, S * h, S * h + S), (whi[:, r, at], wlo[:, r, at]),
                                           [a[:, S * k:S * k + S] for a in pair], True, k == 0, k == KD - 1)
                ins.then_inc(slot_used, 1)

            def to_rows(g, tiles, pair, k0, b0, nb, n, first, last, i=0, signal=False):
                pe.wait_ge(lo_ready, g + 1 + R * i)
                r = g % R
                for t in range(T):
                    for k in range(tiles):
                        at = S * (k0 + k) + P * t
                        for m in range(nb):
                            c0 = k * nb * n + m * n
                            ins = three_passes(bank(b0 + nb * t + m, 0, n), (whi[:, r, c0:c0 + n], wlo[:, r, c0:c0 + n]),
                                               [a[:, at:at + P] for a in pair], False,
                                               first and k == 0, last and k == tiles - 1)
                    if signal and t == 0:
                        ins.then_inc(rows_done, 1)
                ins.then_inc(slot_used, 1)

            def free(b, n):
                if n > 0:
                    pe.wait_ge(bank_read[b], n)

            def transpose_norm(name):
                m = TNORMS.index(name)
                for b in range(4):
                    free(b, USES[name][b])
                for t in range(T):
                    pe.wait_ge(norm_xn, T * m + t + 1)
                    for c in range(KD):
                        last = nc.tensor.transpose(bank(c // 2, c % 2 * S + P * t, c % 2 * S + P * t + P),
                                                   xn[:, t, P * c:P * c + P], ident[:, :])
                        if t == T - 1 and c % 2:
                            last.then_inc(norm_tr, 1)

            def ready_low(phase):
                for b in range(4):
                    free(b, USES[phase][b] + 1)

            def parts_product(dst, left, right, first, last):
                (lh, ll), (rh, rl) = left, right
                for n, (a, b) in enumerate(((lh, rh), (lh, rl), (ll, rh))):
                    ins = nc.tensor.matmul(dst, a, b, start=first and n == 0, stop=last and n == 2)
                return ins

            def scores(name, i):
                units, H, u0, n0, scale, biased, k = ATT[name]
                u, h = i // H, i % H
                pe.wait_ge(qk_lo, u0 + u + 1)
                if i < 2:
                    free(i, USES[name][i])
                else:
                    pe.wait_ge(at_max if biased else at_e, n0 + i - 1)
                parts = unit_sides(u, H)
                rows, chunks = units[u]["rows"][h], units[u]["chunks"][h]
                for t in range(T):
                    for j, (q0, k0) in enumerate(chunks):
                        q0, k0 = UNIT_Q + q0 + P * t, UNIT_K + k0
                        ins = parts_product(bank(i % 2, S * t, S * t + S), [a[rows, q0:q0 + P] for a in parts],
                                            [a[rows, k0:k0 + S] for a in parts], j == 0, j == len(chunks) - 1)
                ins.then_inc(at_s, 1)

            def attention(name):
                units, H, u0, n0, scale, biased, k = ATT[name]
                N = H * len(units)
                for i in range(2, N + 4):
                    n = n0 + i
                    if i < N:
                        scores(name, i)
                    if 2 <= i < N + 2:
                        b = 2 + i % 2
                        free(b, USES[name][b] + (i - 2) // 2)
                        pe.wait_ge(at_p, n - 1)
                        for m in range(2):
                            for t in range(T):
                                ins = nc.tensor.transpose(bank(b, S * m + P * t, S * m + P * t + P),
                                                          prob[:, (i - 2) % 3, t, P * m:P * m + P], ident[:, :])
                        ins.then_inc(at_t, 1)
                    if i >= 4:
                        v, b = i - 4, 2 + i % 2
                        u, h = v // H, v % H
                        if i == 4:
                            if H == 2:
                                pe.wait_ge(v_zero, 4 * k)
                            for high in range(4, 8):
                                free(high, USES[name][high])
                        pe.wait_ge(v_lo, u0 + u + 1)
                        free(b, USES[name][b] + v // 2 + 1)
                        if name == "att1" and v == MEM_HEADS - 1:
                            pe.wait_ge(ln_ms, 1)
                        for j in range(2 // H):
                            at = S * (2 * u + j) if H == 1 else S * u
                            for m in range(2):
                                v0 = UNIT_V + S * m + (P * j if H == 1 else HD * h)
                                p0 = UNIT + S * m
                                ins = parts_product(
                                    bank(4 + at // BW, at % BW, at % BW + S),
                                    [a[:, v0:v0 + P] for a in unit_sides(u, H)],
                                    [a[v % 2][:, p0:p0 + S] for a in (unit_hi, unit_lo)],
                                    h == 0 and m == 0, h == H - 1 and m == 1)
                        ins.then_inc(at_v, 1)
                    if name == "att1" and i == 2:
                        pe.wait_ge(ln_sq, 1)
                        for t in range(T):
                            for c in range(KD):
                                last = nc.tensor.matmul(bank(7, t, t + 1), ln_sqs[:, S * c + P * t:S * c + P * t + P],
                                                        mean_w[:, 0:1], start=c == 0, stop=c == KD - 1)
                        last.then_inc(ln_var, 1)

            p_pair, q_pair = (p_hi, p_lo), (q_hi, q_lo)

            pe.wait_ge(const_ready, 2)
            pe.wait_ge(vec_in, 16)
            for c in range(KD):
                last = nc.tensor.transpose(bank(0, NV * c, NV * (c + 1)), vec_rows[:, P * c:P * c + P],
                                           ident[0:NV, 0:NV])
            last.then_inc(vec_tr, 1)
            transpose_norm("n_mix")
            phases = (("ugq", G_UGQ), ("cvb", G_CVB), ("gate", G_GATE))

            def memory():
                pe.wait_ge(cwf_in, 16)
                for k in range(K_F):
                    last = nc.tensor.transpose(bank(3, FT * k, FT * (k + 1)), cwf_rows[:, P * k:P * k + P],
                                               ident[0:FT, 0:FT])
                last.then_inc(vec_tr, 1)
                pe.wait_ge(glu, 5)
                transpose_norm("n_mem")
                for i in range(4):
                    free(i, USES["kv"][i])
                    to_channels(G_KV + i, i, q_pair, 0, "n_mem" if i == 0 else None)
                for i in range(4):
                    to_rows(G_KV + 4 + i, 2, q_pair, 2 * i, 4, 2, BW, i == 0, i == 3)

            ready_low("n_mix")
            for phase, g0 in phases:
                if phase == "cvb":
                    memory()
                with pe.Fori(0, 4) as i:
                    for j in range(3):
                        if phase == "ugq" and j == 0:
                            pe.wait_ge(glu, 1 + i)
                        elif phase == "cvb" and j == 0:
                            pe.wait_ge(bank_read[0], USES["cvb"][0] + i)
                        else:
                            pe.wait_ge(bank_read[j], USES[phase][j] + i)
                        to_channels(g0 + j, j, p_pair, i)
            for i in range(4):
                free(i, USES["a_out"][i])
                if i == 0:
                    pe.wait_ge(an_lo, 4)
                if i == 3:
                    scores("att1", 0)
                to_channels(G_AO + i, i, q_pair)
            pe.wait_ge(conv_tap, (K_B + 3) * CONV_DVE)
            pe.wait_ge(pool_tap, K_B * (KD - CONV_DVE))
            free(7, USES["att1"][7])
            for c in range(KD):
                last = nc.tensor.matmul(bank(7, 0, S), mean_w[:, :], conv[:, S * c:S * c + S],
                                        start=c == 0, stop=c == KD - 1)
            last.then_inc(ln_mean, 1)
            scores("att1", 1)
            attention("att1")
            free(3, USES["att_out"][3])
            pe.wait_ge(ln_dg, 1)
            for t in range(T):
                last = nc.tensor.matmul(bank(3, P * t, P * t + P), mean_w[:, :], ln_diag[:, P * t:P * t + P],
                                        start=True, stop=True)
            last.then_inc(ln_bc, 1)
            for i in range(4):
                free(i, USES["att_out"][i])
                if i == 3:
                    pe.wait_ge(ln_z, 1)
                to_channels(G_ATT + i, i, p_pair, 0, "att1" if i == 0 else None, 4)
            pe.wait_ge(ln_lo, 2)
            for i in range(4):
                free(i, USES["b_out"][i])
                to_channels(G_BO + i, i, q_pair)
            for b in range(4, 8):
                free(b, USES["w_o"][b])
            for i in range(4):
                pe.wait_ge(mg_lo, i + 1)
                to_rows(G_WO + i, 2, p_pair, 2 * i, 4, 2, BW, i == 0, i == 3, 0, i == 3)
            transpose_norm("n_ffn")

            def gate_up(n, g, i=0, after=None):
                for part in range(2):
                    if not after or part:
                        free(part, USES["ffn1"][part] + n + i)
                    to_channels(g + part, part, p_pair, i, after if part == 0 else None)

            gate_up(0, G_FFN1, 0, "n_ffn")
            for b in range(4, 8):
                free(b, USES["ffn1"][b])

            def ffn1_round(i):
                first = isinstance(i, int) and i == 0
                gate_up(1, G_FFN1 + 2, i)
                pe.wait_ge(f_lo, 1 + i)
                to_rows(G_FFN1 + 4, 2, q_pair, 0, 4, 2, BW, first, False, i)

            ffn1_round(0)
            with pe.Fori(1, FG - 1) as i:
                ffn1_round(i)
            pe.wait_ge(f_lo, FG)
            to_rows(G_EV - 1, 2, q_pair, 0, 4, 2, BW, False, True, 0, True)
            transpose_norm("n_mix2a")
            ready_low("n_mix2a")
            for b in (4, 5):
                free(b, USES["ev_in"][b])
            for i in range(KD):
                to_rows(G_EV + i, 1, p_pair, i, 0, 3, 480, i == 0, i == KD - 1)
            pe.wait_ge(l_x, 2)
            for b in range(3):
                free(b, USES["lat"][b])
            for t in range(T):
                for c in range(5):
                    last = nc.tensor.transpose(bank(c // 2, c % 2 * S + P * t, c % 2 * S + P * t + P),
                                               z[:, t, Z_CQ + P * c:Z_CQ + P * c + P], ident[:, :])
            last.then_inc(l_tr, 1)
            for b in range(3):
                free(b, USES["lat"][b] + 1)
            free(3, USES["uq"][3])
            for i in range(3):
                to_rows(G_UQ + i, 1, p_pair, i, 0, 2, 384, i == 0, i == 2)
            for b in range(4, 8):
                free(b, USES["ukv"][b])
            to_rows(G_UKV, 2, p_pair, 3, 4, 2, BW, True, True)
            for i in range(11):
                b = i % 4
                pe.wait_ge(rope_a, 2) if i == 0 else None
                pe.wait_ge(rope_b, 4) if i == 3 else None
                free(b, USES["ev_tr"][b] + i // 4)
                for c in range(1 if i == 2 else 2):
                    for t in range(T):
                        at = slice(S * c + P * t, S * c + P * t + P)
                        if i < 2:
                            src = qrot[:, t, P * (2 * i + c):P * (2 * i + c) + P]
                        elif i == 2:
                            src = z[:, t, Z_K:Z_V]
                        else:
                            h = 2 * ((i - 3) % 4) + c
                            src = (qb if i < 7 else kf)[:, t, B_QK * h:B_QK * h + B_QK]
                        dst = ps[:, b, at] if i < 3 else ps[0:B_QK, b, at]
                        last = nc.tensor.transpose(dst, src, ident[:, :])
                last.then_inc(ev_tr, 1)
            for b in range(4):
                free(b, USES["att2"][b])
            for i in range(2):
                scores("att2", i)
            attention("att2")
            for b in range(4):
                free(b, USES["ev_out"][b])
            for i in range(4):
                free(4 + i, USES["att2"][4 + i] + 1)
                to_rows(G_EVO + i, 2, p_pair, 2 * i, 0, 2, BW, i == 0, i == 3, 0, i == 3)
            transpose_norm("n_ffn2a")

            def ffn2(phase, k, g0, after):
                to_channels(g0, 0, p_pair, 0, after)
                for b in range(4, 8):
                    free(b, USES[phase][b])

                def three(i):
                    for j in range(3):
                        to_channels(g0 + 1 + 2 * j, (1 + j) % 3, p_pair, 2 * i)
                        pe.wait_ge(f2_lo, FP * k + j + 1 + 3 * i)
                        to_rows(g0 + 2 + 2 * j, 2, q_pair, 2 * j, 4, 2, BW,
                                isinstance(i, int) and i == 0 and j == 0, False, 2 * i)

                three(0)
                with pe.Fori(1, (FP - 1) // 3) as i:
                    three(i)
                pe.wait_ge(f2_lo, FP * (k + 1))
                to_rows(g0 + 2 * FP - 1, 2, q_pair, 0, 4, 2, BW, False, True, 0, True)

            ffn2("ffn2a", 0, G_F2A, "n_ffn2a")
            transpose_norm("n_mix2b")
            for i in range(8):
                if i:
                    free(i % 4, USES["qk"][i % 4] + i // 4)
                to_channels(G_QK + i, i % 4, p_pair, 0, None if i else "n_mix2b")
            for b in range(4, 8):
                free(b, USES["v"][b])
            for i in range(4):
                if i == 3:
                    scores("att3", 0)
                    scores("att3", 1)
                to_rows(G_V + i, 2, p_pair, 2 * i, 4, 2, BW, i == 0, i == 3)
            attention("att3")
            for b in range(4):
                free(b, USES["od_out"][b])
            for i in range(4):
                free(4 + i, USES["att3"][4 + i] + 1)
                to_rows(G_ODO + i, 2, p_pair, 2 * i, 0, 2, BW, i == 0, i == 3, 0, i == 3)
            transpose_norm("n_ffn2b")
            ffn2("ffn2b", 1, G_F2B, "n_ffn2b")


def rope_table():
    import numpy as np
    t = np.arange(S)
    pos = (t // GRID_W, t % GRID_W)
    parts = []
    for width in (HD // 2, B_ROPE // 2):
        inv = np.float32(10000.0) ** (-np.arange(0, width, 2, dtype=np.float32) / np.float32(width))
        ang = [(p.astype(np.float32)[:, None] * inv[None, :]).astype(np.float32) for p in pos]
        cos, sin = [np.cos(a) for a in ang], [np.sin(a) for a in ang]
        parts += [cos[0], cos[0], cos[1], cos[1], -sin[0], sin[0], -sin[1], sin[1]]
    return np.ascontiguousarray(np.concatenate(parts, axis=1).astype(np.float32))


def kernel(**inputs):
    import numpy as np
    import concourse.bacc as bacc
    from concourse.bass_utils import run_bass_kernel_spmd as run

    a = {k: np.asarray(v) for k, v in inputs.items()}
    rows = [a["conv_b_w"][0], a["conv_a_w"][0], a["norm_mix_g"], a["norm_mem_g"], a["b_gate"].reshape(3, D),
            a["conv_b_bias"], a["ln_b_g"], a["ln_b_b"], a["norm_ffn_g"], a["norm_mix_2"], a["norm_ffn_2"],
            np.concatenate([a["ev_b_q_norm_2"][0], a["ev_b_kv_norm_2"][0],
                            np.zeros(D - B_Q_RANK - B_KV_RANK, np.float32)])[None]]
    ev_out = a["ev_w_out_2"][0]
    by_pair = ev_out[:A_HEADS * HD].reshape(A_KV, A_HEADS // A_KV, HD, D).transpose(1, 0, 2, 3)
    data = {
        "x": a["x"][0], "mem": a["mem"][0], "vecs": np.concatenate(rows, axis=0),
        "w_in": a["w_in"][0], "w_a_out": a["w_a_out"][0], "w_b_out": a["w_b_out"][0], "w_kv": a["w_kv"][0],
        "w_att_out": a["w_att_out"][0], "w_o": a["w_o"][0], "w_up": a["w_up"][0],
        "conv_ffn_w": a["conv_ffn_w"][0], "w_down": a["w_down"][0],
        "norm_final_g": a["norm_final_g"], "final_norm": a["final_norm_2"],
        "gq": a["ev_a_q_norm_2"][0], "gk": a["ev_a_k_norm_2"][0], "rope": rope_table(),
        "ev_w_in": a["ev_w_in_2"][0], "uq": a["ev_b_w_uq_2"][0], "ukv": a["ev_b_w_ukv_2"][0],
        "ev_w_out": np.concatenate([by_pair.reshape(A_HEADS * HD, D), ev_out[A_HEADS * HD:]], axis=0), "od_w_qkv": a["od_w_qkv_2"][0], "od_w_out": a["od_w_out_2"][0],
        "rpb_rev": a["od_rpb_2"][0][..., ::-1],
        "up_a": a["ffn_w_up_2"][0], "up_b": a["ffn_w_up_2"][1],
        "down_a": a["ffn_w_down_2"][0], "down_b": a["ffn_w_down_2"][1],
    }
    data = {k: np.ascontiguousarray(v) for k, v in data.items()}
    nc = bacc.Bacc("TRN2", target_bir_lowering=False, num_devices=1)
    aps = {k: nc.dram_tensor("in_" + k, list(v.shape), F32, kind="ExternalInput").ap() for k, v in data.items()}
    out = nc.dram_tensor("out", [S, D], F32, kind="ExternalOutput").ap()
    two_blocks(nc, aps, out)
    r = run(nc, [{"in_" + k: v for k, v in data.items()}], core_ids=[0])
    return r.results[0]["out"].reshape(1, S, D)
```
